# Optimizing a Trainium2 kernel written in Bass

```python
import math
import jax
import jax.numpy as jnp
from jax import lax
import numpy as np

D_MODEL = 1024
BATCH = 1
SEQ = 512
DEPTH = 1
DEC_BATCH = 8
DEC_SEQ = 4
PAST_LEN = 2048
PAGE_SIZE = 128

A_HEADS = 8
A_HEAD_DIM = 64
A_WIDTH = A_HEADS * A_HEAD_DIM
MOBA_BLOCK = 256
MOBA_TOPK = 3
Q_BLOCK = 128
REL_BUCKETS = 32
REL_MAX_DIST = 128
G_HEADS = 4
G_KEY_DIM = D_MODEL // 2
G_VAL_DIM = D_MODEL
G_DK = G_KEY_DIM // G_HEADS
G_DV = G_VAL_DIM // G_HEADS
G_GATE_RANK = 16
G_GATE_NORMALIZER = 16.0
G_CHUNK = 32
N_GROUPS = 4
EXPERTS_PER_GROUP = 8
N_EXPERTS = N_GROUPS * EXPERTS_PER_GROUP
EXPERT_TOPK = 2
EXPERT_HIDDEN = 512
MOE_BLOCK = 128
EPS = 1e-6

IN_SIZES = (A_WIDTH, A_WIDTH, A_WIDTH, G_KEY_DIM, G_KEY_DIM, G_VAL_DIM, G_VAL_DIM, G_GATE_RANK, D_MODEL, D_MODEL)
IN_WIDTH = sum(IN_SIZES)

kernel_name = 'hybrid_moba_gla_hmoe_decode_step'

def _in_offsets():
    return [int(o) for o in np.cumsum(IN_SIZES)[:-1]]

def rms_norm(x, g):
    xf = x.astype(jnp.float32)
    y = xf * lax.rsqrt(jnp.mean(xf * xf, axis=-1, keepdims=True) + EPS)
    return (y * g.astype(jnp.float32)).astype(x.dtype)

def t5_bucket(dist):
    n = jnp.maximum(dist, 0)
    max_exact = REL_BUCKETS // 2
    nf = jnp.maximum(n, 1).astype(jnp.float32)
    large = max_exact + (jnp.log(nf / max_exact) / math.log(REL_MAX_DIST / max_exact)
                         * (REL_BUCKETS - max_exact)).astype(jnp.int32)
    large = jnp.minimum(large, REL_BUCKETS - 1)
    return jnp.where(n < max_exact, n, large)

def moba_sequence(q, k, v, rel_bias, offset):
    tq = q.shape[0]
    tk = k.shape[0]
    n_blocks = -(-tk // MOBA_BLOCK)
    pad = n_blocks * MOBA_BLOCK - tk
    kbh = jnp.pad(k, ((0, pad), (0, 0), (0, 0))).reshape(n_blocks, MOBA_BLOCK, A_HEADS, A_HEAD_DIM).transpose(2, 0, 1, 3)
    vbh = jnp.pad(v, ((0, pad), (0, 0), (0, 0))).reshape(n_blocks, MOBA_BLOCK, A_HEADS, A_HEAD_DIM).transpose(2, 0, 1, 3)
    k_mean = jnp.mean(kbh.astype(jnp.float32), axis=2)
    rb_t = rel_bias.T.astype(jnp.float32)
    n_sel = min(MOBA_TOPK, n_blocks)
    qc = math.gcd(tq, Q_BLOCK)
    head = jnp.arange(A_HEADS)
    blk = jnp.arange(MOBA_BLOCK)
    scale = A_HEAD_DIM ** -0.5

    def chunk(ci):
        start = ci * qc
        q_c = lax.dynamic_slice_in_dim(q, start, qc, 0).transpose(1, 0, 2)
        pos_q = offset + start + jnp.arange(qc)
        n_past = pos_q // MOBA_BLOCK
        own = (offset + start) // MOBA_BLOCK
        gate = jnp.einsum('hqd,hnd->hqn', q_c, k_mean, preferred_element_type=jnp.float32)
        is_past = jnp.arange(n_blocks)[None, None, :] < n_past[None, :, None]
        _, sel = lax.top_k(jnp.where(is_past, gate, -jnp.inf), n_sel)
        sel_ok = jnp.arange(n_sel)[None, :] < n_past[:, None]
        k_sel = kbh[head[:, None, None], sel]
        v_sel = vbh[head[:, None, None], sel]
        key_pos_sel = sel[..., None] * MOBA_BLOCK + blk
        bias_sel = rb_t[head[:, None, None, None], t5_bucket(pos_q[None, :, None, None] - key_pos_sel)]
        logit_sel = jnp.einsum('hqd,hqnkd->hqnk', q_c, k_sel, preferred_element_type=jnp.float32) * scale + bias_sel
        logit_sel = jnp.where(sel_ok[None, :, :, None], logit_sel, -jnp.inf)
        k_own = lax.dynamic_index_in_dim(kbh, own, axis=1, keepdims=False)
        v_own = lax.dynamic_index_in_dim(vbh, own, axis=1, keepdims=False)
        dist_own = pos_q[:, None] - (own * MOBA_BLOCK + blk)[None, :]
        logit_own = jnp.einsum('hqd,hkd->hqk', q_c, k_own, preferred_element_type=jnp.float32) * scale + rb_t[:, t5_bucket(dist_own)]
        logit_own = jnp.where(dist_own[None] >= 0, logit_own, -jnp.inf)
        logits = jnp.concatenate([logit_sel.reshape(A_HEADS, qc, n_sel * MOBA_BLOCK), logit_own], axis=-1)
        p = jax.nn.softmax(logits, axis=-1)
        p_sel = p[..., : n_sel * MOBA_BLOCK].reshape(A_HEADS, qc, n_sel, MOBA_BLOCK).astype(v.dtype)
        p_own = p[..., n_sel * MOBA_BLOCK:].astype(v.dtype)
        out = jnp.einsum('hqnk,hqnkd->hqd', p_sel, v_sel) + jnp.einsum('hqk,hkd->hqd', p_own, v_own)
        return out.transpose(1, 0, 2)

    out = lax.map(chunk, jnp.arange(tq // qc))
    return out.reshape(tq, A_HEADS, A_HEAD_DIM)

def gla_chunked(q, k, v, log_a, s0):
    b, t = q.shape[:2]
    c = math.gcd(t, G_CHUNK)
    n = t // c

    def to_chunks(z):
        return z.astype(jnp.float32).reshape(b, n, c, *z.shape[2:]).swapaxes(0, 1)

    causal = jnp.tril(jnp.ones((c, c), dtype=bool))

    def step(s, inp):
        q_c, k_c, v_c, a_c = inp
        cum = jnp.cumsum(a_c, axis=1)
        q_t = q_c * jnp.exp(cum)
        k_t = k_c * jnp.exp(-cum)
        inter = jnp.einsum('bthk,bhkv->bthv', q_t, s)
        att = jnp.where(causal, jnp.einsum('bthk,bshk->bhts', q_t, k_t), 0.0)
        intra = jnp.einsum('bhts,bshv->bthv', att, v_c)
        last = cum[:, -1]
        k_end = k_c * jnp.exp(last[:, None] - cum)
        s_new = s * jnp.exp(last)[..., None] + jnp.einsum('bshk,bshv->bhkv', k_end, v_c)
        return s_new, inter + intra

    s_fin, o = lax.scan(step, s0.astype(jnp.float32), (to_chunks(q), to_chunks(k), to_chunks(v), to_chunks(log_a)))
    o = o.swapaxes(0, 1).reshape(b, t, G_HEADS, G_DV)
    return o, s_fin.astype(s0.dtype)

def hier_moe(h, w_router_group, b_router_group, w_router_expert, b_router_expert, w_exp_gate, w_exp_up, w_exp_down):
    b, t, d = h.shape
    hf = h.reshape(-1, d)
    n = hf.shape[0]
    g_logits = (hf @ w_router_group + b_router_group).astype(jnp.float32)
    grp = jnp.argmax(g_logits, axis=-1)
    p_grp = jnp.take_along_axis(jax.nn.softmax(g_logits, axis=-1), grp[:, None], axis=-1)
    e_logits = (hf @ w_router_expert + b_router_expert).astype(jnp.float32).reshape(n, N_GROUPS, EXPERTS_PER_GROUP)
    e_in = jnp.take_along_axis(e_logits, grp[:, None, None], axis=1)[:, 0]
    top_val, top_idx = lax.top_k(e_in, EXPERT_TOPK)
    weights = p_grp * jax.nn.softmax(top_val, axis=-1)
    expert = grp[:, None] * EXPERTS_PER_GROUP + top_idx

    n_assign = n * EXPERT_TOPK
    flat_e = expert.reshape(-1)
    order = jnp.argsort(flat_e)
    se = flat_e[order]
    sw = weights.reshape(-1)[order]
    stok = jnp.repeat(jnp.arange(n, dtype=jnp.int32), EXPERT_TOPK)[order]
    counts = jnp.bincount(flat_e, length=N_EXPERTS)
    starts = jnp.cumsum(counts) - counts
    padded = (counts + MOE_BLOCK - 1) // MOE_BLOCK * MOE_BLOCK
    pad_ends = jnp.cumsum(padded)
    pad_starts = pad_ends - padded
    dest = pad_starts[se] + (jnp.arange(n_assign) - starts[se])
    n_rows = (n_assign + N_EXPERTS * (MOE_BLOCK - 1) + MOE_BLOCK - 1) // MOE_BLOCK * MOE_BLOCK
    n_blk = n_rows // MOE_BLOCK
    row_tok = jnp.full((n_rows,), n, dtype=jnp.int32).at[dest].set(stok)
    row_w = jnp.zeros((n_rows,), dtype=jnp.float32).at[dest].set(sw)
    blk_expert = jnp.minimum(jnp.searchsorted(pad_ends, jnp.arange(n_blk) * MOE_BLOCK, side='right'), N_EXPERTS - 1)
    h_pad = jnp.concatenate([hf, jnp.zeros((1, d), hf.dtype)], axis=0)

    def block(args):
        toks, wts, e = args
        xb = h_pad[toks]
        a = xb @ w_exp_gate[e]
        u = xb @ w_exp_up[e]
        return ((jax.nn.silu(a) * u) @ w_exp_down[e]) * wts[:, None].astype(xb.dtype)

    y_rows = lax.map(block, (row_tok.reshape(n_blk, MOE_BLOCK), row_w.reshape(n_blk, MOE_BLOCK), blk_expert))
    y = jax.ops.segment_sum(y_rows.reshape(n_rows, d), row_tok, num_segments=n + 1)[:n]
    return y.reshape(b, t, d)

def decoder_layer(x, c, attend, s0, norm1_g, norm2_g, w_ada, b_ada, w_in, w_gk2, b_gk,
                  q_norm_g, k_norm_g, o_norm_g, w_branch_a, w_branch_b, w_out,
                  w_router_group, b_router_group, w_router_expert, b_router_expert,
                  w_exp_gate, w_exp_up, w_exp_down):
    b, t, _ = x.shape
    mod = jax.nn.silu(c) @ w_ada + b_ada
    shift1, scale1, gate1, shift2, scale2, gate2 = jnp.split(mod[:, None, :], 6, axis=-1)
    h = rms_norm(x, norm1_g) * (1 + scale1) + shift1
    q_a, k_a, v_a, q_g, k_g, v_g, og_g, gk_lr, gate_a, gate_b = jnp.split(h @ w_in, _in_offsets(), axis=-1)
    q_a = rms_norm(q_a.reshape(b, t, A_HEADS, A_HEAD_DIM), q_norm_g)
    k_a = rms_norm(k_a.reshape(b, t, A_HEADS, A_HEAD_DIM), k_norm_g)
    v_a = v_a.reshape(b, t, A_HEADS, A_HEAD_DIM)
    o_a = attend(q_a, k_a, v_a).reshape(b, t, A_WIDTH)
    log_a = jax.nn.log_sigmoid((gk_lr @ w_gk2 + b_gk).astype(jnp.float32)) / G_GATE_NORMALIZER
    o_g, s_new = gla_chunked(q_g.reshape(b, t, G_HEADS, G_DK) * (G_DK ** -0.5),
                             k_g.reshape(b, t, G_HEADS, G_DK),
                             v_g.reshape(b, t, G_HEADS, G_DV),
                             log_a.reshape(b, t, G_HEADS, G_DK), s0)
    o_g = rms_norm(o_g.astype(x.dtype), o_norm_g) * jax.nn.silu(og_g).reshape(b, t, G_HEADS, G_DV)
    o_g = o_g.reshape(b, t, G_VAL_DIM)
    merged = jax.nn.sigmoid(gate_a) * (o_a @ w_branch_a) + jax.nn.sigmoid(gate_b) * (o_g @ w_branch_b)
    x = x + gate1 * (merged @ w_out)
    h2 = rms_norm(x, norm2_g) * (1 + scale2) + shift2
    x = x + gate2 * hier_moe(h2, w_router_group, b_router_group, w_router_expert, b_router_expert,
                             w_exp_gate, w_exp_up, w_exp_down)
    return x, k_a, v_a, s_new

def setup_inputs(seed: int = 0) -> dict:
    key = jax.random.key(seed)
    ks = list(jax.random.split(key, 32))
    n_pages = PAST_LEN // PAGE_SIZE
    n_pool = (DEC_BATCH * n_pages * 5) // 4
    f32 = jnp.float32

    def nrm(k, shape, s=1.0):
        return jax.random.normal(k, shape, f32) * s

    def gain(k, shape):
        return 1.0 + nrm(k, shape, 0.02)

    page_table = jax.random.permutation(ks[7], n_pool)[: DEC_BATCH * n_pages].reshape(DEC_BATCH, n_pages).astype(jnp.int32)
    return {
        'x_prompt': nrm(ks[0], (BATCH, SEQ, D_MODEL)),
        'x_sample': nrm(ks[1], (DEC_BATCH, DEC_SEQ, D_MODEL)),
        'c_prompt': nrm(ks[2], (BATCH, D_MODEL)),
        'c_sample': nrm(ks[3], (DEC_BATCH, D_MODEL)),
        'cache_k': nrm(ks[4], (DEPTH, n_pool, PAGE_SIZE, A_HEADS, A_HEAD_DIM)),
        'cache_v': nrm(ks[5], (DEPTH, n_pool, PAGE_SIZE, A_HEADS, A_HEAD_DIM)),
        'state_gla': nrm(ks[6], (DEPTH, DEC_BATCH, G_HEADS, G_DK, G_DV)),
        'page_table': page_table,
        'rel_bias': nrm(ks[8], (REL_BUCKETS, A_HEADS), 0.5),
        'norm1_g': gain(ks[9], (DEPTH, D_MODEL)),
        'norm2_g': gain(ks[10], (DEPTH, D_MODEL)),
        'w_ada': nrm(ks[11], (DEPTH, D_MODEL, 6 * D_MODEL), 0.5 * D_MODEL ** -0.5),
        'b_ada': nrm(ks[12], (DEPTH, 6 * D_MODEL), 0.01),
        'w_in': nrm(ks[13], (DEPTH, D_MODEL, IN_WIDTH), D_MODEL ** -0.5),
        'w_gk2': nrm(ks[14], (DEPTH, G_GATE_RANK, G_KEY_DIM), G_GATE_RANK ** -0.5),
        'b_gk': nrm(ks[15], (DEPTH, G_KEY_DIM), 0.01),
        'q_norm_g': gain(ks[16], (DEPTH, A_HEAD_DIM)),
        'k_norm_g': gain(ks[17], (DEPTH, A_HEAD_DIM)),
        'o_norm_g': gain(ks[18], (DEPTH, G_DV)),
        'w_branch_a': nrm(ks[19], (DEPTH, A_WIDTH, D_MODEL), A_WIDTH ** -0.5),
        'w_branch_b': nrm(ks[20], (DEPTH, G_VAL_DIM, D_MODEL), G_VAL_DIM ** -0.5),
        'w_out': nrm(ks[21], (DEPTH, D_MODEL, D_MODEL), D_MODEL ** -0.5),
        'w_router_group': nrm(ks[22], (DEPTH, D_MODEL, N_GROUPS), D_MODEL ** -0.5),
        'b_router_group': nrm(ks[23], (DEPTH, N_GROUPS), 0.01),
        'w_router_expert': nrm(ks[24], (DEPTH, D_MODEL, N_EXPERTS), D_MODEL ** -0.5),
        'b_router_expert': nrm(ks[25], (DEPTH, N_EXPERTS), 0.01),
        'w_exp_gate': nrm(ks[26], (DEPTH, N_EXPERTS, D_MODEL, EXPERT_HIDDEN), D_MODEL ** -0.5),
        'w_exp_up': nrm(ks[27], (DEPTH, N_EXPERTS, D_MODEL, EXPERT_HIDDEN), D_MODEL ** -0.5),
        'w_exp_down': nrm(ks[28], (DEPTH, N_EXPERTS, EXPERT_HIDDEN, D_MODEL), EXPERT_HIDDEN ** -0.5),
    }

def reference(x_prompt, x_sample, c_prompt, c_sample, cache_k, cache_v, state_gla, page_table,
              rel_bias, norm1_g, norm2_g, w_ada, b_ada, w_in, w_gk2, b_gk, q_norm_g, k_norm_g, o_norm_g,
              w_branch_a, w_branch_b, w_out, w_router_group, b_router_group, w_router_expert, b_router_expert,
              w_exp_gate, w_exp_up, w_exp_down):
    n_pages = page_table.shape[1]
    past_len = n_pages * cache_k.shape[2]

    def attend_prompt(q, k, v):
        return lax.map(lambda a: moba_sequence(a[0], a[1], a[2], rel_bias, 0), (q, k, v))

    def make_attend_sample(layer):
        def attend_sample(q, k, v):
            def one(a):
                qb, kn, vn, pages = a
                k_past = cache_k[layer, pages].reshape(past_len, A_HEADS, A_HEAD_DIM)
                v_past = cache_v[layer, pages].reshape(past_len, A_HEADS, A_HEAD_DIM)
                k_full = jnp.concatenate([k_past, kn.astype(k_past.dtype)], axis=0)
                v_full = jnp.concatenate([v_past, vn.astype(v_past.dtype)], axis=0)
                return moba_sequence(qb, k_full, v_full, rel_bias, past_len)
            return lax.map(one, (q, k, v, page_table))
        return attend_sample

    y_p, y_s = x_prompt, x_sample
    kp_list, vp_list, sp_list, ks_list, vs_list, ss_list = [], [], [], [], [], []
    for layer in range(DEPTH):
        lw = (norm1_g[layer], norm2_g[layer], w_ada[layer], b_ada[layer], w_in[layer], w_gk2[layer], b_gk[layer],
              q_norm_g[layer], k_norm_g[layer], o_norm_g[layer], w_branch_a[layer], w_branch_b[layer], w_out[layer],
              w_router_group[layer], b_router_group[layer], w_router_expert[layer], b_router_expert[layer],
              w_exp_gate[layer], w_exp_up[layer], w_exp_down[layer])
        s0_prompt = jnp.zeros((x_prompt.shape[0], G_HEADS, G_DK, G_DV), state_gla.dtype)
        y_p, k_p, v_p, s_p = decoder_layer(y_p, c_prompt, attend_prompt, s0_prompt, *lw)
        y_s, k_s, v_s, s_s = decoder_layer(y_s, c_sample, make_attend_sample(layer), state_gla[layer], *lw)
        kp_list.append(k_p)
        vp_list.append(v_p)
        sp_list.append(s_p)
        ks_list.append(k_s)
        vs_list.append(v_s)
        ss_list.append(s_s)
    k_prompt = jnp.stack(kp_list)
    v_prompt = jnp.stack(vp_list)
    state_gla_prompt = jnp.stack(sp_list)
    k_sample = jnp.stack(ks_list)
    v_sample = jnp.stack(vs_list)
    state_gla_sample = jnp.stack(ss_list)
    return (y_p, y_s, k_prompt, v_prompt, state_gla_prompt, k_sample, v_sample, state_gla_sample)


_drawn_inputs = setup_inputs


def setup_inputs(seed=0):
    import zlib

    import numpy as np

    out = dict(_drawn_inputs(seed))
    spreads = {}
    factors = {'cache_k': 5.076,
     'cache_v': 5.623,
     'rel_bias': 4.02,
     'norm2_g': 4.512,
     'b_gk': 8.0,
     'q_norm_g': 8.0,
     'k_norm_g': 2.822,
     'o_norm_g': 8.0,
     'b_router_group': 8.0,
     'b_router_expert': 7.917}
    for name, (base, spread) in spreads.items():
        noise = np.random.default_rng([zlib.crc32(name.encode()), seed]).standard_normal(out[name].shape)
        drawn = base * np.exp(spread * noise) if base else spread * noise
        out[name] = jnp.asarray(drawn.astype(out[name].dtype))
    for name, factor in factors.items():
        out[name] = (out[name] * factor).astype(out[name].dtype)
    return out
```

```python
from contextlib import ExitStack

import numpy as np
import concourse.bass as bass
from concourse import mybir

ALU = mybir.AluOpType
ACT = mybir.ActivationFunctionType
F32 = mybir.dt.float32
I32 = mybir.dt.int32
U32 = mybir.dt.uint32
AX = mybir.AxisListType

P = 128
D = 1024
KD = D // P
SEQ, DEC_B, DEC_T = 512, 8, 4
NS = DEC_B * DEC_T
NT = SEQ + NS
PT = SEQ // P
TILES = [(t * P, P) for t in range(PT)] + [(SEQ, NS)]
HALF = NT // 2
PAST, PAGE = 2048, 128
PAGES = PAST // PAGE
AH, AD = 8, 64
AW = AH * AD
PAIRS = AH // 2
BLK = 256
NBLK = PAST // BLK
TOPK = 3
BUCKETS, MAXDIST = 32, 128
GH, GDK, GDV = 4, 128, 256
RANK = 16
GNORM = 16.0
CHUNK = 32
NCH = SEQ // CHUNK
CPT = P // CHUNK
NG, EPG, NE, HID = 4, 8, 32, 512
CAP = 64
MORE = 2 * NT // CAP - 1
EB = NE + MORE
EDGES = -(-NT // CAP) - 1
EPS = 1e-6
NEG = -1e30
OFF = dict(qa=0, ka=AW, va=2 * AW, qg=3 * AW, kg=3 * AW + 512, vg=3 * AW + 1024, og=3 * AW + 2048,
           gk=3 * AW + 3072, ga=3 * AW + 3088, gb=3 * AW + 4112)
IN_W = 3 * AW + 5136
RING = 6
UNIT = KD * 512
TAB = 384
WORK = 16550
RBM = 255


def shape_constants():
    c = {}
    i = np.arange(P)
    c["ident"] = np.eye(P)
    c["ones"] = np.ones((P, P))
    c["before"] = (i[:, None] < i[None, :])
    c["chunk_causal"] = (i[:, None] <= i[None, :]) & (i[:, None] // CHUNK == i[None, :] // CHUNK)
    s = i[:NS]
    c["seq_causal"] = (s[:, None] <= s[None, :]) & (s[:, None] // DEC_T == s[None, :] // DEC_T)
    c["seq_member"] = (s[:, None] // DEC_T == np.arange(DEC_B)[None, :])
    dist = RBM - np.arange(TAB)
    n = np.maximum(dist, 0)
    exact = BUCKETS // 2
    nf = np.maximum(n, 1).astype(np.float32)
    large = exact + (np.log(nf / np.float32(exact)) / np.float32(np.log(MAXDIST / exact))
                     * np.float32(BUCKETS - exact)).astype(np.int32)
    bucket = np.where(n < exact, n, np.minimum(large, BUCKETS - 1))
    hot = np.zeros((BUCKETS + 1, TAB))
    hot[bucket, np.arange(TAB)] = 1
    hot[:, dist < 0] = 0
    hot[BUCKETS, dist < 0] = 1
    c["lower_index"] = np.broadcast_to((np.arange(8)[None, :] < np.arange(8)[:, None]).reshape(1, 64), (P, 64))
    c["lower_index4"] = np.broadcast_to((np.arange(4)[None, :] < np.arange(4)[:, None]).reshape(1, 16), (P, 16))
    tok = i[:, None] + P * np.arange(PT + 1)[None, :]
    c["token_real"] = tok < NT
    c["token_id"] = np.minimum(tok, NT - 1)
    c["expert_id"] = np.broadcast_to(np.arange(NE)[None, :], (P, NE))
    c["block_edge"] = np.broadcast_to(CAP * (1 + np.arange(EDGES))[None, :], (P, EDGES))
    c["more_id"] = np.broadcast_to(np.arange(MORE)[None, :], (P, MORE))
    c["minus_half"] = np.full((P, 8), -0.5)
    c["bucket_hot"] = hot
    at, cols = {}, 0
    for k, v in c.items():
        at[k] = (cols, v.shape[0], v.shape[1])
        cols += v.shape[1]
    table = np.zeros((P, cols), np.float32)
    for k, v in c.items():
        o, r, w = at[k]
        table[:r, o:o + w] = v
    return table, at


CONST_TABLE, CONST_AT = shape_constants()


def layer_kernel(nc, x_prompt, x_sample, c_prompt, c_sample, cache_k, cache_v, state_gla, page_table,
                 rel_bias, norm1_g, norm2_g, w_ada, b_ada, w_in, w_gk2, b_gk, q_norm_g, k_norm_g, o_norm_g,
                 w_branch_a, w_branch_b, w_out, w_router_group, b_router_group, w_router_expert,
                 b_router_expert, w_exp_gate, w_exp_up, w_exp_down, shape_table,
                 y_prompt, y_sample, k_prompt, v_prompt, state_prompt, k_sample, v_sample, state_sample):
    with ExitStack() as ctx:
        def sb(name, shape, dt=F32):
            return ctx.enter_context(nc.sbuf_tensor(name, shape, dt))

        def sem(name):
            return ctx.enter_context(nc.semaphore(name))

        bias_dram = nc.dram_tensor("bias_rows", [AH, P, TAB], F32, kind="Internal").ap()
        h2_dram = nc.dram_tensor("h2_rows", [NT, D], F32, kind="Internal").ap()
        slot_dram = nc.dram_tensor("slot_tokens", [CAP * EB, 1], I32, kind="Internal").ap()
        y_dram = nc.dram_tensor("expert_rows", [CAP * EB, D], F32, kind="Internal").ap()

        KEPT = CONST_AT["bucket_hot"][0]
        cst = sb("cst", [P, KEPT])

        def const(name):
            o, r, w = CONST_AT[name]
            return cst[0:r, o:o + w]

        ident, ones = const("ident"), const("ones")
        ring = sb("ring", [P, RING, UNIT])
        xT = sb("xT", [P, KD, NT])
        hT = sb("hT", [P, KD, NT])
        work = sb("work", [P, WORK])
        cT = sb("cT", [P, KD, DEC_B + 1])
        vT = sb("vT", [P, 64])
        mod = sb("mod", [P, 6, KD, DEC_B + 1])
        gain = sb("gain", [P, 2, KD, DEC_B + 1])
        wgk = sb("wgk", [P, KD, RANK])
        gk2 = sb("gk2", [RANK + 1, 512])
        qkg = sb("qkg", [P, 2, AD])
        ong = sb("ong", [P, GDV])
        rbx = sb("rbx", [BUCKETS + 1, AH])
        rbfar = sb("rbfar", [P, AH])
        st = sb("stats", [P, 256])
        far_s = sb("far_s", [P, 1])
        ps = ctx.enter_context(nc.psum_tensor("ps", [P, 8, 512], F32))

        def carve(base, *sizes):
            out = []
            for n in sizes:
                out.append(work[:, base:base + n])
                base += n
            assert base <= WORK, base
            return out

        def grid(v, n):
            return v.rearrange("p (a b) -> p a b", a=n)

        o_aT = grid(work[:, 0:PAIRS * NT], PAIRS)
        o_gT = grid(work[:, 2176:2176 + KD * NT], KD)

        def wide(w, rows=P):
            return ps[0:rows, 2 * w:2 * w + 2, 0:HALF]

        def halves(v):
            return v.rearrange("p (a c) -> p a c", a=2)

        S = {}

        def s(name):
            if name not in S:
                S[name] = sem(name)
            return S[name]

        slot_sem = [sem(f"slot{i}_landed") for i in range(RING)]
        w_used = sem("w_used")
        slot_count = [0] * RING
        stream = []

        def add_block(pieces, dmas, used):
            n = len(stream)
            slot_count[n % RING] += 16 * dmas
            stream.append((slot_count[n % RING], pieces, used))
            return n

        def slot(n):
            return ring[:, n % RING, :]

        def columns(w, lo, n, cols, at=0, k=KD):
            dst = slot(n)[:, at:at + k * cols].rearrange("p (k c) -> p k c", k=k)
            return dst, w.rearrange("(k p) c -> p k c", p=P)[:, :, lo:lo + cols]

        def block(used, *parts):
            n = len(stream)
            return add_block([columns(w, lo, n, cols, at, k) for w, lo, cols, at, k in parts], len(parts), used)

        ADA = [block((w_used, i + 1), (w_ada[0], 512 * i, 512, 0, KD)) for i in range(12)]
        QKV = [block((s("pj"), 5 * i + 5), (w_in[0], OFF[c], 512, 0, KD)) for i, c in enumerate(("qa", "ka", "va"))]
        PAGED = {}
        for g in range(2):
            for what in ("k", "v"):
                for j in range(4):
                    for half in range(2):
                        b = 4 * g + j
                        used = (s("page_tr"), PAGES * b + 8 * half + 8) if what == "k" else (s("pv_s"), b + 1)
                        PAGED[(what, b, half)] = add_block((what, b, half), 8, used)
        GLA = []
        for h in range(GH):
            a = block((s("v_ps"), 3 * h + 3), (w_in[0], OFF["qg"] + GDK * h, GDK, 0, KD), (w_in[0], OFF["kg"] + GDK * h, GDK, KD * GDK, KD),
                      (w_in[0], OFF["vg"] + GDV * h, GDV, 2 * KD * GDK, KD))
            b = block((s("og_ps"), 3 * h + 3), (w_in[0], OFF["og"] + GDV * h, GDV, 0, KD))
            GLA.append((a, b))
        MERGE = [block((s("pb_ps"), t + 1), (w_in[0], OFF["ga"] + P * t, P, 0, KD), (w_in[0], OFF["gb"] + P * t, P, KD * P, KD),
                       (w_branch_b[0], P * t, P, 2 * KD * P, KD), (w_branch_a[0], P * t, P, 3 * KD * P, AW // P))
                 for t in range(KD)]
        OUT = [block((s("out_ps"), 4 * i + 4), (w_out[0], 512 * i, 512, 0, KD)) for i in range(2)]
        N0 = len(stream)
        EXP_USED = len(ADA)
        EXP_COUNT = [slot_count[i] for i in range(RING)]

        def landed(pe, n):
            pe.wait_ge(slot_sem[n % RING], stream[n][0])

        ONCE = {
            "pe": ["c_tr", "own_ps", "gk_ps", "lg_ps", "pos_ps", "g_tr"],
            "dve": ["rbx_set", "sample_set", "rbw_ready", "cT", "var_ready", "qbd", "own_T", "att_set", "gk_ones",
                    "var2_ready", "g_exp2", "lg_max", "e_gap", "chosen", "dest_ready", "more_ready"],
            "act": ["c_silu", "rstd_ready", "gk_ready", "rstd2_ready", "lg_exp", "e_gap_exp", "g_rows", "rows_out"],
            "pool": ["zero_set", "zero_rows"],
        }
        once_sem = {e: sem(e + "_steps") for e in ONCE}

        def done(name):
            return next(once_sem[e] for e in ONCE if name in ONCE[e]), 1

        def after(name):
            return next((once_sem[e], ONCE[e].index(name) + 1) for e in ONCE if name in ONCE[e])

        class Chain:

            def __init__(self, name):
                self.sem, self.n = sem(name), 0

            def __call__(self, eng, ins):
                ins.then_inc(self.sem, 1)
                self.n += 1
                eng.wait_ge(self.sem, self.n)

        dve_chain, act_chain, pool_chain = Chain("dve_own"), Chain("act_own"), Chain("pool_own")

        x_tok, sq, var, rstd, bias_stage, rbw, crow, vrow, zero_i, hot = carve(
            2176, 5 * D, 2 * NT, NT, NT, 2 * TAB, AH * P, 2 * D, P, CAP * EB // P, TAB)
        crow, vrow, zero_i, hot = grid(crow[0:DEC_B + 1], 2), vrow[0:64, :], zero_i.bitcast(I32), hot[0:BUCKETS + 1, :]
        qbd, own_T, near_s, own_s, ptab = carve(15000, PAIRS * DEC_B * 8, DEC_B * 32, PAGE + DEC_T, 2 * NS, DEC_B * PAGES)
        qbd = qbd.rearrange("p (a b c) -> p a b c", a=PAIRS, b=DEC_B)
        own_T, own_s, ptab = own_T[0:NS, :], grid(own_s, 2), ptab[0:1, :].bitcast(I32)
        x_tok = grid(x_tok, 5)
        sq = grid(sq, 2)
        bias_stage = grid(bias_stage, 2)
        rbw = rbw[0:BUCKETS + 1, :]

        qT, kT, v_tok, near, sc_p, pt_p, tok, tok_sq = carve(
            2176, PAIRS * NT, PAIRS * NT, 5 * AW, AH * 2 * P, 2 * 512, 2 * 512, 2 * AW, AW)
        qT, kT, v_tok = grid(qT, PAIRS), grid(kT, PAIRS), grid(v_tok, 5)
        near, sc_p, pt_p, tok = grid(near, AH), grid(sc_p, 2), grid(pt_p, 2), grid(tok, 2)
        after_v = 2176 + 2 * PAIRS * NT + 5 * AW
        prT, logit, kpage = carve(after_v, (PAGES + 1) * P, PAST + NS, 3 * AW)
        prT, kpage = grid(prT, PAGES + 1), grid(kpage, 3)
        scT = prT[:, 0:PAGES, :]
        cmp8 = sb("cmp8", [P, 2, 5 * NE])
        junk = cmp8[:, :, :].rearrange("p a b -> p (a b)")[:, 64:64 + GDV]

        (e_cum, e_neg, e_end, v_g, og, la, kend, state, att, state_s, q_mask, on_, gkT) = carve(
            2176 + KD * NT, NT, NT, NT, 5 * GDV, 5 * GDV, 8 * P, 5 * P, 2 * GDV, 2 * P, DEC_B * GDV, 288, 2 * GDV, NT)
        v_g, og, kend, state, att = grid(v_g, 5), grid(og, 5), grid(kend, 5), grid(state, 2), grid(att, 2)
        state_s, on_ = grid(state_s, DEC_B), grid(on_, 2)
        kend_m = grid(la, DEC_B)[0:NS]
        gkT = gkT[0:RANK + 1, :]

        mergedT, m_a, m_b = carve(2176 + KD * NT, KD * NT, 2 * NT, 2 * NT)
        mergedT, m_a, m_b = grid(mergedT, KD), grid(m_a, 2), grid(m_b, 2)
        sq2, var2, rstd2, tmp2 = carve(2176, 2 * NT, NT, NT, NT)
        sq2 = grid(sq2, 2)

        h2_tok, x1_tok, g2p, g2s, g_exp = carve(0, 5 * D, 5 * D, D, D, KD * (P + NS))
        wr, brow, lg, one1, one2, both = carve(13600, KD * (NG + NE), NG + NE, 5 * (NG + NE), 5 * NE, 5 * NE, 5 * NE)
        wr, brow, lg = grid(wr, KD), brow[0:1, :], grid(lg, 5)
        one1, one2, both = grid(one1, 5), grid(one2, 5), grid(both, 5)
        h2_tok, x1_tok, g_exp = grid(h2_tok, 5), grid(x1_tok, 5), grid(g_exp, KD)
        g2s = g2s[0:NS, :]
        ya = grid(h2_tok.rearrange("p a b -> p (a b)")[:, 0:2 * D], 2)
        yb = grid(h2_tok.rearrange("p a b -> p (a b)")[:, 2 * D:4 * D], 2)
        hflat = hT[:, :, :].rearrange("p a b -> p (a b)")
        xflat = xT[:, :, :].rearrange("p a b -> p (a b)")
        xs = [hflat[0:CAP, D * i:D * i + D] for i in range(2)]
        xsT = [hflat[:, 2 * D + 512 * i:2 * D + 512 * i + 512] for i in range(2)]
        hid = [hflat[:, 3 * D + 256 * (i + 1):3 * D + 256 * (i + 2)] for i in range(2)]
        ye = [xflat[0:CAP, D * i:D * i + D] for i in range(2)]

        blk_cmp, zero_rows = carve(14600, NE * MORE, D)
        zero_rows = zero_rows[0:CAP, :]
        wts = sb("wts", [P, 2, 5])
        dest = sb("dest", [P, 2, 5])
        dest_i = sb("dest_i", [P, 2, 5], I32)
        row_i = sb("row_i", [P, 2, 5], I32)
        tok_i = sb("tok_i", [P, 5], I32)
        cnt = sb("cnt", [P, NE])
        base = sb("base", [P, NE])
        more_i = sb("more_i", [1, MORE + 1], I32)
        idx = sb("idx", [CAP, EB], I32)

        idx_cur = sb("idx_cur", [CAP, 1], I32)

        def bc(v, shape):
            return v.broadcast_to(shape)

        def further_blocks(eng, body):
            eng.wait_ge(*after("more_ready"))
            count = eng.value_load(more_i[0:1, MORE:MORE + 1], min_val=0, max_val=MORE)
            with eng.If(count > 0):
                with eng.Fori(0, MORE) as c:
                    with eng.If(count > c):
                        body(c)
            return count

        sample = slice(SEQ, NT)
        own_lower8, own_lower4 = const("lower_index"), const("lower_index4")
        blk = ctx.enter_context(nc.Block())

        @blk.sync
        def _(sp):
            sp.wait_ge(s("page_table_in"), 16)
            for n, (_, pieces, _) in enumerate(stream):
                if n >= RING:
                    sp.wait_ge(*stream[n - RING][2])
                if isinstance(pieces, tuple):
                    what, b, half = pieces
                    cache = cache_k if what == "k" else cache_v
                    for q in range(PAGES // 2):
                        at = b * PAGES + half * (PAGES // 2) + q
                        page = sp.value_load(ptab[0:1, at:at + 1], min_val=0, max_val=cache.shape[1] - 1)
                        src = cache[0, bass.DynSlice(page, 1)].rearrange("a t h d -> (a t) (h d)")
                        sp.dma_start(slot(n)[:, AW * q:AW * q + AW], src).then_inc(slot_sem[n % RING], 16)
                else:
                    for dst, src in pieces:
                        sp.dma_start(dst, src).then_inc(slot_sem[n % RING], 16)

            def expert_blocks(e, par, before, expert=None):
                for m, w in enumerate((w_exp_gate, w_exp_up, w_exp_down)):
                    at = 3 * par + m
                    sp.wait_ge(*(stream[N0 + at - RING][2] if before is None else (w_used, before * 3 + (EXP_USED + m + 1))))
                    src = w[0, bass.DynSlice(e if expert is None else expert, 1)].rearrange("a (p k) c -> p (a k c)", k=w.shape[2] // P)
                    sp.dma_start(slot(N0 + at), src).then_inc(slot_sem[(N0 + at) % RING], 16)

            for par in range(2):
                expert_blocks(par, par, None)
            with sp.Fori(1, NE // 2) as i:
                for par in range(2):
                    expert_blocks(2 * i + par, par, 2 * i + (par - 2))

            def more(c):
                expert = sp.value_load(more_i[0:1, bass.DynSlice(c, 1)], min_val=0, max_val=NE - 1)
                expert_blocks(c + NE, 0, c + (NE - 1), expert)

            further_blocks(sp, more)

        @blk.gpsimd
        def _(pool):
            minus_half = const("minus_half")
            pool.memset(zero_i, 0).then_inc(*done("zero_set"))
            pool.wait_ge(*after("zero_set"))
            pool.dma_start(slot_dram.rearrange("(p n) a -> p (n a)", p=P), zero_i).then_inc(s("slots_cleared"), 16)
            for h in range(AH):
                pool.wait_ge(s("bias_copied"), h + 1)
                pool.dma_start(bias_dram[h], bias_stage[:, h % 2, :]).then_inc(s(f"bias_out{h % 2}"), 16)
            for a in range(2):
                pool.wait_ge(s(f"bias_out{a}"), 16 * AH // 2)
            for j in range(4):
                src = bass.AP(tensor=bias_dram.tensor, offset=P - 1, ap=[[P * TAB, AH], [TAB - 1, DEC_T], [1, PAGE + DEC_T]])
                pool.dma_start(near_s[32 * j:32 * j + 32, :], src).then_inc(s("near_s_in"), 16)
                src = bass.AP(tensor=bias_dram.tensor, offset=0, ap=[[P * TAB, AH], [TAB, DEC_T], [1, 1]])
                pool.dma_start(far_s[32 * j:32 * j + 32, :], src, allow_slow_non_contiguous=True).then_inc(s("near_s_in"), 16)
            pool.wait_ge(s("const_in"), 16)
            pool.wait_ge(s("h_ready"), KD)
            src = bass.AP(tensor=bias_dram.tensor, offset=P - 1, ap=[[TAB - 1, P], [P * TAB, AH], [1, 2 * P]])
            pool.dma_start(near, src).then_inc(s("near_in"), 16)
            for m in range(11):
                if m < 10:
                    pool.wait_ge(s("qk_var"), m + 1)
                    T = TILES[m % 5][1]
                    v8 = st[0:T, 16 * (m % 2):16 * (m % 2) + 8]
                    pool.tensor_tensor(st[0:T, 16 * (m % 2) + 8:16 * (m % 2) + 16], v8, minus_half[0:T, 0:8],
                                       ALU.pow).then_inc(s("qk_rstd"), 1)
                if m - 1 >= 5:
                    i = m - 6
                    pool.wait_ge(s("qk_tok"), m)
                    dst = (k_prompt[0, 0, P * i:P * i + P] if i < PT else k_sample[0].rearrange("b t h d -> (b t) h d"))
                    T = TILES[i][1]
                    pool.dma_start(dst.rearrange("t h d -> t (h d)"), tok[0:T, (m - 1) % 2, :]).then_inc(s(f"k_out{(m - 1) % 2}"), 16)
            pool.wait_ge(s("v_ready"), 5)
            pool.dma_start(v_prompt[0, 0].rearrange("(i p) h d -> p i (h d)", p=P), v_tok[:, 0:PT, :]).then_inc(s("v_out"), 16)
            pool.dma_start(v_sample[0].rearrange("b t h d -> (b t) (h d)"), v_tok[0:NS, PT, :]).then_inc(s("v_out"), 16)
            pool.wait_ge(s("k_out0"), 16 * 2)
            pool.wait_ge(s("k_out1"), 16 * 3)
            pool.wait_ge(s("v_out"), 32)
            for h in range(GH):
                if h:
                    pool.wait_ge(s("state_s_out"), 16 * h)
                else:
                    pool.wait_ge(s("oa_taken"), DEC_B)
                pool.dma_start(state_s, state_gla[0, :, h].rearrange("b k v -> k b v")).then_inc(s("state_s_in"), 16)
                for i, (_, T) in enumerate(TILES):
                    n = 5 * h + i
                    pool.wait_ge(s("og_raw"), n + 1)
                    pool.tensor_tensor(og[0:T, i, :], og[0:T, i, :], ong[0:T, :], ALU.mult).then_inc(s("og_ready"), 1)
                for i, (_, T) in enumerate(TILES):
                    n = 5 * h + i
                    pool.wait_ge(s("o_var"), n + 1)
                    c = 64 + 2 * (n % 2)
                    pool.tensor_tensor(st[0:T, c + 1:c + 2], st[0:T, c:c + 1], minus_half[0:T, 0:1], ALU.pow).then_inc(s("o_rstd"), 1)
                    if i == 3:
                        pool.wait_ge(s("state_new"), NCH * (h + 1))
                        pool.dma_start(state_prompt[0, 0, h], state[:, NCH % 2, :]).then_inc(s("state_p_out"), 16)
                pool.wait_ge(s("state_s_new"), DEC_B * (h + 1))
                pool.dma_start(state_sample[0, :, h].rearrange("b k v -> k b v"), state_s).then_inc(s("state_s_out"), 16)
            pool.wait_ge(s("state_s_out"), 16 * GH)
            pool.wait_ge(s("state_p_out"), 16 * GH)
            for t in range(KD):
                pool.wait_ge(s("m_ready"), t + 1)
                pool.tensor_tensor(halves(mergedT[:, t, :]), halves(m_a[:, t % 2, :]), halves(m_b[:, t % 2, :]), ALU.add).then_inc(s("merged"), 1)
            pool.memset(zero_rows, 0.0).then_inc(*done("zero_rows"))
            pool.wait_ge(*after("zero_rows"))
            dst = y_dram.rearrange("(r b) c -> r b c", b=EB)[:, NE:, :]
            pool.dma_start(dst, bc(zero_rows.unsqueeze(1), [CAP, MORE, D])).then_inc(s("y_cleared"), 16)
            pool.dma_start(wr[:, :, 0:NG], w_router_group[0].rearrange("(k p) c -> p k c", p=P)).then_inc(s("router_in"), 16)
            pool.dma_start(wr[:, :, NG:NG + NE], w_router_expert[0].rearrange("(k p) c -> p k c", p=P)).then_inc(s("router_in"), 16)
            pool.dma_start(brow[:, 0:NG], b_router_group).then_inc(s("router_in"), 16)
            pool.dma_start(brow[:, NG:NG + NE], b_router_expert).then_inc(s("router_in"), 16)
            for i, (t0, T) in enumerate(TILES):
                pool.wait_ge(s("h2_tok"), i + 1)
                pool.dma_start(h2_dram[t0:t0 + T, :], h2_tok[0:T, i, :]).then_inc(s("h2_out"), 16)
            pool.wait_ge(s("slots_cleared"), 16)
            pool.wait_ge(*after("dest_ready"))
            for i, (t0, T) in enumerate(TILES):
                for c in range(2):
                    pool.indirect_dma_start(slot_dram[:, :], bass.IndirectOffsetOnAxis(ap=dest_i[0:T, c, i:i + 1], axis=0),
                                            tok_i[0:T, i:i + 1], None).then_inc(s("slots_set"), 16)
            pool.wait_ge(s("slots_set"), 160)
            pool.dma_start(idx[:, :], slot_dram.rearrange("(r b) a -> r (b a)", b=EB)).then_inc(s("idx_in"), 16)
            pool.wait_ge(s("h2_out"), 80)
            pool.wait_ge(s("idx_in"), 16)
            pool.wait_ge(*after("g_tr"))
            for e in range(NE):
                if e >= 2:
                    pool.wait_ge(s("xs_tr"), e - 1)
                pool.indirect_dma_start(xs[e % 2], None, h2_dram[:, :],
                                        bass.IndirectOffsetOnAxis(ap=idx[:, e:e + 1], axis=0)).then_inc(s(f"xs_in{e % 2}"), 16)
            turns = pool.alloc_register("turns")
            pool.reg_mov(turns, 1)

            def more(c):
                pool.wait_ge(s("idx_cur"), turns)
                pool.reg_add(turns, turns, 1)
                pool.wait_ge(s("y_cleared"), 16)
                pool.indirect_dma_start(xs[0], None, h2_dram[:, :],
                                        bass.IndirectOffsetOnAxis(ap=idx_cur[:, 0:1], axis=0)).then_inc(s("xs_in0"), 16)

            further_blocks(pool, more)
            pool.wait_ge(s("y_cleared"), 16)
            pool.wait_ge(*after("rows_out"))
            for i, (_, T) in enumerate(TILES):
                if i >= 2:
                    pool.wait_ge(s(f"y_out{i % 2}"), 16 * (i // 2))
                for c, v in ((0, ya), (1, yb)):
                    pool.indirect_dma_start(v[0:T, i % 2, :], None, y_dram[:, :],
                                            bass.IndirectOffsetOnAxis(ap=dest_i[0:T, c, i:i + 1], axis=0)).then_inc(s(f"ya_in{i % 2}"), 16)

        @blk.scalar
        def _(act):
            act.dma_start(cst[:, :], shape_table[:, 0:KEPT]).then_inc(s("const_in"), 16)
            act.dma_start(hot, shape_table[0:BUCKETS + 1, KEPT:]).then_inc(s("small_in"), 16)
            act.dma_start(crow[0:1, 0, :], c_prompt).then_inc(s("c_in"), 16)
            act.dma_start(crow[1:DEC_B + 1, 0, :], c_sample).then_inc(s("c_in"), 16)
            act.dma_start(vrow[0:48, :], b_ada[0].rearrange("(a p) -> a p", p=P)).then_inc(s("vec_in"), 16)
            act.dma_start(vrow[48:56, :], norm1_g[0].rearrange("(a p) -> a p", p=P)).then_inc(s("vec_in"), 16)
            act.dma_start(vrow[56:64, :], norm2_g[0].rearrange("(a p) -> a p", p=P)).then_inc(s("vec_in"), 16)
            act.dma_start(x_tok[:, 0:PT, :], x_prompt[0].rearrange("(i p) d -> p i d", p=P)).then_inc(s("x_in"), 16)
            act.dma_start(x_tok[0:NS, PT, :], x_sample.rearrange("b t d -> (b t) d")).then_inc(s("x_in"), 16)
            act.wait_ge(*after("rbx_set"))
            act.dma_start(rbx[0:BUCKETS, :], rel_bias).then_inc(s("small_in"), 16)
            act.dma_start(ptab[:, :], page_table.rearrange("(a b) n -> a (b n)", a=1)).then_inc(s("page_table_in"), 16)

            def rows(v, n):
                return bass.AP(tensor=v.tensor, offset=v.offset, ap=[[0, P], [1, n]])

            act.dma_start(qkg[:, 0, :], rows(q_norm_g, AD)).then_inc(s("small_in"), 16)
            act.dma_start(qkg[:, 1, :], rows(k_norm_g, AD)).then_inc(s("small_in"), 16)
            act.dma_start(ong[:, :], rows(o_norm_g, GDV)).then_inc(s("small_in"), 16)
            act.dma_start(wgk[:, :, :], w_in[0].rearrange("(k p) c -> p k c", p=P)[:, :, OFF["gk"]:OFF["gk"] + RANK]).then_inc(s("small_in"), 16)
            act.dma_start(gk2[0:RANK, :], w_gk2[0]).then_inc(s("small_in"), 16)
            act.dma_start(gk2[RANK:, :], b_gk).then_inc(s("small_in"), 16)

            act.wait_ge(s("c_in"), 32)
            act.activation(crow[:, 1, :], crow[:, 0, :], ACT.Silu).then_inc(*done("c_silu"))
            for h in range(AH):
                act.wait_ge(s("bias_ps"), h + 1)
                if h >= 2:
                    act.wait_ge(s(f"bias_out{h % 2}"), 16 * (h // 2))
                act.activation(bias_stage[:, h % 2, :], ps[:, 6 + h % 2, 0:TAB], ACT.Copy)
                act.activation(rbfar[:, h:h + 1], ps[:, 6 + h % 2, 0:1], ACT.Copy).then_inc(s("bias_copied"), 1)
            for k in range(KD):
                act.wait_ge(s("xT_ready"), k + 1)
                if k >= 2:
                    act.wait_ge(s("sq_used"), k - 1)
                act.activation(sq[:, k % 2, :], xT[:, k, :], ACT.Square).then_inc(s("sq_ready"), 1)
            act.wait_ge(*after("var_ready"))
            act.activation(rstd, var, ACT.Sqrt).then_inc(*done("rstd_ready"))
            for n in range(15):
                t0, T = TILES[n % 5]
                act.wait_ge(s("pj"), n + 1)
                if n == 0:
                    act.wait_ge(s("h_ready"), KD)
                if n < 10:
                    if n:
                        act.wait_ge(s("qk_var"), n)
                    act.activation(tok_sq[0:T, :], ps[0:T, n % 4, :], ACT.Square).then_inc(s("qk_sq"), 1)
                else:
                    act.activation(v_tok[0:T, n % 5, :], ps[0:T, n % 4, :], ACT.Copy).then_inc(s("v_ready"), 1)
            for x in range(33):
                if x < 32:
                    n = P * (x % 4 + 1)
                    c = 32 + 4 * (x % 2)
                    act.wait_ge(s("sc_max"), x + 1)
                    act.activation(sc_p[:, x % 2, 0:n], sc_p[:, x % 2, 0:n], ACT.Exp, bias=st[:, c:c + 1],
                                   accum_out=st[:, c + 1:c + 2]).then_inc(s("sc_exp"), 1)
                if x >= 1:
                    y = x - 1
                    act.wait_ge(s("p_tr"), y + 1)
                    if y >= 2:
                        act.wait_ge(s("p_pv"), y - 1)
                    act.activation(pt_p[:, y % 2, 0:P * (y % 4 + 1)], ps[:, 2 + y % 2, 0:P * (y % 4 + 1)], ACT.Copy).then_inc(s("p_T"), 1)
            act.wait_ge(s("p_ov"), 32)
            act.wait_ge(s("p_pv"), 32)
            act.wait_ge(s("k_out0"), 16 * 2)
            act.wait_ge(s("k_out1"), 16 * 3)
            for g in range(2):
                for pg in range(64 * g, 64 * g + 64):
                    act.wait_ge(s("page_tr"), pg + 1)
                    if pg >= 3:
                        act.wait_ge(s("page_sc"), pg - 2)
                    act.activation(kpage[:, pg % 3, :], ps[:, pg % 3, :], ACT.Copy).then_inc(s("page_T"), 1)
                act.wait_ge(s("l_max"), g + 1)
                act.activation(logit, logit, ACT.Exp, bias=st[:, 48:49], accum_out=st[:, 49:50]).then_inc(s("l_exp"), 1)
                for q in range(5):
                    act.wait_ge(s("pr_tr"), 5 * g + q + 1)
                    if q == 0 and g:
                        act.wait_ge(s("pv_s"), 4 * g)
                    if q < 4:
                        act.activation(prT[:, 4 * q:4 * q + 4, :], grid(ps[:, 6 + q % 2, :], 4), ACT.Copy).then_inc(s("pr_T"), 1)
                    else:
                        act.activation(prT[0:NS, PAGES, :], ps[0:NS, 3, 384:512], ACT.Copy).then_inc(s("pr_T"), 1)
            act.wait_ge(*after("gk_ps"))
            act.wait_ge(*after("gk_ones"))
            act.wait_ge(s("v_out"), 32)
            act.activation(halves(gkT[0:RANK, :]), wide(0, RANK), ACT.Copy).then_inc(*done("gk_ready"))
            for h in range(GH):
                act.wait_ge(s("la_min"), h + 1)
                parts = [(ps[:, 0, :], la[:, 0:512], kend.rearrange("p a b -> p (a b)")[:, 0:512]),
                         (ps[0:NS, 1, 0:P], la[0:NS, 512:640], kend.rearrange("p a b -> p (a b)")[0:NS, 512:640])]
                for a, b, c in parts:
                    act_chain(act, act.activation(c, a, ACT.Abs))
                    act_chain(act, act.activation(c, c, ACT.Exp, scale=-1.0))
                    last = act.activation(c, c, ACT.Ln, bias=1.0)
                last.then_inc(s("la_ln"), 1)
                act.wait_ge(s("cum_ps"), h + 1)
                for a, b in ((ps[:, 2, :], slice(0, SEQ)), (ps[:, 3, 0:NS], sample)):
                    act.activation(e_cum[:, b], a, ACT.Exp)
                    last = act.activation(e_neg[:, b], a, ACT.Exp, scale=-1.0)
                last.then_inc(s("e_ready"), 1)
                act.wait_ge(s("end_ready"), h + 1)
                act.activation(e_end, e_end, ACT.Exp).then_inc(s("e_end"), 1)
                for i, (_, T) in enumerate(TILES):
                    act.wait_ge(s("v_ps"), 3 * h + i // 2 + 1)
                    act.activation(v_g[0:T, i, :], ps[0:T, i // 2, GDV * (i % 2):GDV * (i % 2) + GDV], ACT.Copy).then_inc(s("vg_ready"), 1)
                for i, (_, T) in enumerate(TILES):
                    act.wait_ge(s("og_ps"), 3 * h + i // 2 + 1)
                    act.activation(og[0:T, i, :], ps[0:T, 4 + i // 2, GDV * (i % 2):GDV * (i % 2) + GDV], ACT.Silu).then_inc(s("og_raw"), 1)
                act.wait_ge(s("kend_tr"), h + 1)
                act.activation(kend[:, 0:4, :], grid(ps[:, 3, :], 4), ACT.Copy)
                act.activation(kend[0:NS, 4, :], ps[0:NS, 7, 0:P], ACT.Copy).then_inc(s("kend_ready"), 1)
                for i, (t0, T) in enumerate(TILES):
                    n = 5 * h + i
                    act.wait_ge(*((s("inter"), (NCH - 1) * h + CPT * i + CPT - 1) if i < PT else (s("o_ps"), h + 1)))
                    if n >= 1:
                        act.wait_ge(s("o_var"), n)
                    act.activation(junk[0:T, :], ps[0:T, i % 2, 0:GDV], ACT.Square,
                                   accum_out=st[0:T, 60:61]).then_inc(s("o_sq"), 1)
                    act.wait_ge(s("on_tr"), n + 1)
                    act.activation(o_gT[:, 2 * h:2 * h + 2, t0:t0 + T], grid(ps[:, 3, 0:2 * T], 2), ACT.Copy).then_inc(s("og_T"), 1)
            act.wait_ge(s("state_p_out"), 16 * GH)
            act.wait_ge(s("state_s_out"), 16 * GH)
            for t in range(KD):
                act.wait_ge(s("ga_ps"), t + 1)
                if t >= 2:
                    act.wait_ge(s("merged"), t - 1)
                act.activation(halves(m_a[:, t % 2, :]), wide(0), ACT.Sigmoid).then_inc(s("ga_sig"), 1)
                act.wait_ge(s("gb_ps"), t + 1)
                act.activation(halves(m_b[:, t % 2, :]), wide(1), ACT.Sigmoid).then_inc(s("gb_sig"), 1)
            for k in range(KD):
                act.wait_ge(s("x1T"), k + 1)
                if k == 0:
                    act.wait_ge(s("out_ps"), KD)
                if k >= 2:
                    act.wait_ge(s("sq_used"), KD + k - 1)
                act.activation(sq2[:, k % 2, :], xT[:, k, :], ACT.Square).then_inc(s("sq_ready"), 1)
            act.wait_ge(*after("var2_ready"))
            act.activation(rstd2, var2, ACT.Sqrt).then_inc(*done("rstd2_ready"))
            for i, (_, T) in enumerate(TILES):
                act.wait_ge(s("x1_tr"), i + 1)
                act.activation(x1_tok[0:T, i, :].rearrange("p (a b) -> p a b", a=2), ps[0:T, 2:4, :], ACT.Copy).then_inc(s("x1_tok"), 1)
            act.wait_ge(*after("lg_max"))
            act.activation(both[:, :, 0:NG], both[:, :, 0:NG], ACT.Exp).then_inc(*done("lg_exp"))
            act.wait_ge(*after("e_gap"))
            act.activation(st[:, 200:205], st[:, 200:205], ACT.Exp).then_inc(*done("e_gap_exp"))
            act.wait_ge(*after("g_tr"))
            act.activation(grid(g2p, 2), ps[:, 4:6, :], ACT.Copy)
            act.activation(grid(g2s, 2), ps[0:NS, 6:8, :], ACT.Copy).then_inc(*done("g_rows"))
            def act_down(e, par):
                act.wait_ge(s("ye_ready"), e + 1)
                dst = y_dram.rearrange("(r b) c -> r b c", b=EB)[:, bass.DynSlice(e, 1), :]
                act.dma_start(dst, ye[par].unsqueeze(1)).then_inc(s(f"ye_out{par}"), 16)

            def act_step(e, par, before):
                act.wait_ge(s("xs_tr"), e + 1)
                act.activation(xsT[par], ps[:, par, :], ACT.Copy).then_inc(s("xsT"), 1)
                if before:
                    act_down(e - 1, 1 - par)
                act.wait_ge(w_used, e * 3 + (EXP_USED + 2))
                act.activation(hid[par], ps[:, 2 + par, 0:256], ACT.Silu).then_inc(s("hid_gate"), 1)

            act_step(0, 0, False)
            with act.Fori(0, NE // 2 - 1) as i:
                act_step(2 * i + 1, 1, True)
                act_step(2 * i + 2, 0, True)
            act_step(NE - 1, 1, True)
            act_down(NE - 1, 1)

            def more(c):
                act_step(c + NE, 0, False)
                act_down(c + NE, 0)

            count = further_blocks(act, more)
            act.wait_ge(s("ye_out1"), 16 * (NE // 2))
            act.wait_ge(s("ye_out0"), count * 16 + 16 * (NE // 2))
            act.activation(st[0:1, 250:251], st[0:1, 200:201], ACT.Copy).then_inc(*done("rows_out"))
            for i, (t0, T) in enumerate(TILES):
                act.wait_ge(s("y_ready"), i + 1)
                dst = y_prompt[0, t0:t0 + T, :] if i < PT else y_sample.rearrange("b t d -> (b t) d")
                act.dma_start(dst, ya[0:T, i % 2, :]).then_inc(s(f"y_out{i % 2}"), 16)
            act.wait_ge(s("y_out0"), 48)
            act.wait_ge(s("y_out1"), 32)
        @blk.vector
        def _(dve):
            link = lambda ins: dve_chain(dve, ins)
            dve.memset(rbx[:, :], NEG).then_inc(*done("rbx_set"))
            dve.memset(qbd, 0.0)
            dve.memset(own_s, NEG).then_inc(*done("sample_set"))
            dve.wait_ge(*after("sample_set"))
            dve.wait_ge(s("small_in"), 16 * 8)
            dve.wait_ge(s("const_in"), 16)
            link(dve.tensor_scalar(qkg[:, 0, :], qkg[:, 0, :], AD ** -0.5, None, ALU.mult))
            dve.tensor_copy(rbw.rearrange("b (h p) -> b h p", h=AH), bc(rbx[:, :].unsqueeze(2), [BUCKETS + 1, AH, P])).then_inc(*done("rbw_ready"))
            dve.wait_ge(*after("c_tr"))
            dve.tensor_copy(cT[:, :, :], grid(ps[:, 5, 0:72], KD)).then_inc(*done("cT"))
            link(dve.tensor_copy(vT[:, :], ps[:, 5, 128:192]))
            for k in range(KD):
                dve.wait_ge(s("x_tr"), k + 1)
                w = k % 2
                dve.tensor_copy(xT[:, k, 0:SEQ], ps[:, 2 * w, :])
                dve.tensor_copy(xT[:, k, sample], ps[:, 2 * w + 1, 0:NS]).then_inc(s("xT_ready"), 1)
            dve.wait_ge(s("sq_used"), KD)
            link(dve.tensor_scalar(halves(var), wide(3), 1.0 / D, EPS, ALU.mult, ALU.add))
            dve.reciprocal(var, var).then_inc(*done("var_ready"))
            dve.wait_ge(w_used, len(ADA))
            flat_mod = mod[:, :, :, :].rearrange("p a k c -> p (a k) c")
            link(dve.tensor_tensor(flat_mod, grid(ps[:, 4, 0:432], 48), bc(vT[:, 0:48].unsqueeze(2), [P, 48, DEC_B + 1]), ALU.add))
            for a in range(2):
                last = dve.scalar_tensor_tensor(gain[:, a, :, :], mod[:, 3 * a + 1, :, :], 1.0,
                                                bc(vT[:, 48 + 8 * a:56 + 8 * a].unsqueeze(2), [P, KD, DEC_B + 1]), ALU.add, ALU.mult)
            link(last)

            def by_sequence(v):
                return v.rearrange("p (b t) -> p b t", t=DEC_T)

            def modulate(a, r, ready):
                for k in range(KD):
                    last = dve.tensor_tensor(hT[:, k, :], xT[:, k, :], r, ALU.mult)
                link(last)
                for k in range(KD):
                    dve.tensor_scalar(hT[:, k, 0:SEQ], hT[:, k, 0:SEQ], gain[:, a, k, 0:1], mod[:, 3 * a, k, 0:1], ALU.mult, ALU.add)
                    last = dve.tensor_tensor(by_sequence(hT[:, k, sample]), by_sequence(hT[:, k, sample]),
                                             bc(gain[:, a, k, 1:].unsqueeze(2), [P, DEC_B, DEC_T]), ALU.mult)
                link(last)
                for k in range(KD):
                    dve.tensor_tensor(by_sequence(hT[:, k, sample]), by_sequence(hT[:, k, sample]),
                                      bc(mod[:, 3 * a, k, 1:].unsqueeze(2), [P, DEC_B, DEC_T]), ALU.add).then_inc(s(ready), 1)

            dve.wait_ge(*after("rstd_ready"))
            modulate(0, rstd, "h_ready")
            dve.wait_ge(s("near_s_in"), 16 * 8)
            for g in range(2):
                for j in range(4):
                    q = slice(32 * j, 32 * j + 32)
                    b = DEC_T * (4 * g + j)
                    dve.tensor_copy(own_s[q, g, b:b + DEC_T], near_s[q, PAGE:PAGE + DEC_T])
            for m in range(11):
                if m < 10:
                    t0, T = TILES[m % 5]
                    c = 16 * (m % 2)
                    dve.wait_ge(s("qk_sq"), m + 1)
                    link(dve.tensor_reduce(st[0:T, c:c + 8], tok_sq[0:T, :].rearrange("p (h d) -> p h d", h=AH), AX.X, ALU.add))
                    dve.tensor_scalar(st[0:T, c:c + 8], st[0:T, c:c + 8], 1.0 / AD, EPS, ALU.mult, ALU.add).then_inc(s("qk_var"), 1)
                if m:
                    y = m - 1
                    t0, T = TILES[y % 5]
                    dve.wait_ge(s("qk_tr"), y + 1)
                    dst = (qT, kT)[y // 5]
                    dve.tensor_copy(dst[:, :, t0:t0 + T], grid(ps[:, 4 + y % 2, 0:4 * T], PAIRS)).then_inc(s("qk_T"), 1)
                if m < 10:
                    t0, T = TILES[m % 5]
                    c = 16 * (m % 2)
                    dve.wait_ge(s("qk_rstd"), m + 1)
                    if m >= 7:
                        dve.wait_ge(s(f"k_out{m % 2}"), 16 * ((m - 5) // 2))
                    v = tok[0:T, m % 2, :].rearrange("p (h d) -> p h d", h=AH)
                    dve.tensor_tensor(v, grid(ps[0:T, m % 4, :], AH), bc(st[0:T, c + 8:c + 16].unsqueeze(2), [T, AH, AD]),
                                      ALU.mult).then_inc(s("pj_free"), 1)
                    dve.wait_ge(s("pj_free"), m + 1)
                    dve.tensor_tensor(v, v, bc(qkg[0:T, m // 5, :].unsqueeze(1), [T, AH, AD]), ALU.mult).then_inc(s("qk_tok"), 1)
            dve.wait_ge(s("qk_T"), 10)
            for a in range(2):
                rows = slice(64 * a, 64 * a + 64)
                last = dve.tensor_copy(qbd[rows, :, :, 4 * a:4 * a + 4],
                                       qT[rows, :, sample].rearrange("p a (b t) -> p a b t", t=DEC_T))
            last.then_inc(*done("qbd"))
            dve.wait_ge(s("near_in"), 16)
            for x in range(32 + 3):
                if x < 32:
                    h, i = x // 4, x % 4
                    c = 32 + 4 * (x % 2)
                    n = P * (i + 1)
                    far = P * max(i - 1, 0)
                    dve.wait_ge(s("sc_ps"), x + 1)
                    if x >= 2:
                        dve.wait_ge(s("p_tr"), x - 1)
                    if far:
                        dve.tensor_scalar(sc_p[:, x % 2, 0:far], ps[:, x % 2, 0:far], rbfar[:, h:h + 1], None, ALU.add)
                    link(dve.tensor_tensor(sc_p[:, x % 2, far:n], ps[:, x % 2, far:n], near[:, h, 2 * P - (n - far):2 * P], ALU.add))
                    dve.tensor_reduce(st[:, c:c + 1], sc_p[:, x % 2, 0:n], AX.X, ALU.max, negate=True).then_inc(s("sc_max"), 1)
                if 1 <= x <= 32:
                    y = x - 1
                    c = 32 + 4 * (y % 2)
                    n = P * (y % 4 + 1)
                    dve.wait_ge(s("sc_exp"), y + 1)
                    link(dve.reciprocal(st[:, c + 2:c + 3], st[:, c + 1:c + 2]))
                    dve.tensor_scalar(sc_p[:, y % 2, 0:n], sc_p[:, y % 2, 0:n], st[:, c + 2:c + 3], None, ALU.mult).then_inc(s("p_norm"), 1)
                if x >= 3:
                    y = x - 3
                    h, i = y // 4, y % 4
                    rows = slice(64 * (h % 2), 64 * (h % 2) + 64)
                    dve.wait_ge(s("p_pv"), y + 1)
                    dve.tensor_copy(o_aT[rows, h // 2, P * i:P * i + P], ps[rows, 4 + y % 2, 0:P]).then_inc(s("p_ov"), 1)
            dve.wait_ge(*after("own_ps"))
            dve.tensor_copy(own_T[:, :], ps[0:NS, 3, 0:256]).then_inc(*done("own_T"))
            for g in range(2):
                for j in range(4):
                    b = 4 * g + j
                    dve.wait_ge(s("page_sc"), PAGES * (b + 1))
                    if g and j == 0:
                        dve.wait_ge(s("l_tr"), 5)
                    dve.tensor_copy(scT[:, :, 32 * j:32 * j + 32], grid(ps[:, 4 + b % 2, :], PAGES)).then_inc(s("scT"), 1)
                for q in range(4):
                    dve.wait_ge(s("l_tr"), 5 * g + q + 1)
                    if g and q == 0:
                        dve.wait_ge(s("pr_tr"), 5)
                    dve.tensor_copy(logit[:, 512 * q:512 * q + 512], ps[:, 6 + q % 2, :]).then_inc(s("l_taken"), 1)
                dve.wait_ge(s("l_tr"), 5 * g + 5)
                dve.tensor_tensor(logit[:, PAST:], ps[:, 3, 256:256 + NS], own_s[:, g, :], ALU.add).then_inc(s("l_taken"), 1)
                dve.wait_ge(s("l_taken"), 5 * g + 5)
                gate, comb = st[:, 80:88], st[:, 88:96]
                link(dve.tensor_reduce(gate, grid(logit[:, 0:PAST], NBLK), AX.X, ALU.add))
                c0, c1 = grid(cmp8[:, 0, 0:64], 8), grid(cmp8[:, 1, 0:64], 8)
                gi, gj = bc(gate.unsqueeze(1), [P, 8, 8]), bc(gate.unsqueeze(2), [P, 8, 8])
                link(dve.tensor_tensor(c0, gi, gj, ALU.is_equal))
                link(dve.tensor_tensor(c0, c0, grid(own_lower8, 8), ALU.mult))
                link(dve.tensor_tensor(c1, gi, gj, ALU.is_gt))
                link(dve.tensor_tensor(c0, c0, c1, ALU.add))
                link(dve.tensor_reduce(comb, c0, AX.X, ALU.add))
                link(dve.tensor_scalar(comb, comb, float(TOPK), NEG, ALU.is_ge, ALU.mult))
                near_part = logit[:, PAST - PAGE:PAST]
                link(dve.scalar_tensor_tensor(near_part, near_part, comb[:, 7:8], near_s[:, 0:PAGE], ALU.add, ALU.add))
                link(dve.tensor_scalar(comb, comb, far_s[:, 0:1], None, ALU.add))
                v = grid(logit[:, 0:PAST - BLK], NBLK - 1)
                dve.tensor_tensor(v, v, bc(comb[:, 0:7].unsqueeze(2), [P, NBLK - 1, BLK]), ALU.add)
                v = logit[:, PAST - BLK:PAST - PAGE]
                link(dve.tensor_scalar(v, v, comb[:, 7:8], None, ALU.add))
                dve.tensor_reduce(st[:, 48:49], logit, AX.X, ALU.max, negate=True).then_inc(s("l_max"), 1)
                dve.wait_ge(s("l_exp"), g + 1)
                link(dve.reciprocal(st[:, 50:51], st[:, 49:50]))
                dve.tensor_scalar(logit, logit, st[:, 50:51], None, ALU.mult).then_inc(s("l_norm"), 1)
                for j in range(4):
                    b = 4 * g + j
                    dve.wait_ge(s("pv_s"), b + 1)
                    for a in range(2):
                        rows = slice(64 * a, 64 * a + 64)
                        last = dve.tensor_copy(o_aT[rows, :, SEQ + DEC_T * b:SEQ + DEC_T * b + DEC_T],
                                               grid(ps[rows, 4 + b % 2, 0:32], PAIRS)[:, :, 4 * a:4 * a + 4])
                    last.then_inc(s("oa_taken"), 1)
            dve.wait_ge(s("v_out"), 32)
            dve.memset(att.rearrange("p a b -> p (a b)"), 0.0).then_inc(*done("att_set"))
            dve.memset(gkT, 1.0).then_inc(*done("gk_ones"))
            link(dve.memset(q_mask, 0.0))
            link(dve.memset(on_[0:NS, :, :], 0.0))
            for h in range(GH):
                dve.wait_ge(s("la_ps"), h + 1)
                parts = [(ps[:, 0, :], la[:, 0:512], kend.rearrange("p a b -> p (a b)")[:, 0:512]),
                         (ps[0:NS, 1, 0:P], la[0:NS, 512:640], kend.rearrange("p a b -> p (a b)")[0:NS, 512:640])]
                for a, b, c in parts:
                    last = dve.tensor_scalar(b, a, 0.0, None, ALU.min)
                last.then_inc(s("la_min"), 1)
                dve.wait_ge(s("la_min"), h + 1)
                dve.wait_ge(s("la_ln"), h + 1)
                for a, b, c in parts:
                    last = dve.tensor_tensor(b, b, c, ALU.subtract)
                link(last)
                for a, b, c in parts:
                    last = dve.tensor_scalar(b, b, 1.0 / GNORM, None, ALU.mult)
                last.then_inc(s("la_ready"), 1)
                dve.wait_ge(s("e_ready"), h + 1)
                dve.tensor_copy(e_end[:, 0:SEQ], ps[:, 2, :])
                link(dve.tensor_copy(e_end[:, sample], ps[:, 3, 0:NS]))
                for v, src, n, w in ((e_end[:, 0:SEQ], ps[:, 2, :], NCH, CHUNK), (e_end[:, sample], ps[:, 3, 0:NS], DEC_B, DEC_T)):
                    last = dve.tensor_tensor(grid(v, n), bc(grid(src, n)[:, :, w - 1:w], [P, n, w]), grid(v, n), ALU.subtract)
                last.then_inc(s("end_ready"), 1)
                decay = st[:, 100:124]
                dve.tensor_copy(decay[:, 0:NCH].unsqueeze(2), grid(e_cum[:, 0:SEQ], NCH)[:, :, CHUNK - 1:CHUNK])
                link(dve.tensor_copy(decay[:, NCH:].unsqueeze(2), grid(e_cum[:, sample], DEC_B)[:, :, DEC_T - 1:DEC_T]))
                dve.wait_ge(s("qk_ps"), h + 1)
                dve.scalar_tensor_tensor(halves(e_cum), wide(2), GDK ** -0.5, halves(e_cum), ALU.mult, ALU.mult)
                link(dve.tensor_tensor(halves(e_neg), wide(3), halves(e_neg), ALU.mult))
                dve.wait_ge(s("e_end"), h + 1)
                dve.tensor_tensor(halves(e_end), wide(3), halves(e_end), ALU.mult).then_inc(s("qkt_ready"), 1)
                dve.tensor_copy(grid(q_mask, DEC_B)[:, :, 0:DEC_T], e_cum[:, sample].rearrange("p (b t) -> p b t", t=DEC_T))\
                   .then_inc(s("q_mask"), 1)
                def finish(i, T):
                    n = 5 * h + i
                    c = 64 + 2 * (n % 2)
                    dve.wait_ge(s("o_sq"), n + 1)
                    dve.tensor_scalar(st[0:T, c:c + 1], st[0:T, 60:61], 1.0 / GDV, EPS, ALU.mult, ALU.add).then_inc(s("o_var"), 1)
                    dve.wait_ge(s("o_rstd"), n + 1)
                    dve.wait_ge(s("og_ready"), n + 1)
                    dve.scalar_tensor_tensor(on_[0:T, n % 2, :], ps[0:T, i % 2, 0:GDV], st[0:T, c + 1:c + 2], og[0:T, i, :],
                                             ALU.mult, ALU.mult).then_inc(s("on_ready"), 1)

                def masked(i, T, mask, n):
                    dve.wait_ge(s("att_ps"), n + 1)
                    dst = att[:, i % 2, :] if T == P else cmp8[0:NS, 0, 0:NS]
                    dve.copy_predicated(dst, mask.bitcast(U32), ps[0:T, 2, P * (i % 2):P * (i % 2) + T]).then_inc(s("att_ready"), 1)

                for i in range(PT):
                    masked(i, P, const("chunk_causal"), 5 * h + i)
                    for c in range(CPT * i, CPT * i + CPT):
                        n = NCH * h + c
                        dve.wait_ge(s("u_ps"), n + 1)
                        new, old = state[:, (c + 1) % 2, :], state[:, c % 2, :]
                        if c == 0:
                            if h:
                                dve.wait_ge(s("state_p_out"), 16 * h)
                            dve.tensor_copy(new, ps[:, 4 + c % 4, 0:GDV]).then_inc(s("state_new"), 1)
                        else:
                            dve.wait_ge(s("state_new"), n)
                            dve.wait_ge(s("inter"), (NCH - 1) * h + c - 1)
                            dve.scalar_tensor_tensor(new, old, decay[:, c:c + 1], ps[:, 4 + c % 4, 0:GDV], ALU.mult, ALU.add)\
                               .then_inc(s("state_new"), 1)
                    finish(i, P)
                if h == 0:
                    link(dve.memset(cmp8[0:NS, 0, 0:NS], 0.0))
                masked(4, NS, const("seq_causal"), 5 * h + 4)
                dve.tensor_tensor(kend_m, bc(kend[0:NS, 4, :].unsqueeze(1), [NS, DEC_B, P]),
                                  bc(const("seq_member").unsqueeze(2), [NS, DEC_B, P]), ALU.mult).then_inc(s("kend_m"), 1)
                finish(4, NS)
                for b in range(DEC_B):
                    n = DEC_B * h + b
                    dve.wait_ge(s("us_ps"), n + 1)
                    dve.scalar_tensor_tensor(state_s[:, b, :], state_s[:, b, :], decay[:, NCH + b:NCH + b + 1],
                                             ps[:, 4 + b % 4, 0:GDV], ALU.mult, ALU.add).then_inc(s("state_s_new"), 1)
            for t in range(KD):
                for v, w, a in ((m_a, 2, "a"), (m_b, 3, "b")):
                    dve.wait_ge(s(f"g{a}_sig"), t + 1)
                    dve.wait_ge(s(f"p{a}_ps"), t + 1)
                    dve.tensor_tensor(halves(v[:, t % 2, :]), halves(v[:, t % 2, :]), wide(w), ALU.mult).then_inc(s("m_ready" if a == "b" else "m_half"), 1)
            for t in range(KD):
                w = 2 * (t % 3)
                dve.wait_ge(s("out_ps"), t + 1)
                g1 = mod[:, 2, t, 0:1]
                dve.scalar_tensor_tensor(xT[:, t, 0:HALF], ps[:, w, 0:HALF], g1, xT[:, t, 0:HALF], ALU.mult, ALU.add)
                dve.scalar_tensor_tensor(xT[:, t, HALF:SEQ], ps[:, w + 1, 0:SEQ - HALF], g1, xT[:, t, HALF:SEQ], ALU.mult, ALU.add)
                z = st[:, 128 + 32 * (t % 2):160 + 32 * (t % 2)]
                link(dve.tensor_tensor(by_sequence(z), by_sequence(ps[:, w + 1, SEQ - HALF:HALF]),
                                       bc(mod[:, 2, t, 1:].unsqueeze(2), [P, DEC_B, DEC_T]), ALU.mult))
                dve.tensor_tensor(xT[:, t, sample], xT[:, t, sample], z, ALU.add).then_inc(s("x1T"), 1)
            dve.wait_ge(s("sq_used"), 2 * KD)
            link(dve.tensor_scalar(halves(var2), wide(3), 1.0 / D, EPS, ALU.mult, ALU.add))
            dve.reciprocal(var2, var2).then_inc(*done("var2_ready"))
            dve.wait_ge(*after("rstd2_ready"))
            modulate(1, rstd2, "h2_ready")
            dve.wait_ge(s("h2_ready"), KD)
            for t in range(KD):
                dve.tensor_copy(g_exp[:, t, 0:P], bc(mod[:, 5, t, 0:1], [P, P]))
                last = dve.tensor_copy(by_sequence(g_exp[:, t, P:]), bc(mod[:, 5, t, 1:].unsqueeze(2), [P, DEC_B, DEC_T]))
            last.then_inc(*done("g_exp2"))
            for i, (_, T) in enumerate(TILES):
                dve.wait_ge(s("h2_tr"), i + 1)
                dve.tensor_copy(grid(h2_tok[0:T, i, :], 2), ps[0:T, 0:2, :]).then_inc(s("h2_tok"), 1)
            link(dve.memset(lg[:, :, :], 0.0))
            dve.wait_ge(*after("lg_ps"))
            dve.tensor_copy(lg[:, 0:PT, :], grid(ps[:, 6, 0:PT * 36], PT))
            link(dve.tensor_copy(lg[0:NS, PT, :], ps[0:NS, 6, PT * 36:5 * 36]))
            lgg = lg[:, :, 0:NG]
            W = P
            c0, c1 = (grid(cmp8[:, a, 0:80], 5).rearrange("p a (j i) -> p a j i", j=NG) for a in range(2))
            gsel = cmp8[:, 1, 128:148].rearrange("p (a j) -> p a j", a=5)

            def tie(dst, v, n, low):
                a = grid(cmp8[:, 0, 0:n * n], n)
                b = grid(cmp8[:, 1, 0:n * n], n)
                vi, vj = bc(v.unsqueeze(1), [P, n, n]), bc(v.unsqueeze(2), [P, n, n])
                link(dve.tensor_tensor(a, vi, vj, ALU.is_equal))
                link(dve.tensor_tensor(a, a, grid(low, n), ALU.mult))
                link(dve.tensor_tensor(b, vi, vj, ALU.is_gt))
                link(dve.tensor_tensor(a, a, b, ALU.add))
                link(dve.tensor_reduce(dst, a, AX.X, ALU.add))

            grank = cmp8[:, 1, 100:120].rearrange("p (a j) -> p a j", a=5)
            for i in range(5):
                tie(grank[:, i, :], lg[:, i, 0:NG], NG, own_lower4)
            link(dve.tensor_scalar(gsel, grank, 0.5, None, ALU.is_lt))
            gmax = st[:, 128:133]
            link(dve.tensor_reduce(gmax, lgg, AX.X, ALU.max))
            dve.tensor_tensor(both[:, :, 0:NG], lgg, bc(gmax.unsqueeze(2), [P, 5, NG]), ALU.subtract).then_inc(*done("lg_max"))
            dve.wait_ge(*after("lg_exp"))
            psum_g = st[:, 136:141]
            link(dve.tensor_reduce(psum_g, both[:, :, 0:NG], AX.X, ALU.add))
            pg = st[:, 144:149]
            link(dve.reciprocal(pg, psum_g))
            e4 = lg[:, :, NG:].rearrange("p a (g e) -> p a g e", g=NG)
            b4 = both[:, :, :].rearrange("p a (g e) -> p a g e", g=NG)
            link(dve.tensor_tensor(b4, e4, bc(gsel.unsqueeze(3), [P, 5, NG, EPG]), ALU.mult))
            ein = st[:, 152:192].rearrange("p (a e) -> p a e", a=5)
            link(dve.tensor_reduce(ein, both[:, :, :].rearrange("p a (g e) -> p a e g", g=NG), AX.X, ALU.add))
            erank = st[:, 208:248].rearrange("p (a e) -> p a e", a=5)
            for i in range(5):
                tie(erank[:, i, :], ein[:, i, :], EPG, own_lower8)
            hots = []
            for c, oh in ((0, one1), (1, one2)):
                r = cmp8[:, 0, 0:40].rearrange("p (a e) -> p a e", a=5)
                link(dve.tensor_scalar(r, erank, float(c), None, ALU.is_equal))
                o4 = oh[:, :, :].rearrange("p a (g e) -> p a g e", g=NG)
                for i in range(5):
                    dve.tensor_tensor(o4[:, i], bc(gsel[:, i, :].unsqueeze(2), [P, NG, EPG]), bc(r[:, i, :].unsqueeze(1), [P, NG, EPG]), ALU.mult)
                z = cmp8[:, 0, 40:80].rearrange("p (a e) -> p a e", a=5)
                link(dve.tensor_tensor(z, r, ein, ALU.mult))
                link(dve.tensor_reduce(st[:, 192 + 8 * c:197 + 8 * c], z, AX.X, ALU.add))
            dve.tensor_tensor(st[:, 200:205], st[:, 200:205], st[:, 192:197], ALU.subtract).then_inc(*done("e_gap"))
            real = bc(const("token_real").unsqueeze(2), [P, 5, NE])
            link(dve.tensor_tensor(both[:, :, :], one1[:, :, :], one2[:, :, :], ALU.add))
            dve.tensor_tensor(both[:, :, :], both[:, :, :], real, ALU.mult).then_inc(*done("chosen"))
            dve.wait_ge(*after("e_gap_exp"))
            den = st[:, 128:133]
            link(dve.tensor_scalar(den, st[:, 200:205], 1.0, None, ALU.add))
            link(dve.reciprocal(den, den))
            link(dve.tensor_tensor(wts[:, 0, :], den, pg, ALU.mult))
            link(dve.tensor_tensor(wts[:, 1, :], wts[:, 0, :], st[:, 200:205], ALU.mult))
            link(dve.tensor_copy(tok_i[:, :], const("token_id")))
            dve.wait_ge(*after("pos_ps"))
            link(dve.tensor_copy(cnt[:, :], ps[:, 7, 5 * NE:6 * NE]))
            over = blk_cmp[:, 0:NE * EDGES].rearrange("p (e c) -> p e c", e=NE)
            link(dve.tensor_tensor(over, bc(cnt[:, :].unsqueeze(2), [P, NE, EDGES]),
                                   bc(const("block_edge").unsqueeze(1), [P, NE, EDGES]), ALU.is_gt))
            link(dve.tensor_reduce(cnt[:, :], over, AX.X, ALU.add))
            ends = [cmp8[:, a, 0:NE] for a in range(2)]
            link(dve.tensor_copy(ends[0], cnt[:, :]))
            step = 1
            while step < NE:
                a, b = ends
                dve.tensor_copy(b[:, 0:step], a[:, 0:step])
                link(dve.tensor_tensor(b[:, step:], a[:, step:], a[:, 0:NE - step], ALU.add))
                ends, step = [b, a], 2 * step
            ends = ends[0]
            over = blk_cmp[:, 0:NE * MORE].rearrange("p (c e) -> p c e", c=MORE)
            link(dve.tensor_tensor(over, bc(ends.unsqueeze(1), [P, MORE, NE]), bc(const("more_id").unsqueeze(2), [P, MORE, NE]), ALU.is_le))
            link(dve.tensor_reduce(blk_cmp[:, 0:MORE], over, AX.X, ALU.add))
            link(dve.tensor_scalar(blk_cmp[:, 0:MORE], blk_cmp[:, 0:MORE], float(NE - 1), None, ALU.min))
            link(dve.tensor_copy(more_i[:, 0:MORE], blk_cmp[0:1, 0:MORE]))
            ids = const("expert_id")
            link(dve.tensor_tensor(base[:, :], ends, cnt[:, :], ALU.subtract))
            link(dve.tensor_tensor(base[:, :], base[:, :], ids, ALU.subtract))
            link(dve.tensor_scalar(base[:, :], base[:, :], float(CAP), float(CAP * (NE - 1)), ALU.mult, ALU.add))
            pos = grid(ps[:, 7, 0:5 * NE], 5)
            over = grid(blk_cmp[:, 0:5 * NE], 5)
            link(dve.tensor_scalar(over, pos, float(CAP), None, ALU.is_ge))
            link(dve.tensor_tensor(over, over, bc(base[:, :].unsqueeze(1), [P, 5, NE]), ALU.mult))
            link(dve.scalar_tensor_tensor(over, bc(ids.unsqueeze(1), [P, 5, NE]), float(CAP), over, ALU.mult, ALU.add))
            link(dve.tensor_tensor(both[:, :, :], over, pos, ALU.add))
            for c, oh in ((0, one1), (1, one2)):
                link(dve.tensor_tensor(oh[:, :, :], oh[:, :, :], both[:, :, :], ALU.mult))
                link(dve.tensor_reduce(dest[:, c, :], oh[:, :, :], AX.X, ALU.add))
            link(dve.tensor_copy(dest_i[:, :, :], dest[:, :, :]))
            link(dve.tensor_scalar(row_i[:, :, :], dest_i[:, :, :], CAP - 1, None, ALU.bitwise_and))
            link(dve.tensor_scalar(dest_i[:, :, :], dest_i[:, :, :], CAP.bit_length() - 1, None, ALU.logical_shift_right))
            dve.scalar_tensor_tensor(dest_i[:, :, :], row_i[:, :, :], float(EB), dest_i[:, :, :], ALU.mult, ALU.add)\
               .then_inc(*done("dest_ready"))
            dve.wait_ge(s("idx_in"), 16)
            dve.tensor_copy(more_i[:, MORE:], ends[0:1, NE - 1:NE]).then_inc(*done("more_ready"))
            def dve_down(e, it, par, first=False):
                dve.wait_ge(w_used, e * 3 + (EXP_USED + 3))
                if not first:
                    dve.wait_ge(s(f"ye_out{par}"), it * 16)
                dve.tensor_copy(grid(ye[par], 2), ps[0:CAP, 4 + 2 * par:6 + 2 * par, :]).then_inc(s("ye_ready"), 1)

            def dve_step(e, it, par, before):
                if before:
                    dve_down(e - 1, before[0], 1 - par, isinstance(before[0], int) and before[0] == 0)
                dve.wait_ge(w_used, e * 3 + (EXP_USED + 2))
                dve.wait_ge(s("hid_gate"), e + 1)
                dve.tensor_tensor(hid[par], hid[par], ps[:, 2 + par, 256:512], ALU.mult).then_inc(s("hid"), 1)

            dve_step(0, 0, 0, None)
            dve_step(1, 0, 1, (0,))
            dve_step(2, 1, 0, (0,))
            with dve.Fori(1, NE // 2 - 1) as i:
                dve_step(2 * i + 1, i, 1, (i,))
                dve_step(2 * i + 2, i + 1, 0, (i,))
            dve_step(NE - 1, NE // 2 - 1, 1, (NE // 2 - 1,))
            dve_down(NE - 1, NE // 2 - 1, 1)

            def more(c):
                dve.wait_ge(s("xs_tr"), c + NE)
                dve.tensor_copy(idx_cur[:, :], idx[:, bass.DynSlice(c + NE, 1)]).then_inc(s("idx_cur"), 1)
                dve_step(c + NE, c + NE // 2, 0, None)
                dve_down(c + NE, c + NE // 2, 0)

            further_blocks(dve, more)
            for i, (_, T) in enumerate(TILES):
                q = i % 2
                dve.wait_ge(s(f"ya_in{q}"), 32 * (i // 2) + 32)
                a, b = ya[0:T, q, :], yb[0:T, q, :]
                link(dve.tensor_scalar(a, a, wts[0:T, 0, i:i + 1], None, ALU.mult))
                link(dve.scalar_tensor_tensor(a, b, wts[0:T, 1, i:i + 1], a, ALU.mult, ALU.add))
                link(dve.tensor_tensor(a, a, g2p if i < PT else g2s, ALU.mult))
                dve.tensor_tensor(a, a, x1_tok[0:T, i, :], ALU.add).then_inc(s("y_ready"), 1)
        @blk.tensor
        def _(pe):
            def mm(out, lhsT, rhs, start, stop, **k):
                return pe.matmul(out, lhsT, rhs, start=start, stop=stop, **k)

            def product(w, lhs, rhs, K, rows=P):
                for half in range(2):
                    for k in range(K):
                        last = mm(ps[0:rows, 2 * w + half, 0:HALF], lhs(k), rhs(k)[:, HALF * half:HALF * half + HALF], k == 0, k == K - 1)
                return last

            def turn(out, v):
                n = v.shape[0]
                return pe.transpose(out, v, ident[0:n, 0:n])

            pe.wait_ge(s("const_in"), 16)
            pe.wait_ge(s("vec_in"), 48)
            turn(ps[:, 5, 128:192], vrow)
            pe.wait_ge(*after("c_silu"))
            for k in range(KD):
                last = turn(ps[:, 5, 9 * k:9 * k + 9], crow[:, 1, P * k:P * k + P])
            last.then_inc(*done("c_tr"))
            pe.wait_ge(*after("rbw_ready"))
            for h in range(AH):
                if h >= 2:
                    pe.wait_ge(s("bias_copied"), h - 1)
                mm(ps[:, 6 + h % 2, 0:TAB], rbw[:, P * h:P * h + P], hot, True, True).then_inc(s("bias_ps"), 1)
            pe.wait_ge(s("x_in"), 32)
            for k in range(KD + 1):
                if k < KD:
                    if k >= 2:
                        pe.wait_ge(s("xT_ready"), k - 1)
                    for i in range(PT):
                        turn(ps[:, 2 * (k % 2), P * i:P * i + P], x_tok[:, i, P * k:P * k + P])
                    turn(ps[:, 2 * (k % 2) + 1, 0:NS], x_tok[0:NS, PT, P * k:P * k + P]).then_inc(s("x_tr"), 1)
                if k:
                    y = k - 1
                    if y == 0:
                        pe.wait_ge(s("bias_copied"), AH)
                    pe.wait_ge(s("sq_ready"), y + 1)
                    for half in range(2):
                        last = mm(ps[:, 6 + half, 0:HALF], ones, sq[:, y % 2, HALF * half:HALF * half + HALF], y == 0, y == KD - 1)
                    last.then_inc(s("sq_used"), 1)
            pe.wait_ge(*after("cT"))
            for i, n in enumerate(ADA):
                landed(pe, n)
                w = grid(slot(n), KD)
                for t in range(4):
                    at = 9 * (4 * i + t)
                    for k in range(KD):
                        last = mm(ps[:, 4, at:at + 9], w[:, k, P * t:P * t + P], cT[:, k, :], k == 0, k == KD - 1)
                last.then_inc(w_used, 1)
            pe.wait_ge(s("h_ready"), KD)
            for n in range(15 + 1):
                if n < 15:
                    t0, T = TILES[n % 5]
                    b = QKV[n // 5]
                    landed(pe, b)
                    w = grid(slot(b), KD)
                    if 4 <= n < 14:
                        pe.wait_ge(s("pj_free"), n - 3)
                    elif n == 14:
                        pe.wait_ge(s("v_ready"), 1)
                    for k in range(KD):
                        last = mm(ps[0:T, n % 4, :], hT[:, k, t0:t0 + T], w[:, k, :], k == 0, k == KD - 1)
                    last.then_inc(s("pj"), 1)
                if 1 <= n <= 10:
                    y = n - 1
                    t0, T = TILES[y % 5]
                    pe.wait_ge(s("qk_tok"), y + 1)
                    if y >= 2:
                        pe.wait_ge(s("qk_T"), y - 1)
                    for a in range(PAIRS):
                        last = turn(ps[:, 4 + y % 2, T * a:T * a + T], tok[0:T, y % 2, P * a:P * a + P])
                    last.then_inc(s("qk_tr"), 1)
            pe.wait_ge(s("qk_T"), 10)
            pe.wait_ge(s("v_ready"), 5)
            for x in range(32 + 2):
                if x < 32:
                    h, i = x // 4, x % 4
                    rows = slice(64 * (h % 2), 64 * (h % 2) + 64)
                    n = P * (i + 1)
                    if x >= 2:
                        pe.wait_ge(s("sc_max"), x - 1)
                    mm(ps[:, x % 2, 0:n], qT[rows, h // 2, P * i:P * i + P], kT[rows, h // 2, 0:n], True, True).then_inc(s("sc_ps"), 1)
                if 1 <= x <= 32:
                    y = x - 1
                    pe.wait_ge(s("p_norm"), y + 1)
                    if y >= 2:
                        pe.wait_ge(s("p_T"), y - 1)
                    for j in range(y % 4 + 1):
                        last = turn(ps[:, 2 + y % 2, P * j:P * j + P], sc_p[:, y % 2, P * j:P * j + P])
                    last.then_inc(s("p_tr"), 1)
                if x >= 2:
                    y = x - 2
                    h, i = y // 4, y % 4
                    pe.wait_ge(s("p_T"), y + 1)
                    if y >= 2:
                        pe.wait_ge(s("p_ov"), y - 1)
                    rows = slice(64 * (h % 2), 64 * (h % 2) + 64)
                    for j in range(i + 1):
                        last = mm(ps[rows, 4 + y % 2, 0:P], v_tok[:, j, AD * h:AD * h + AD], pt_p[:, y % 2, P * j:P * j + P], j == 0, j == i)
                    last.then_inc(s("p_pv"), 1)
            pe.wait_ge(*after("qbd"))
            pe.wait_ge(s("p_ov"), 32)
            for a in range(PAIRS):
                last = mm(grid(ps[0:NS, 3, 0:256], DEC_B)[:, :, 8 * a:8 * a + 8], kT[:, a, sample], qbd[:, a, :, :], True, True)
            last.then_inc(*done("own_ps"))
            for g in range(2):
                for pg in range(64 * g, 64 * g + 65):
                    b, page = pg // PAGES, pg % PAGES
                    if pg < 64 * g + 64:
                        n = PAGED[("k", b, page // 8)]
                        landed(pe, n)
                        if pg >= 3:
                            pe.wait_ge(s("page_T"), pg - 2)
                        for a in range(PAIRS):
                            last = turn(ps[:, pg % 3, P * a:P * a + P], slot(n)[:, AW * (page % 8) + P * a:AW * (page % 8) + P * a + P])
                        last.then_inc(s("page_tr"), 1)
                    if pg > 64 * g:
                        y = pg - 1
                        b, page = y // PAGES, y % PAGES
                        pe.wait_ge(s("page_T"), y + 1)
                        if page == 0 and b >= 2:
                            pe.wait_ge(s("scT"), b - 1)
                        if page == 0 and g and b % 4 < 2:
                            pe.wait_ge(s("oa_taken"), 4 * g)
                        for a in range(PAIRS):
                            last = mm(ps[:, 4 + b % 2, 32 * page + 8 * a:32 * page + 8 * a + 8], kpage[:, y % 3, P * a:P * a + P],
                                      qbd[:, a, b, :], True, True)
                        last.then_inc(s("page_sc"), 1)
                pe.wait_ge(s("scT"), 4 * g + 4)
                pe.wait_ge(*after("own_T"))
                for q in range(4):
                    if q >= 2:
                        pe.wait_ge(s("l_taken"), 5 * g + q - 1)
                    for page in range(4 * q, 4 * q + 4):
                        last = turn(ps[:, 6 + q % 2, P * (page % 4):P * (page % 4) + P], scT[:, page, :])
                    last.then_inc(s("l_tr"), 1)
                turn(ps[:, 3, 256:256 + NS], own_T[:, P * g:P * g + P]).then_inc(s("l_tr"), 1)
                pe.wait_ge(s("l_norm"), g + 1)
                for q in range(4):
                    if q >= 2:
                        pe.wait_ge(s("pr_T"), 5 * g + q - 1)
                    for page in range(4 * q, 4 * q + 4):
                        last = turn(ps[:, 6 + q % 2, P * (page % 4):P * (page % 4) + P], logit[:, P * page:P * page + P])
                    last.then_inc(s("pr_tr"), 1)
                turn(ps[0:NS, 3, 384:512], logit[:, PAST:]).then_inc(s("pr_tr"), 1)
                pe.wait_ge(s("pr_T"), 5 * g + 5)
                for j in range(4):
                    b = 4 * g + j
                    if j >= 2:
                        pe.wait_ge(s("oa_taken"), b - 1)
                    ns = [PAGED[("v", b, half)] for half in range(2)]
                    for n in ns:
                        landed(pe, n)
                    for a in range(PAIRS):
                        out = ps[:, 4 + b % 2, 8 * a:8 * a + 8]
                        q = slice(32 * j + 8 * a, 32 * j + 8 * a + 8)
                        for page in range(PAGES):
                            v = slot(ns[page // 8])[:, AW * (page % 8) + P * a:AW * (page % 8) + P * a + P]
                            mm(out, v, prT[:, page, q], page == 0, False)
                        last = mm(out, v_tok[0:NS, PT, P * a:P * a + P], prT[0:NS, PAGES, q], False, True)
                    last.then_inc(s("pv_s"), 1)
            product(0, lambda k: wgk[:, k, :], lambda k: hT[:, k, :], KD, RANK).then_inc(*done("gk_ps"))
            pe.wait_ge(*after("gk_ready"))
            for h in range(GH):
                a_blk, b_blk = GLA[h]
                if h:
                    pe.wait_ge(s("og_T"), 5 * h)
                for i, (t0, T) in enumerate(TILES):
                    out = ps[0:T, i // 4, P * (i % 4):P * (i % 4) + P]
                    last = mm(out, gkT[:, t0:t0 + T], gk2[:, P * h:P * h + P], True, True)
                last.then_inc(s("la_ps"), 1)
                landed(pe, a_blk)
                wq = grid(slot(a_blk)[:, 0:KD * P], KD)
                wk = grid(slot(a_blk)[:, KD * P:2 * KD * P], KD)
                wv = grid(slot(a_blk)[:, 2 * KD * P:], KD)
                if h:
                    pe.wait_ge(s("state_s_new"), DEC_B * h)
                product(2, lambda k: wq[:, k, :], lambda k: hT[:, k, :], KD)
                product(3, lambda k: wk[:, k, :], lambda k: hT[:, k, :], KD).then_inc(s("qk_ps"), 1)
                pe.wait_ge(s("la_ready"), h + 1)
                for i in range(PT):
                    mm(ps[:, 2, P * i:P * i + P], la[:, P * i:P * i + P], const("chunk_causal"), True, True)
                mm(ps[:, 3, 0:NS], la[0:NS, 4 * P:5 * P], const("seq_causal"), True, True).then_inc(s("cum_ps"), 1)
                for i, (t0, T) in enumerate(TILES):
                    if i == 4:
                        pe.wait_ge(s("end_ready"), h + 1)
                        pe.wait_ge(s("e_ready"), h + 1)
                    for k in range(KD):
                        last = mm(ps[0:T, i // 2, GDV * (i % 2):GDV * (i % 2) + GDV], hT[:, k, t0:t0 + T], wv[:, k, :], k == 0, k == KD - 1)
                    if i % 2 or i == PT:
                        last.then_inc(s("v_ps"), 1)
                landed(pe, b_blk)
                wo = grid(slot(b_blk)[:, 0:KD * GDV], KD)
                pe.wait_ge(s("qkt_ready"), h + 1)
                for i, (t0, T) in enumerate(TILES):
                    for k in range(KD):
                        last = mm(ps[0:T, 4 + i // 2, GDV * (i % 2):GDV * (i % 2) + GDV], hT[:, k, t0:t0 + T], wo[:, k, :], k == 0, k == KD - 1)
                    if i % 2 or i == PT:
                        last.then_inc(s("og_ps"), 1)
                for i in range(PT):
                    turn(ps[:, 3, P * i:P * i + P], e_end[:, P * i:P * i + P])
                turn(ps[0:NS, 7, 0:P], e_end[:, sample]).then_inc(s("kend_tr"), 1)
                pe.wait_ge(s("kend_ready"), h + 1)
                pe.wait_ge(s("vg_ready"), 5 * h + 5)
                pe.wait_ge(s("og_raw"), 5 * h + 5)
                if h == 0:
                    pe.wait_ge(*after("att_set"))

                def turned(i, T):
                    n = 5 * h + i
                    pe.wait_ge(s("on_ready"), n + 1)
                    if n:
                        pe.wait_ge(s("og_T"), n)
                    for a in range(2):
                        last = turn(ps[:, 3, T * a:T * a + T], on_[0:T, n % 2, P * a:P * a + P])
                    last.then_inc(s("on_tr"), 1)

                for i in range(PT):
                    t0 = P * i
                    mm(ps[:, 2, P * (i % 2):P * (i % 2) + P], e_neg[:, t0:t0 + P], e_cum[:, t0:t0 + P], True, True).then_inc(s("att_ps"), 1)
                    for c in range(CPT):
                        n = NCH * h + CPT * i + c
                        if n >= 4:
                            pe.wait_ge(s("state_new"), n - 3)
                        r = slice(CHUNK * c, CHUNK * c + CHUNK)
                        mm(ps[:, 4 + c, 0:GDV], kend[r, i, :], v_g[r, i, :], True, True).then_inc(s("u_ps"), 1)
                    pe.wait_ge(s("att_ready"), 5 * h + i + 1)
                    if i >= 2:
                        pe.wait_ge(s("on_ready"), 5 * h + i - 1)
                    last = mm(ps[:, i % 2, 0:GDV], att[:, i % 2, :], v_g[:, i, :], True, False, skip_group_check=True)
                    for c in range(CPT):
                        n = CPT * i + c
                        if n == 0:
                            continue
                        pe.wait_ge(s("state_new"), NCH * h + n)
                        r = slice(CHUNK * c, CHUNK * c + CHUNK)
                        last = mm(ps[r, i % 2, 0:GDV], e_cum[:, t0 + CHUNK * c:t0 + CHUNK * c + CHUNK], state[:, n % 2, :], False, c == CPT - 1,
                                  skip_group_check=True)
                        last.then_inc(s("inter"), 1)
                    if i:
                        turned(i - 1, P)
                mm(ps[0:NS, 2, 0:NS], e_neg[:, sample], e_cum[:, sample], True, True).then_inc(s("att_ps"), 1)
                turned(3, P)
                pe.wait_ge(s("att_ready"), 5 * h + 5)
                pe.wait_ge(s("q_mask"), h + 1)
                pe.wait_ge(s("state_s_in"), 16 * h + 16)
                mm(ps[0:NS, 0, 0:GDV], cmp8[0:NS, 0, 0:NS], v_g[0:NS, 4, :], True, False)
                for b in range(DEC_B):
                    last = mm(ps[0:NS, 0, 0:GDV], q_mask[:, NS * b:NS * b + NS], state_s[:, b, :], False, b == DEC_B - 1)
                last.then_inc(s("o_ps"), 1)
                pe.wait_ge(s("kend_m"), h + 1)
                pe.wait_ge(s("state_new"), NCH * h + NCH)
                for b in range(DEC_B):
                    if b >= 4:
                        pe.wait_ge(s("state_s_new"), DEC_B * h + b - 3)
                    mm(ps[:, 4 + b % 4, 0:GDV], kend_m[:, b, :], v_g[0:NS, 4, :], True, True).then_inc(s("us_ps"), 1)
                turned(4, NS)
            pe.wait_ge(s("og_T"), 5 * GH)
            pe.wait_ge(s("state_s_new"), DEC_B * GH)
            for t in range(KD):
                n = MERGE[t]
                landed(pe, n)
                wga, wgb, wb = (grid(slot(n)[:, KD * P * a:KD * P * a + KD * P], KD) for a in range(3))
                wa = grid(slot(n)[:, 3 * KD * P:3 * KD * P + AW], AW // P)
                if t:
                    pe.wait_ge(s("ga_sig"), t)
                product(0, lambda k: wga[:, k, :], lambda k: hT[:, k, :], KD).then_inc(s("ga_ps"), 1)
                if t:
                    pe.wait_ge(s("gb_sig"), t)
                product(1, lambda k: wgb[:, k, :], lambda k: hT[:, k, :], KD).then_inc(s("gb_ps"), 1)
                if t:
                    pe.wait_ge(s("m_half"), t)
                product(2, lambda k: wa[:, k, :], lambda k: o_aT[:, k, :], AW // P).then_inc(s("pa_ps"), 1)
                if t:
                    pe.wait_ge(s("m_ready"), t)
                product(3, lambda k: wb[:, k, :], lambda k: o_gT[:, k, :], KD).then_inc(s("pb_ps"), 1)
            pe.wait_ge(s("merged"), KD)
            for t in range(KD):
                n = OUT[t // 4]
                landed(pe, n)
                w = grid(slot(n), KD)
                if t >= 3:
                    pe.wait_ge(s("x1T"), t - 2)
                product(t % 3, lambda k: w[:, k, P * (t % 4):P * (t % 4) + P], lambda k: mergedT[:, k, :], KD).then_inc(s("out_ps"), 1)
            for k in range(KD):
                pe.wait_ge(s("sq_ready"), KD + k + 1)
                for half in range(2):
                    last = mm(ps[:, 6 + half, 0:HALF], ones, sq2[:, k % 2, HALF * half:HALF * half + HALF], k == 0, k == KD - 1)
                last.then_inc(s("sq_used"), 1)
            for i, (t0, T) in enumerate(TILES):
                if i:
                    pe.wait_ge(s("x1_tok"), i)
                for k in range(KD):
                    last = turn(ps[0:T, 2 + k // 4, P * (k % 4):P * (k % 4) + P], xT[:, k, t0:t0 + T])
                last.then_inc(s("x1_tr"), 1)
            pe.wait_ge(s("h2_ready"), KD)
            for i, (t0, T) in enumerate(TILES):
                if i:
                    pe.wait_ge(s("h2_tok"), i)
                for k in range(KD):
                    last = turn(ps[0:T, k // 4, P * (k % 4):P * (k % 4) + P], hT[:, k, t0:t0 + T])
                last.then_inc(s("h2_tr"), 1)
            pe.wait_ge(s("router_in"), 64)
            for i, (t0, T) in enumerate(TILES):
                out = ps[0:T, 6, 36 * i:36 * i + 36]
                for k in range(KD):
                    mm(out, hT[:, k, t0:t0 + T], wr[:, k, :], k == 0, False)
                last = mm(out, ones[0:1, 0:T], brow[:, :], False, True)
            last.then_inc(*done("lg_ps"))
            pe.wait_ge(*after("chosen"))
            for i in range(6):
                out = ps[:, 7, NE * i:NE * i + NE]
                top = min(i, 4)
                for j in range(top + 1):
                    last = mm(out, const("before") if j == i else ones, both[:, j, :], j == 0, j == top)
            last.then_inc(*done("pos_ps"))
            pe.wait_ge(*after("g_exp2"))
            for t in range(KD):
                turn(ps[:, 4 + t // 4, P * (t % 4):P * (t % 4) + P], g_exp[:, t, 0:P])
            pe.wait_ge(*after("more_ready"))
            for t in range(KD):
                last = turn(ps[0:NS, 6 + t // 4, P * (t % 4):P * (t % 4) + P], g_exp[:, t, P:])
            last.then_inc(*done("g_tr"))
            pe.wait_ge(*after("g_rows"))
            pe.wait_ge(s("h2_tok"), 5)
            pe.wait_ge(s("x1_tok"), 5)

            def step(e, it, par, before):
                pe.wait_ge(s(f"xs_in{par}"), it * 16 + 16)
                rows = xs[par].rearrange("r (p k) -> r k p", k=KD)
                mm(ps[:, par, 0:CAP], rows[:, 0, :], ident[0:CAP, 0:CAP], True, True)
                for j in range(1, KD):
                    last = turn(ps[:, par, CAP * j:CAP * j + CAP], rows[:, j, :])
                last.then_inc(s("xs_tr"), 1)
                if before:
                    down(e - 1, before[0], 1 - par)
                pe.wait_ge(s("xsT"), e + 1)
                for m in range(2):
                    q = (N0 + 3 * par + m) % RING
                    pe.wait_ge(slot_sem[q], it * 16 + (EXP_COUNT[q] + 16))
                    w = ring[:, q, :].rearrange("p (k c j) -> p k j c", k=KD, j=4)
                    for f in range(4):
                        for k in range(KD):
                            last = mm(ps[:, 2 + par, 256 * m + CAP * f:256 * m + CAP * f + CAP], w[:, k, f, :], xsT[par][:, CAP * k:CAP * k + CAP],
                                      k == 0, k == KD - 1)
                    last.then_inc(w_used, 1)

            def down(e, it, par):
                q = (N0 + 3 * par + 2) % RING
                pe.wait_ge(slot_sem[q], it * 16 + (EXP_COUNT[q] + 16))
                pe.wait_ge(s("hid"), e + 1)
                w = grid(ring[:, q, :], 4)
                for half in range(2):
                    for f in range(4):
                        last = mm(ps[0:CAP, 4 + 2 * par + half, :], hid[par][:, CAP * f:CAP * f + CAP], w[:, f, 512 * half:512 * half + 512],
                                  f == 0, f == 3)
                last.then_inc(w_used, 1)

            step(0, 0, 0, None)
            with pe.Fori(0, NE // 2 - 1) as i:
                step(2 * i + 1, i, 1, (i,))
                step(2 * i + 2, i + 1, 0, (i,))
            step(NE - 1, NE // 2 - 1, 1, (NE // 2 - 1,))
            down(NE - 1, NE // 2 - 1, 1)

            def more(c):
                step(c + NE, c + NE // 2, 0, None)
                down(c + NE, c + NE // 2, 0)

            further_blocks(pe, more)


_INS = ['x_prompt', 'x_sample', 'c_prompt', 'c_sample', 'cache_k', 'cache_v', 'state_gla', 'page_table',
        'rel_bias', 'norm1_g', 'norm2_g', 'w_ada', 'b_ada', 'w_in', 'w_gk2', 'b_gk', 'q_norm_g', 'k_norm_g', 'o_norm_g',
        'w_branch_a', 'w_branch_b', 'w_out', 'w_router_group', 'b_router_group', 'w_router_expert',
        'b_router_expert', 'w_exp_gate', 'w_exp_up', 'w_exp_down']
_OUTS = [(1, SEQ, D), (DEC_B, DEC_T, D), (1, 1, SEQ, AH, AD), (1, 1, SEQ, AH, AD), (1, 1, GH, GDK, GDV),
         (1, DEC_B, DEC_T, AH, AD), (1, DEC_B, DEC_T, AH, AD), (1, DEC_B, GH, GDK, GDV)]


def kernel(**inputs):
    import concourse.bacc as bacc
    from concourse.bass_utils import run_bass_kernel_spmd

    nc = bacc.Bacc("TRN2", target_bir_lowering=False, num_devices=1)
    arrays, args = {}, []
    for name in _INS + ["shape_table"]:
        a = np.ascontiguousarray(CONST_TABLE if name == "shape_table" else inputs[name])
        arrays["in_" + name] = a
        args.append(nc.dram_tensor("in_" + name, a.shape, mybir.dt.from_np(a.dtype), kind="ExternalInput").ap())
    for i, shape in enumerate(_OUTS):
        args.append(nc.dram_tensor(f"out_{i}", shape, F32, kind="ExternalOutput").ap())
    layer_kernel(nc, *args)
    r = run_bass_kernel_spmd(nc, [arrays], core_ids=[0])
    return tuple(r.results[0][f"out_{i}"] for i in range(len(_OUTS)))
```

```python
from contextlib import ExitStack

import numpy as np
import concourse.bass as bass
from concourse import mybir

ALU = mybir.AluOpType
ACT = mybir.ActivationFunctionType
F32 = mybir.dt.float32
I32 = mybir.dt.int32
U32 = mybir.dt.uint32
AX = mybir.AxisListType

P = 128
D = 1024
KD = D // P
SEQ, DEC_B, DEC_T = 512, 8, 4
NS = DEC_B * DEC_T
NT = SEQ + NS
PT = SEQ // P
TILES = [(t * P, P) for t in range(PT)] + [(SEQ, NS)]
HALF = NT // 2
PAST, PAGE = 2048, 128
PAGES = PAST // PAGE
AH, AD = 8, 64
AW = AH * AD
PAIRS = AH // 2
BLK = 256
NBLK = PAST // BLK
TOPK = 3
BUCKETS, MAXDIST = 32, 128
GH, GDK, GDV = 4, 128, 256
RANK = 16
GNORM = 16.0
CHUNK = 32
NCH = SEQ // CHUNK
CPT = P // CHUNK
NG, EPG, NE, HID = 4, 8, 32, 512
CAP = 64
MORE = 2 * NT // CAP - 1
EB = NE + MORE
EDGES = -(-NT // CAP) - 1
EPS = 1e-6
NEG = -1e30
OFF = dict(qa=0, ka=AW, va=2 * AW, qg=3 * AW, kg=3 * AW + 512, vg=3 * AW + 1024, og=3 * AW + 2048,
           gk=3 * AW + 3072, ga=3 * AW + 3088, gb=3 * AW + 4112)
IN_W = 3 * AW + 5136
RING = 6
UNIT = KD * 512
TAB = 384
WORK = 16550
RBM = 255


def shape_constants():
    c = {}
    i = np.arange(P)
    c["ident"] = np.eye(P)
    c["ones"] = np.ones((P, P))
    c["before"] = (i[:, None] < i[None, :])
    c["chunk_causal"] = (i[:, None] <= i[None, :]) & (i[:, None] // CHUNK == i[None, :] // CHUNK)
    s = i[:NS]
    c["seq_causal"] = (s[:, None] <= s[None, :]) & (s[:, None] // DEC_T == s[None, :] // DEC_T)
    c["seq_member"] = (s[:, None] // DEC_T == np.arange(DEC_B)[None, :])
    dist = RBM - np.arange(TAB)
    n = np.maximum(dist, 0)
    exact = BUCKETS // 2
    nf = np.maximum(n, 1).astype(np.float32)
    large = exact + (np.log(nf / np.float32(exact)) / np.float32(np.log(MAXDIST / exact))
                     * np.float32(BUCKETS - exact)).astype(np.int32)
    bucket = np.where(n < exact, n, np.minimum(large, BUCKETS - 1))
    hot = np.zeros((BUCKETS + 1, TAB))
    hot[bucket, np.arange(TAB)] = 1
    hot[:, dist < 0] = 0
    hot[BUCKETS, dist < 0] = 1
    c["lower_index"] = np.broadcast_to((np.arange(8)[None, :] < np.arange(8)[:, None]).reshape(1, 64), (P, 64))
    c["lower_index4"] = np.broadcast_to((np.arange(4)[None, :] < np.arange(4)[:, None]).reshape(1, 16), (P, 16))
    tok = i[:, None] + P * np.arange(PT + 1)[None, :]
    c["token_real"] = tok < NT
    c["token_id"] = np.minimum(tok, NT - 1)
    c["expert_id"] = np.broadcast_to(np.arange(NE)[None, :], (P, NE))
    c["block_edge"] = np.broadcast_to(CAP * (1 + np.arange(EDGES))[None, :], (P, EDGES))
    c["more_id"] = np.broadcast_to(np.arange(MORE)[None, :], (P, MORE))
    c["row_head"] = i[:, None] % 32 // DEC_T == np.arange(AH)[None, :]
    c["row_token"] = (i[:, None] // 32 == np.arange(16)[None, :] // DEC_T) & (i[:, None] % DEC_T == np.arange(16)[None, :] % DEC_T)
    c["minus_half"] = np.full((P, 8), -0.5)
    c["bucket_hot"] = hot
    at, cols = {}, 0
    for k, v in c.items():
        at[k] = (cols, v.shape[0], v.shape[1])
        cols += v.shape[1]
    table = np.zeros((P, cols), np.float32)
    for k, v in c.items():
        o, r, w = at[k]
        table[:r, o:o + w] = v
    return table, at


CONST_TABLE, CONST_AT = shape_constants()


def layer_kernel(nc, x_prompt, x_sample, c_prompt, c_sample, cache_k, cache_v, state_gla, page_table,
                 rel_bias, norm1_g, norm2_g, w_ada, b_ada, w_in, w_gk2, b_gk, q_norm_g, k_norm_g, o_norm_g,
                 w_branch_a, w_branch_b, w_out, w_router_group, b_router_group, w_router_expert,
                 b_router_expert, w_exp_gate, w_exp_up, w_exp_down, shape_table,
                 y_prompt, y_sample, k_prompt, v_prompt, state_prompt, k_sample, v_sample, state_sample):
    with ExitStack() as ctx:
        def sb(name, shape, dt=F32):
            return ctx.enter_context(nc.sbuf_tensor(name, shape, dt))

        def sem(name):
            return ctx.enter_context(nc.semaphore(name))

        bias_dram = nc.dram_tensor("bias_rows", [AH, P, TAB], F32, kind="Internal").ap()
        h2_dram = nc.dram_tensor("h2_rows", [NT, D], F32, kind="Internal").ap()
        slot_dram = nc.dram_tensor("slot_tokens", [CAP * EB, 1], I32, kind="Internal").ap()
        y_dram = nc.dram_tensor("expert_rows", [CAP * EB, D], F32, kind="Internal").ap()

        KEPT = CONST_AT["bucket_hot"][0]
        cst = sb("cst", [P, KEPT])

        def const(name):
            o, r, w = CONST_AT[name]
            return cst[0:r, o:o + w]

        ident, ones = const("ident"), const("ones")
        ring = sb("ring", [P, RING, UNIT])
        xT = sb("xT", [P, KD, NT])
        hT = sb("hT", [P, KD, NT])
        work = sb("work", [P, WORK])
        cT = sb("cT", [P, KD, DEC_B + 1])
        vT = sb("vT", [P, 64])
        mod = sb("mod", [P, 6, KD, DEC_B + 1])
        gain = sb("gain", [P, 2, KD, DEC_B + 1])
        wgk = sb("wgk", [P, KD, RANK])
        gk2 = sb("gk2", [RANK + 1, 512])
        qkg = sb("qkg", [P, 2, AD])
        ong = sb("ong", [P, GDV])
        rbx = sb("rbx", [BUCKETS + 1, AH])
        rbfar = sb("rbfar", [P, AH])
        st = sb("stats", [P, 256])
        far_s = sb("far_s", [P, 1])
        ps = ctx.enter_context(nc.psum_tensor("ps", [P, 8, 512], F32))

        def carve(base, *sizes):
            out = []
            for n in sizes:
                out.append(work[:, base:base + n])
                base += n
            assert base <= WORK, base
            return out

        def grid(v, n):
            return v.rearrange("p (a b) -> p a b", a=n)

        o_aT = grid(work[:, 0:PAIRS * NT], PAIRS)
        o_gT = grid(work[:, 2176:2176 + KD * NT], KD)

        def wide(w, rows=P):
            return ps[0:rows, 2 * w:2 * w + 2, 0:HALF]

        def halves(v):
            return v.rearrange("p (a c) -> p a c", a=2)

        S = {}

        def s(name):
            if name not in S:
                S[name] = sem(name)
            return S[name]

        slot_sem = [sem(f"slot{i}_landed") for i in range(RING)]
        page_sem = [sem(f"pages{i}_landed") for i in range(RING)]
        w_used = sem("w_used")
        slot_count = [0] * RING
        stream = []

        def add_block(pieces, dmas, used):
            n = len(stream)
            slot_count[n % RING] += 16 * dmas
            stream.append((slot_count[n % RING], pieces, used))
            return n

        def slot(n):
            return ring[:, n % RING, :]

        def columns(w, lo, n, cols, at=0, k=KD):
            dst = slot(n)[:, at:at + k * cols].rearrange("p (k c) -> p k c", k=k)
            return dst, w.rearrange("(k p) c -> p k c", p=P)[:, :, lo:lo + cols]

        def block(used, *parts):
            n = len(stream)
            return add_block([columns(w, lo, n, cols, at, k) for w, lo, cols, at, k in parts], len(parts), used)

        ADA = [block((w_used, i + 1), (w_ada[0], 512 * i, 512, 0, KD)) for i in range(12)]
        QKV = [block((s("pj"), 5 * i + 5), (w_in[0], OFF[c], 512, 0, KD)) for i, c in enumerate(("qa", "ka", "va"))]
        PAGED = {}
        for what in ("k", "v"):
            for i in range(DEC_B * PAGES // 8):
                used = (s("page_tr"), 8 * i + 8) if what == "k" else (s("pv_s"), i + 1)
                PAGED[(what, i)] = add_block((what, i), PAGES // 4, used)
        GLA = []
        for h in range(GH):
            a = block((s("v_ps"), 3 * h + 3), (w_in[0], OFF["qg"] + GDK * h, GDK, 0, KD), (w_in[0], OFF["kg"] + GDK * h, GDK, KD * GDK, KD),
                      (w_in[0], OFF["vg"] + GDV * h, GDV, 2 * KD * GDK, KD))
            b = block((s("og_ps"), 3 * h + 3), (w_in[0], OFF["og"] + GDV * h, GDV, 0, KD))
            GLA.append((a, b))
        MERGE = [block((s("pb_ps"), t + 1), (w_in[0], OFF["ga"] + P * t, P, 0, KD), (w_in[0], OFF["gb"] + P * t, P, KD * P, KD),
                       (w_branch_b[0], P * t, P, 2 * KD * P, KD), (w_branch_a[0], P * t, P, 3 * KD * P, AW // P))
                 for t in range(KD)]
        OUT = [block((s("out_ps"), 4 * i + 4), (w_out[0], 512 * i, 512, 0, KD)) for i in range(2)]
        N0 = len(stream)
        EXP_USED = len(ADA)
        EXP_COUNT = [slot_count[i] for i in range(RING)]

        def landed(pe, n):
            pe.wait_ge(slot_sem[n % RING], stream[n][0])
            if isinstance(stream[n][1], tuple):
                paged = [m for m in PAGED.values() if m % RING == n % RING and m <= n]
                pe.wait_ge(page_sem[n % RING], 16 * PAGES // 4 * len(paged))

        ONCE = {
            "pe": ["c_tr", "own_ps", "gk_ps", "lg_ps", "pos_ps", "g_tr"],
            "dve": ["rbx_set", "sample_set", "rbw_ready", "cT", "var_ready", "h_sample", "q_row", "att_set", "gk_ones",
                    "var2_ready", "h2_sample", "g_exp2", "lg_max", "e_gap", "chosen", "dest_ready", "more_ready"],
            "act": ["c_silu", "rstd_ready", "gk_ready", "rstd2_ready", "lg_exp", "e_gap_exp", "g_rows", "rows_out"],
            "pool": ["zero_set", "zero_rows"],
        }
        once_sem = {e: sem(e + "_steps") for e in ONCE}

        def done(name):
            return next(once_sem[e] for e in ONCE if name in ONCE[e]), 1

        def after(name):
            return next((once_sem[e], ONCE[e].index(name) + 1) for e in ONCE if name in ONCE[e])

        KEY_PAGES = DEC_B * PAGES
        QUADS = KEY_PAGES // 4
        EXP_AT, WEIGHTS_AT = 22, 24

        class Chain:

            def __init__(self, name):
                self.sem, self.n = sem(name), 0

            def __call__(self, eng, ins):
                ins.then_inc(self.sem, 1)
                self.n += 1
                eng.wait_ge(self.sem, self.n)

        dve_chain, act_chain, pool_chain = Chain("dve_own"), Chain("act_own"), Chain("pool_own")

        x_tok, sq, var, rstd, bias_stage, rbw, crow, vrow, zero_i, hot, mod_rows = carve(
            2176, 5 * D, 2 * NT, NT, NT, 2 * TAB, AH * P, 2 * D, P, CAP * EB // P, TAB, 2 * 512)
        crow, vrow, zero_i, hot = grid(crow[0:DEC_B + 1], 2), vrow[0:64, :], zero_i.bitcast(I32), hot[0:BUCKETS + 1, :]
        near_s, own_s, ptab = carve(16000, PAGE + DEC_T, 2 * NS, DEC_B * PAGES)
        own_s, ptab = grid(own_s, 2), ptab[0:1, :].bitcast(I32)
        x_tok, mod_rows = grid(x_tok, 5), grid(mod_rows[0:DEC_B + 1], 2)
        sq = grid(sq, 2)
        bias_stage = grid(bias_stage, 2)
        rbw = rbw[0:BUCKETS + 1, :]

        qT, kT, v_tok, near, sc_p, pt_p, tok, tok_sq = carve(
            2176, PAIRS * NT, PAIRS * NT, 5 * AW, AH * 2 * P, 3 * 512, 2 * 512, 2 * AW, AW)
        qT, kT, v_tok = grid(qT, PAIRS), grid(kT, PAIRS), grid(v_tok, 5)
        near, sc_p, pt_p, tok = grid(near, AH), grid(sc_p, 3), grid(pt_p, 2), grid(tok, 2)
        after_v = 2176 + 2 * PAIRS * NT + 5 * AW
        kpage, = carve(2176, 8 * AW)
        q_row, = carve(2176 + 2 * PAIRS * NT, PAIRS * DEC_B * 32)
        prT, logit0, logit1 = carve(after_v, (PAGES + 1) * P, PAST + NS, PAST + NS)
        o_rows = grid(kpage[:, 0:2 * AW], 2)
        prT, logits, kpage = grid(prT, PAGES + 1), [logit0, logit1], grid(kpage, 8)
        q_row = q_row.rearrange("p (a b c) -> p a b c", a=PAIRS, b=DEC_B)
        cmp8 = sb("cmp8", [P, 2, 5 * NE])
        junk = cmp8[:, :, :].rearrange("p a b -> p (a b)")[:, 64:64 + GDV]

        (e_cum, e_neg, e_end, v_g, og, la, kend, state, att, state_s, q_mask, on_, gkT) = carve(
            2176 + KD * NT, NT, NT, NT, 5 * GDV, 5 * GDV, 8 * P, 5 * P, 2 * GDV, 2 * P, DEC_B * GDV, 288, 2 * GDV, NT)
        v_g, og, kend, state, att = grid(v_g, 5), grid(og, 5), grid(kend, 5), grid(state, 2), grid(att, 2)
        state_s, on_ = grid(state_s, DEC_B), grid(on_, 2)
        kend_m = grid(la, DEC_B)[0:NS]
        gkT = gkT[0:RANK + 1, :]

        mergedT, m_a, m_b = carve(2176 + KD * NT, KD * NT, 2 * NT, 2 * NT)
        mergedT, m_a, m_b = grid(mergedT, KD), grid(m_a, 2), grid(m_b, 2)
        sq2, var2, rstd2, tmp2 = carve(2176, 2 * NT, NT, NT, NT)
        sq2 = grid(sq2, 2)

        h2_tok, x1_tok, g2p, g2s, g_exp = carve(0, 5 * D, 5 * D, D, D, KD * (P + NS))
        wr, brow, lg, one1, one2, both = carve(13600, KD * (NG + NE), NG + NE, 5 * (NG + NE), 5 * NE, 5 * NE, 5 * NE)
        wr, brow, lg = grid(wr, KD), brow[0:1, :], grid(lg, 5)
        one1, one2, both = grid(one1, 5), grid(one2, 5), grid(both, 5)
        h2_tok, x1_tok, g_exp = grid(h2_tok, 5), grid(x1_tok, 5), grid(g_exp, KD)
        g2s = g2s[0:NS, :]
        ya = grid(h2_tok.rearrange("p a b -> p (a b)")[:, 0:2 * D], 2)
        yb = grid(h2_tok.rearrange("p a b -> p (a b)")[:, 2 * D:4 * D], 2)
        hflat = hT[:, :, :].rearrange("p a b -> p (a b)")
        xflat = xT[:, :, :].rearrange("p a b -> p (a b)")
        xs = [hflat[0:CAP, D * i:D * i + D] for i in range(2)]
        xsT = [hflat[:, 2 * D + 512 * i:2 * D + 512 * i + 512] for i in range(2)]
        hid = [hflat[:, 3 * D + 256 * (i + 1):3 * D + 256 * (i + 2)] for i in range(2)]
        ye = [xflat[:, 512 * i:512 * i + 512] for i in range(2)]

        blk_cmp, zero_rows = carve(14600, NE * MORE, D)
        zero_rows = zero_rows[0:CAP, :]
        wts = sb("wts", [P, 2, 5])
        dest = sb("dest", [P, 2, 5])
        dest_i = sb("dest_i", [P, 2, 5], I32)
        row_i = sb("row_i", [P, 2, 5], I32)
        tok_i = sb("tok_i", [P, 5], I32)
        cnt = sb("cnt", [P, NE])
        base = sb("base", [P, NE])
        more_i = sb("more_i", [1, MORE + 1], I32)
        idx = sb("idx", [CAP, EB], I32)

        idx_cur = sb("idx_cur", [CAP, 1], I32)

        def bc(v, shape):
            return v.broadcast_to(shape)

        def further_blocks(eng, body):
            eng.wait_ge(*after("more_ready"))
            count = eng.value_load(more_i[0:1, MORE:MORE + 1], min_val=0, max_val=MORE)
            with eng.If(count > 0):
                with eng.Fori(0, MORE) as c:
                    with eng.If(count > c):
                        body(c)
            return count

        sample = slice(SEQ, NT)
        own_lower8, own_lower4 = const("lower_index"), const("lower_index4")
        blk = ctx.enter_context(nc.Block())

        def load_pages(eng, n, pieces, which, sems):
            what, i = pieces
            cache = cache_k if what == "k" else cache_v
            for q in which:
                pg = 8 * i + q
                at = (4 * (pg // (4 * PAGES)) + pg % 4) * PAGES + pg // 4 % PAGES
                page = eng.value_load(ptab[0:1, at:at + 1], min_val=0, max_val=cache.shape[1] - 1)
                src = cache[0, bass.DynSlice(page, 1)].rearrange("a t h d -> (a t) (h d)")
                eng.dma_start(slot(n)[:, AW * q:AW * q + AW], src).then_inc(sems[n % RING], 16)

        @blk.sync
        def _(sp):
            for n, (_, pieces, _) in enumerate(stream):
                if n >= RING:
                    sp.wait_ge(*stream[n - RING][2])
                if isinstance(pieces, tuple):
                    sp.wait_ge(s("page_table_in"), 16)
                    load_pages(sp, n, pieces, range(0, 8, 2), slot_sem)
                else:
                    for dst, src in pieces:
                        sp.dma_start(dst, src).then_inc(slot_sem[n % RING], 16)

            def expert_blocks(e, par, before, expert=None):
                for m, w in enumerate((w_exp_gate, w_exp_up, w_exp_down)):
                    at = 3 * par + m
                    sp.wait_ge(*(stream[N0 + at - RING][2] if before is None else (w_used, before * 3 + (EXP_USED + m + 1))))
                    src = w[0, bass.DynSlice(e if expert is None else expert, 1)].rearrange("a (p k) c -> p (a k c)", k=w.shape[2] // P)
                    sp.dma_start(slot(N0 + at), src).then_inc(slot_sem[(N0 + at) % RING], 16)

            for par in range(2):
                expert_blocks(par, par, None)
            with sp.Fori(1, NE // 2) as i:
                for par in range(2):
                    expert_blocks(2 * i + par, par, 2 * i + (par - 2))

            def more(c):
                expert = sp.value_load(more_i[0:1, bass.DynSlice(c, 1)], min_val=0, max_val=NE - 1)
                expert_blocks(c + NE, 0, c + (NE - 1), expert)

            further_blocks(sp, more)

        @blk.gpsimd
        def _(pool):
            minus_half = const("minus_half")
            pool.memset(zero_i, 0).then_inc(*done("zero_set"))
            pool.wait_ge(*after("zero_set"))
            pool.dma_start(slot_dram.rearrange("(p n) a -> p (n a)", p=P), zero_i).then_inc(s("slots_cleared"), 16)
            for h in range(AH):
                pool.wait_ge(s("bias_copied"), h + 1)
                pool.dma_start(bias_dram[h], bias_stage[:, h % 2, :]).then_inc(s(f"bias_out{h % 2}"), 16)
            for a in range(2):
                pool.wait_ge(s(f"bias_out{a}"), 16 * AH // 2)
            for j in range(4):
                src = bass.AP(tensor=bias_dram.tensor, offset=P - 1, ap=[[P * TAB, AH], [TAB - 1, DEC_T], [1, PAGE + DEC_T]])
                pool.dma_start(near_s[32 * j:32 * j + 32, :], src).then_inc(s("near_s_in"), 16)
                src = bass.AP(tensor=bias_dram.tensor, offset=0, ap=[[P * TAB, AH], [TAB, DEC_T], [1, 1]])
                pool.dma_start(far_s[32 * j:32 * j + 32, :], src, allow_slow_non_contiguous=True).then_inc(s("near_s_in"), 16)
            pool.wait_ge(s("const_in"), 16)
            pool.wait_ge(s("h_ready"), KD)
            src = bass.AP(tensor=bias_dram.tensor, offset=P - 1, ap=[[TAB - 1, P], [P * TAB, AH], [1, 2 * P]])
            pool.dma_start(near, src).then_inc(s("near_in"), 16)
            for m in range(11):
                if m < 10:
                    pool.wait_ge(s("qk_var"), m + 1)
                    T = TILES[m % 5][1]
                    v8 = st[0:T, 16 * (m % 2):16 * (m % 2) + 8]
                    pool.tensor_tensor(st[0:T, 16 * (m % 2) + 8:16 * (m % 2) + 16], v8, minus_half[0:T, 0:8],
                                       ALU.pow).then_inc(s("qk_rstd"), 1)
                if m - 1 >= 5:
                    i = m - 6
                    pool.wait_ge(s("qk_tok"), m)
                    dst = (k_prompt[0, 0, P * i:P * i + P] if i < PT else k_sample[0].rearrange("b t h d -> (b t) h d"))
                    T = TILES[i][1]
                    pool.dma_start(dst.rearrange("t h d -> t (h d)"), tok[0:T, (m - 1) % 2, :]).then_inc(s(f"k_out{(m - 1) % 2}"), 16)
            pool.wait_ge(s("v_ready"), 5)
            pool.dma_start(v_prompt[0, 0].rearrange("(i p) h d -> p i (h d)", p=P), v_tok[:, 0:PT, :]).then_inc(s("v_out"), 16)
            pool.dma_start(v_sample[0].rearrange("b t h d -> (b t) (h d)"), v_tok[0:NS, PT, :]).then_inc(s("v_out"), 16)
            pool.wait_ge(s("k_out0"), 16 * 2)
            pool.wait_ge(s("k_out1"), 16 * 3)
            pool.wait_ge(s("v_out"), 32)
            pool.wait_ge(s("page_table_in"), 16)
            for what in ("k", "v"):
                for i in range(KEY_PAGES // 8):
                    n = PAGED[(what, i)]
                    pool.wait_ge(*stream[n - RING][2])
                    load_pages(pool, n, (what, i), range(1, 8, 2), page_sem)
            for h in range(GH):
                if h:
                    pool.wait_ge(s("state_s_out"), 16 * h)
                else:
                    pool.wait_ge(s("oa_taken"), 2)
                pool.dma_start(state_s, state_gla[0, :, h].rearrange("b k v -> k b v")).then_inc(s("state_s_in"), 16)
                for i, (_, T) in enumerate(TILES):
                    n = 5 * h + i
                    pool.wait_ge(s("og_raw"), n + 1)
                    pool.tensor_tensor(og[0:T, i, :], og[0:T, i, :], ong[0:T, :], ALU.mult).then_inc(s("og_ready"), 1)
                for i, (_, T) in enumerate(TILES):
                    n = 5 * h + i
                    pool.wait_ge(s("o_var"), n + 1)
                    c = 64 + 2 * (n % 2)
                    pool.tensor_tensor(st[0:T, c + 1:c + 2], st[0:T, c:c + 1], minus_half[0:T, 0:1], ALU.pow).then_inc(s("o_rstd"), 1)
                    if i == 3:
                        pool.wait_ge(s("state_new"), NCH * (h + 1))
                        pool.dma_start(state_prompt[0, 0, h], state[:, NCH % 2, :]).then_inc(s("state_p_out"), 16)
                pool.wait_ge(s("state_s_new"), DEC_B * (h + 1))
                pool.dma_start(state_sample[0, :, h].rearrange("b k v -> k b v"), state_s).then_inc(s("state_s_out"), 16)
            pool.wait_ge(s("state_s_out"), 16 * GH)
            pool.wait_ge(s("state_p_out"), 16 * GH)
            for t in range(KD):
                pool.wait_ge(s("m_ready"), t + 1)
                pool.tensor_tensor(halves(mergedT[:, t, :]), halves(m_a[:, t % 2, :]), halves(m_b[:, t % 2, :]), ALU.add).then_inc(s("merged"), 1)
            pool.memset(zero_rows, 0.0).then_inc(*done("zero_rows"))
            pool.wait_ge(*after("zero_rows"))
            dst = y_dram.rearrange("(r b) c -> r b c", b=EB)[:, NE:, :]
            pool.dma_start(dst, bc(zero_rows.unsqueeze(1), [CAP, MORE, D])).then_inc(s("y_cleared"), 16)
            pool.dma_start(wr[:, :, 0:NG], w_router_group[0].rearrange("(k p) c -> p k c", p=P)).then_inc(s("router_in"), 16)
            pool.dma_start(wr[:, :, NG:NG + NE], w_router_expert[0].rearrange("(k p) c -> p k c", p=P)).then_inc(s("router_in"), 16)
            pool.dma_start(brow[:, 0:NG], b_router_group).then_inc(s("router_in"), 16)
            pool.dma_start(brow[:, NG:NG + NE], b_router_expert).then_inc(s("router_in"), 16)
            for i, (t0, T) in enumerate(TILES):
                pool.wait_ge(s("h2_tok"), i + 1)
                pool.dma_start(h2_dram[t0:t0 + T, :], h2_tok[0:T, i, :]).then_inc(s("h2_out"), 16)
            pool.wait_ge(s("slots_cleared"), 16)
            pool.wait_ge(*after("dest_ready"))
            for i, (t0, T) in enumerate(TILES):
                for c in range(2):
                    pool.indirect_dma_start(slot_dram[:, :], bass.IndirectOffsetOnAxis(ap=dest_i[0:T, c, i:i + 1], axis=0),
                                            tok_i[0:T, i:i + 1], None).then_inc(s("slots_set"), 16)
            pool.wait_ge(s("slots_set"), 160)
            pool.dma_start(idx[:, :], slot_dram.rearrange("(r b) a -> r (b a)", b=EB)).then_inc(s("idx_in"), 16)
            pool.wait_ge(s("h2_out"), 80)
            pool.wait_ge(s("idx_in"), 16)
            pool.wait_ge(*after("g_tr"))
            for e in range(NE):
                if e >= 2:
                    pool.wait_ge(s("xs_tr"), e - 1)
                pool.indirect_dma_start(xs[e % 2], None, h2_dram[:, :],
                                        bass.IndirectOffsetOnAxis(ap=idx[:, e:e + 1], axis=0)).then_inc(s(f"xs_in{e % 2}"), 16)
            turns = pool.alloc_register("turns")
            pool.reg_mov(turns, 1)

            def more(c):
                pool.wait_ge(s("idx_cur"), turns)
                pool.reg_add(turns, turns, 1)
                pool.wait_ge(s("y_cleared"), 16)
                pool.indirect_dma_start(xs[0], None, h2_dram[:, :],
                                        bass.IndirectOffsetOnAxis(ap=idx_cur[:, 0:1], axis=0)).then_inc(s("xs_in0"), 16)

            further_blocks(pool, more)
            pool.wait_ge(s("y_cleared"), 16)
            pool.wait_ge(*after("rows_out"))
            for i, (_, T) in enumerate(TILES):
                if i >= 2:
                    pool.wait_ge(s(f"y_out{i % 2}"), 16 * (i // 2))
                for c, v in ((0, ya), (1, yb)):
                    pool.indirect_dma_start(v[0:T, i % 2, :], None, y_dram[:, :],
                                            bass.IndirectOffsetOnAxis(ap=dest_i[0:T, c, i:i + 1], axis=0)).then_inc(s(f"ya_in{i % 2}"), 16)

        @blk.scalar
        def _(act):
            act.dma_start(cst[:, :], shape_table[:, 0:KEPT]).then_inc(s("const_in"), 16)
            act.dma_start(hot, shape_table[0:BUCKETS + 1, KEPT:]).then_inc(s("small_in"), 16)
            act.dma_start(crow[0:1, 0, :], c_prompt).then_inc(s("c_in"), 16)
            act.dma_start(crow[1:DEC_B + 1, 0, :], c_sample).then_inc(s("c_in"), 16)
            act.dma_start(vrow[0:48, :], b_ada[0].rearrange("(a p) -> a p", p=P)).then_inc(s("vec_in"), 16)
            act.dma_start(vrow[48:56, :], norm1_g[0].rearrange("(a p) -> a p", p=P)).then_inc(s("vec_in"), 16)
            act.dma_start(vrow[56:64, :], norm2_g[0].rearrange("(a p) -> a p", p=P)).then_inc(s("vec_in"), 16)
            act.dma_start(x_tok[:, 0:PT, :], x_prompt[0].rearrange("(i p) d -> p i d", p=P)).then_inc(s("x_in"), 16)
            act.dma_start(x_tok[0:NS, PT, :], x_sample.rearrange("b t d -> (b t) d")).then_inc(s("x_in"), 16)
            act.wait_ge(*after("rbx_set"))
            act.dma_start(rbx[0:BUCKETS, :], rel_bias).then_inc(s("small_in"), 16)
            act.dma_start(ptab[:, :], page_table.rearrange("(a b) n -> a (b n)", a=1)).then_inc(s("page_table_in"), 16)

            def rows(v, n):
                return bass.AP(tensor=v.tensor, offset=v.offset, ap=[[0, P], [1, n]])

            act.dma_start(qkg[:, 0, :], rows(q_norm_g, AD)).then_inc(s("small_in"), 16)
            act.dma_start(qkg[:, 1, :], rows(k_norm_g, AD)).then_inc(s("small_in"), 16)
            act.dma_start(ong[:, :], rows(o_norm_g, GDV)).then_inc(s("small_in"), 16)
            act.dma_start(wgk[:, :, :], w_in[0].rearrange("(k p) c -> p k c", p=P)[:, :, OFF["gk"]:OFF["gk"] + RANK]).then_inc(s("small_in"), 16)
            act.dma_start(gk2[0:RANK, :], w_gk2[0]).then_inc(s("small_in"), 16)
            act.dma_start(gk2[RANK:, :], b_gk).then_inc(s("small_in"), 16)

            act.wait_ge(s("c_in"), 32)
            act.activation(crow[:, 1, :], crow[:, 0, :], ACT.Silu).then_inc(*done("c_silu"))
            for h in range(AH):
                act.wait_ge(s("bias_ps"), h + 1)
                if h >= 2:
                    act.wait_ge(s(f"bias_out{h % 2}"), 16 * (h // 2))
                act.activation(bias_stage[:, h % 2, :], ps[:, 6 + h % 2, 0:TAB], ACT.Copy)
                act.activation(rbfar[:, h:h + 1], ps[:, 6 + h % 2, 0:1], ACT.Copy).then_inc(s("bias_copied"), 1)
            for k in range(KD):
                act.wait_ge(s("xT_ready"), k + 1)
                if k >= 2:
                    act.wait_ge(s("sq_used"), k - 1)
                act.activation(sq[:, k % 2, :], xT[:, k, :], ACT.Square).then_inc(s("sq_ready"), 1)
            act.wait_ge(*after("var_ready"))
            act.activation(rstd, var, ACT.Sqrt).then_inc(*done("rstd_ready"))

            def modulate(a, name):
                for k in range(KD):
                    act.wait_ge(s(name + "_scaled"), k + 1)
                    act.activation(hT[:, k, 0:SEQ], hT[:, k, 0:SEQ], ACT.Identity, bias=mod[:, 3 * a, k, 0:1],
                                   scale=gain[:, a, k, 0:1]).then_inc(s(name + "_ready"), 1)

            modulate(0, "h")
            for n in range(15):
                t0, T = TILES[n % 5]
                act.wait_ge(s("pj"), n + 1)
                if n == 0:
                    act.wait_ge(s("h_ready"), KD)
                if n < 10:
                    if n:
                        act.wait_ge(s("qk_var"), n)
                    act.activation(tok_sq[0:T, :], ps[0:T, n % 4, :], ACT.Square).then_inc(s("qk_sq"), 1)
                else:
                    act.activation(v_tok[0:T, n % 5, :], ps[0:T, n % 4, :], ACT.Copy).then_inc(s("v_ready"), 1)
            for x in range(34):
                if x < 32:
                    n = P * (x % 4 + 1)
                    c = 32 + 4 * (x % 2)
                    act.wait_ge(s("sc_max"), x + 1)
                    act.activation(sc_p[:, x % 3, 0:n], sc_p[:, x % 3, 0:n], ACT.Exp, bias=st[:, c:c + 1],
                                   accum_out=st[:, c + 1:c + 2]).then_inc(s("sc_exp"), 1)
                if x >= 2:
                    y = x - 2
                    act.wait_ge(s("p_tr"), y + 1)
                    if y >= 2:
                        act.wait_ge(s("p_pv"), y - 1)
                    act.activation(pt_p[:, y % 2, 0:P * (y % 4 + 1)], ps[:, 2 + y % 2, 0:P * (y % 4 + 1)], ACT.Copy).then_inc(s("p_T"), 1)
            def exponent(g):
                act.wait_ge(s("l_max"), g + 1)
                act.activation(logits[g], logits[g], ACT.Exp, bias=st[:, 48:49], accum_out=st[:, 49:50]).then_inc(s("l_exp"), 1)

            def weights(g):
                if g:
                    act.wait_ge(s("pv_s"), KEY_PAGES // 16)
                for q in range(5):
                    act.wait_ge(s("pr_tr"), 5 * g + q + 1)
                    if q < 4:
                        act.activation(prT[:, 4 * q:4 * q + 4, :], grid(ps[:, 6 + q % 2, :], 4), ACT.Copy).then_inc(s("pr_T"), 1)
                    else:
                        act.activation(prT[0:NS, PAGES, :], ps[0:NS, 3, 384:512], ACT.Copy).then_inc(s("pr_T"), 1)

            act.wait_ge(s("p_ov"), 32)
            act.wait_ge(s("p_pv"), 32)
            act.wait_ge(s("k_out0"), 16 * 2)
            act.wait_ge(s("k_out1"), 16 * 3)
            act.wait_ge(*after("own_ps"))
            for pg in range(KEY_PAGES):
                act.wait_ge(s("page_tr"), pg + 1)
                if pg >= 8:
                    act.wait_ge(s("page_sc"), pg // 4 - 1)
                act.activation(kpage[:, pg % 8, :], ps[:, pg % 3, :], ACT.Copy).then_inc(s("page_T"), 1)
                if pg == 4 * EXP_AT + 3:
                    exponent(0)
                if pg == 4 * WEIGHTS_AT + 3:
                    weights(0)
            exponent(1)
            weights(1)
            for g in range(2):
                act.wait_ge(s("o_sel"), g + 1)
                act.activation(o_aT[:, :, SEQ + 16 * g:SEQ + 16 * g + 16], grid(ps[:, 2, 64 * g:64 * g + 64], PAIRS), ACT.Copy)\
                   .then_inc(s("oa_taken"), 1)
            act.wait_ge(*after("gk_ps"))
            act.wait_ge(*after("gk_ones"))
            act.wait_ge(s("v_out"), 32)
            act.activation(halves(gkT[0:RANK, :]), wide(0, RANK), ACT.Copy).then_inc(*done("gk_ready"))
            for h in range(GH):
                act.wait_ge(s("la_min"), h + 1)
                parts = [(ps[:, 0, :], la[:, 0:512], kend.rearrange("p a b -> p (a b)")[:, 0:512]),
                         (ps[0:NS, 1, 0:P], la[0:NS, 512:640], kend.rearrange("p a b -> p (a b)")[0:NS, 512:640])]
                for a, b, c in parts:
                    act_chain(act, act.activation(c, a, ACT.Abs))
                    act_chain(act, act.activation(c, c, ACT.Exp, scale=-1.0))
                    last = act.activation(c, c, ACT.Ln, bias=1.0)
                last.then_inc(s("la_ln"), 1)
                act.wait_ge(s("cum_ps"), h + 1)
                for a, b in ((ps[:, 2, :], slice(0, SEQ)), (ps[:, 3, 0:NS], sample)):
                    act.activation(e_cum[:, b], a, ACT.Exp)
                    last = act.activation(e_neg[:, b], a, ACT.Exp, scale=-1.0)
                last.then_inc(s("e_ready"), 1)
                act.wait_ge(s("end_ready"), h + 1)
                act.activation(e_end, e_end, ACT.Exp).then_inc(s("e_end"), 1)
                for i, (_, T) in enumerate(TILES):
                    act.wait_ge(s("v_ps"), 3 * h + i // 2 + 1)
                    act.activation(v_g[0:T, i, :], ps[0:T, i // 2, GDV * (i % 2):GDV * (i % 2) + GDV], ACT.Copy).then_inc(s("vg_ready"), 1)
                for i, (_, T) in enumerate(TILES):
                    act.wait_ge(s("og_ps"), 3 * h + i // 2 + 1)
                    act.activation(og[0:T, i, :], ps[0:T, 4 + i // 2, GDV * (i % 2):GDV * (i % 2) + GDV], ACT.Silu).then_inc(s("og_raw"), 1)
                act.wait_ge(s("kend_tr"), h + 1)
                act.activation(kend[:, 0:4, :], grid(ps[:, 3, :], 4), ACT.Copy)
                act.activation(kend[0:NS, 4, :], ps[0:NS, 7, 0:P], ACT.Copy).then_inc(s("kend_ready"), 1)
                for i, (t0, T) in enumerate(TILES):
                    n = 5 * h + i
                    act.wait_ge(*((s("inter"), (NCH - 1) * h + CPT * i + CPT - 1) if i < PT else (s("o_ps"), h + 1)))
                    if n >= 1:
                        act.wait_ge(s("o_var"), n)
                    act.activation(junk[0:T, :], ps[0:T, i % 2, 0:GDV], ACT.Square,
                                   accum_out=st[0:T, 60:61]).then_inc(s("o_sq"), 1)
                    act.wait_ge(s("on_tr"), n + 1)
                    act.activation(o_gT[:, 2 * h:2 * h + 2, t0:t0 + T], grid(ps[:, 3, 0:2 * T], 2), ACT.Copy).then_inc(s("og_T"), 1)
            act.wait_ge(s("state_p_out"), 16 * GH)
            act.wait_ge(s("state_s_out"), 16 * GH)
            for t in range(KD):
                act.wait_ge(s("ga_ps"), t + 1)
                if t >= 2:
                    act.wait_ge(s("merged"), t - 1)
                act.activation(halves(m_a[:, t % 2, :]), wide(0), ACT.Sigmoid).then_inc(s("ga_sig"), 1)
                act.wait_ge(s("gb_ps"), t + 1)
                act.activation(halves(m_b[:, t % 2, :]), wide(1), ACT.Sigmoid).then_inc(s("gb_sig"), 1)
            for k in range(KD):
                act.wait_ge(s("x1T"), k + 1)
                if k == 0:
                    act.wait_ge(s("out_ps"), KD)
                if k >= 2:
                    act.wait_ge(s("sq_used"), KD + k - 1)
                act.activation(sq2[:, k % 2, :], xT[:, k, :], ACT.Square).then_inc(s("sq_ready"), 1)
            act.wait_ge(*after("var2_ready"))
            act.activation(rstd2, var2, ACT.Sqrt).then_inc(*done("rstd2_ready"))
            modulate(1, "h2")
            for i, (_, T) in enumerate(TILES):
                act.wait_ge(s("x1_tr"), i + 1)
                act.activation(x1_tok[0:T, i, :].rearrange("p (a b) -> p a b", a=2), ps[0:T, 2:4, :], ACT.Copy).then_inc(s("x1_tok"), 1)
            act.wait_ge(*after("lg_max"))
            act.activation(both[:, :, 0:NG], both[:, :, 0:NG], ACT.Exp).then_inc(*done("lg_exp"))
            act.wait_ge(*after("e_gap"))
            act.activation(st[:, 200:205], st[:, 200:205], ACT.Exp).then_inc(*done("e_gap_exp"))
            act.wait_ge(*after("g_tr"))
            act.activation(grid(g2p, 2), ps[:, 4:6, :], ACT.Copy)
            act.activation(grid(g2s, 2), ps[0:NS, 6:8, :], ACT.Copy).then_inc(*done("g_rows"))
            def act_down(e, par):
                act.wait_ge(s("ye_ready"), e + 1)
                dst = y_dram.rearrange("(r b) (h c) -> b h r c", b=EB, h=2)[bass.DynSlice(e, 1)].rearrange("a h r c -> (a h) r c")
                act.dma_start(dst, ye[par]).then_inc(s(f"ye_out{par}"), 16)

            def act_step(e, par, before):
                act.wait_ge(s("xs_tr"), e + 1)
                act.activation(xsT[par], ps[:, par, :], ACT.Copy).then_inc(s("xsT"), 1)
                if before:
                    act_down(e - 1, 1 - par)
                act.wait_ge(w_used, e * 3 + (EXP_USED + 2))
                act.activation(hid[par], ps[:, 2 + par, 0:256], ACT.Silu).then_inc(s("hid_gate"), 1)

            act_step(0, 0, False)
            with act.Fori(0, NE // 2 - 1) as i:
                act_step(2 * i + 1, 1, True)
                act_step(2 * i + 2, 0, True)
            act_step(NE - 1, 1, True)
            act_down(NE - 1, 1)

            def more(c):
                act_step(c + NE, 0, False)
                act_down(c + NE, 0)

            count = further_blocks(act, more)
            act.wait_ge(s("ye_out1"), 16 * (NE // 2))
            act.wait_ge(s("ye_out0"), count * 16 + 16 * (NE // 2))
            act.activation(st[0:1, 250:251], st[0:1, 200:201], ACT.Copy).then_inc(*done("rows_out"))
            for i, (t0, T) in enumerate(TILES):
                act.wait_ge(s("y_ready"), i + 1)
                dst = y_prompt[0, t0:t0 + T, :] if i < PT else y_sample.rearrange("b t d -> (b t) d")
                act.dma_start(dst, ya[0:T, i % 2, :]).then_inc(s(f"y_out{i % 2}"), 16)
            act.wait_ge(s("y_out0"), 48)
            act.wait_ge(s("y_out1"), 32)
        @blk.vector
        def _(dve):
            link = lambda ins: dve_chain(dve, ins)
            dve.memset(rbx[:, :], NEG).then_inc(*done("rbx_set"))
            dve.memset(own_s, NEG).then_inc(*done("sample_set"))
            dve.wait_ge(*after("sample_set"))
            dve.wait_ge(s("small_in"), 16 * 8)
            dve.wait_ge(s("const_in"), 16)
            link(dve.tensor_scalar(qkg[:, 0, :], qkg[:, 0, :], AD ** -0.5, None, ALU.mult))
            dve.tensor_copy(rbw.rearrange("b (h p) -> b h p", h=AH), bc(rbx[:, :].unsqueeze(2), [BUCKETS + 1, AH, P])).then_inc(*done("rbw_ready"))
            dve.wait_ge(*after("c_tr"))
            link(dve.tensor_copy(vT[:, :], ps[:, 5, 128:192]))
            dve.tensor_copy(cT[:, :, :], grid(ps[:, 5, 0:72], KD)).then_inc(*done("cT"))
            for i in range(len(ADA)):
                k = i - AH // 2 - 1
                if k >= 0:
                    dve.wait_ge(s("x_tr"), k + 1)
                    w = k % 2
                    dve.tensor_copy(xT[:, k, 0:SEQ], ps[:, 2 * w, :])
                    dve.tensor_copy(xT[:, k, sample], ps[:, 2 * w + 1, 0:NS]).then_inc(s("xT_ready"), 1)
                dve.wait_ge(w_used, i + 1)
                if i >= 2:
                    dve.wait_ge(s("mod_tr"), i - 1)
                dve.tensor_copy(mod_rows[:, i % 2, :], ps[0:DEC_B + 1, 5, :]).then_inc(s("mod_rows"), 1)
            dve.wait_ge(s("x_tr"), KD)
            dve.tensor_copy(xT[:, KD - 1, 0:SEQ], ps[:, 2, :])
            dve.tensor_copy(xT[:, KD - 1, sample], ps[:, 3, 0:NS]).then_inc(s("xT_ready"), 1)
            dve.wait_ge(s("sq_used"), KD)
            link(dve.tensor_scalar(halves(var), wide(3), 1.0 / D, EPS, ALU.mult, ALU.add))
            dve.reciprocal(var, var).then_inc(*done("var_ready"))
            dve.wait_ge(s("mod_tr"), len(ADA))
            flat_mod = mod[:, :, :, :].rearrange("p a k c -> p (a k) c")
            link(dve.tensor_tensor(flat_mod, grid(ps[:, 4, 0:432], 48), bc(vT[:, 0:48].unsqueeze(2), [P, 48, DEC_B + 1]), ALU.add))
            for a in range(2):
                last = dve.scalar_tensor_tensor(gain[:, a, :, :], mod[:, 3 * a + 1, :, :], 1.0,
                                                bc(vT[:, 48 + 8 * a:56 + 8 * a].unsqueeze(2), [P, KD, DEC_B + 1]), ALU.add, ALU.mult)
            link(last)

            def by_sequence(v):
                return v.rearrange("p (b t) -> p b t", t=DEC_T)

            def modulate(a, r, ready):
                for k in range(KD):
                    dve.tensor_tensor(hT[:, k, :], xT[:, k, :], r, ALU.mult).then_inc(s(ready + "_scaled"), 1)
                dve.wait_ge(s(ready + "_scaled"), KD)
                v = hT[:, :, sample].rearrange("p k (b t) -> p k b t", t=DEC_T)
                full = [P, KD, DEC_B, DEC_T]
                link(dve.tensor_tensor(v, v, bc(gain[:, a, :, 1:].unsqueeze(3), full), ALU.mult))
                dve.tensor_tensor(v, v, bc(mod[:, 3 * a, :, 1:].unsqueeze(3), full), ALU.add).then_inc(*done(ready + "_sample"))

            dve.wait_ge(*after("rstd_ready"))
            modulate(0, rstd, "h")
            dve.wait_ge(s("near_s_in"), 16 * 8)
            for g in range(2):
                for j in range(4):
                    q = slice(32 * j, 32 * j + 32)
                    b = DEC_T * (4 * g + j)
                    dve.tensor_copy(own_s[q, g, b:b + DEC_T], near_s[q, PAGE:PAGE + DEC_T])
            for m in range(11):
                if m < 10:
                    t0, T = TILES[m % 5]
                    c = 16 * (m % 2)
                    dve.wait_ge(s("qk_sq"), m + 1)
                    link(dve.tensor_reduce(st[0:T, c:c + 8], tok_sq[0:T, :].rearrange("p (h d) -> p h d", h=AH), AX.X, ALU.add))
                    dve.tensor_scalar(st[0:T, c:c + 8], st[0:T, c:c + 8], 1.0 / AD, EPS, ALU.mult, ALU.add).then_inc(s("qk_var"), 1)
                if m:
                    y = m - 1
                    t0, T = TILES[y % 5]
                    dve.wait_ge(s("qk_tr"), y + 1)
                    dst = (qT, kT)[y // 5]
                    dve.tensor_copy(dst[:, :, t0:t0 + T], grid(ps[:, 4 + y % 2, 0:4 * T], PAIRS)).then_inc(s("qk_T"), 1)
                if m < 10:
                    t0, T = TILES[m % 5]
                    c = 16 * (m % 2)
                    dve.wait_ge(s("qk_rstd"), m + 1)
                    if m >= 7:
                        dve.wait_ge(s(f"k_out{m % 2}"), 16 * ((m - 5) // 2))
                    v = tok[0:T, m % 2, :].rearrange("p (h d) -> p h d", h=AH)
                    dve.tensor_tensor(v, grid(ps[0:T, m % 4, :], AH), bc(st[0:T, c + 8:c + 16].unsqueeze(2), [T, AH, AD]),
                                      ALU.mult).then_inc(s("pj_free"), 1)
                    dve.wait_ge(s("pj_free"), m + 1)
                    dve.tensor_tensor(v, v, bc(qkg[0:T, m // 5, :].unsqueeze(1), [T, AH, AD]), ALU.mult).then_inc(s("qk_tok"), 1)
            dve.wait_ge(s("near_in"), 16)
            for x in range(32 + 4):
                if x < 32:
                    h, i = x // 4, x % 4
                    c = 32 + 4 * (x % 2)
                    n = P * (i + 1)
                    far = P * max(i - 1, 0)
                    dve.wait_ge(s("sc_ps"), x + 1)
                    if x >= 3:
                        dve.wait_ge(s("p_tr"), x - 2)
                    if far:
                        dve.tensor_scalar(sc_p[:, x % 3, 0:far], ps[:, x % 2, 0:far], rbfar[:, h:h + 1], None, ALU.add)
                    link(dve.tensor_tensor(sc_p[:, x % 3, far:n], ps[:, x % 2, far:n], near[:, h, 2 * P - (n - far):2 * P], ALU.add))
                    dve.tensor_reduce(st[:, c:c + 1], sc_p[:, x % 3, 0:n], AX.X, ALU.max, negate=True).then_inc(s("sc_max"), 1)
                if 1 <= x <= 32:
                    y = x - 1
                    c = 32 + 4 * (y % 2)
                    n = P * (y % 4 + 1)
                    dve.wait_ge(s("sc_exp"), y + 1)
                    link(dve.reciprocal(st[:, c + 2:c + 3], st[:, c + 1:c + 2]))
                    dve.tensor_scalar(sc_p[:, y % 3, 0:n], sc_p[:, y % 3, 0:n], st[:, c + 2:c + 3], None, ALU.mult).then_inc(s("p_norm"), 1)
                if x >= 4:
                    y = x - 4
                    h, i = y // 4, y % 4
                    rows = slice(64 * (h % 2), 64 * (h % 2) + 64)
                    dve.wait_ge(s("p_pv"), y + 1)
                    dve.tensor_copy(o_aT[rows, h // 2, P * i:P * i + P], ps[rows, 4 + y % 2, 0:P]).then_inc(s("p_ov"), 1)
            dve.wait_ge(s("k_out0"), 16 * 2)
            dve.wait_ge(s("k_out1"), 16 * 3)
            dve.wait_ge(s("v_out"), 32)
            link(dve.memset(q_row.rearrange("p a b c -> p (a b c)"), 0.0))
            for a in range(PAIRS):
                for odd in range(2):
                    rows = slice(64 * odd, 64 * odd + 64)
                    c = 8 * a + 4 * odd
                    last = dve.tensor_copy(q_row[rows, a, :, c:c + DEC_T], qT[rows, a, sample].rearrange("p (b t) -> p b t", t=DEC_T))
            last.then_inc(*done("q_row"))
            dve.wait_ge(*after("own_ps"))
            for g in range(2):
                dve.tensor_tensor(logits[g][:, PAST:], ps[:, 3, NS * g:NS * g + NS], own_s[:, g, :], ALU.add)

            def softmax(g):
                logit = logits[g]
                dve.wait_ge(s("sc_taken"), 4 * g + 4)
                gate, comb = st[:, 80:88], st[:, 88:96]
                link(dve.tensor_reduce(gate, grid(logit[:, 0:PAST], NBLK), AX.X, ALU.add))
                c0, c1 = grid(cmp8[:, 0, 0:64], 8), grid(cmp8[:, 1, 0:64], 8)
                gi, gj = bc(gate.unsqueeze(1), [P, 8, 8]), bc(gate.unsqueeze(2), [P, 8, 8])
                link(dve.tensor_tensor(c0, gi, gj, ALU.is_equal))
                link(dve.tensor_tensor(c0, c0, grid(own_lower8, 8), ALU.mult))
                link(dve.tensor_tensor(c1, gi, gj, ALU.is_gt))
                link(dve.tensor_tensor(c0, c0, c1, ALU.add))
                link(dve.tensor_reduce(comb, c0, AX.X, ALU.add))
                link(dve.tensor_scalar(comb, comb, float(TOPK), NEG, ALU.is_ge, ALU.mult))
                near_part = logit[:, PAST - PAGE:PAST]
                link(dve.scalar_tensor_tensor(near_part, near_part, comb[:, 7:8], near_s[:, 0:PAGE], ALU.add, ALU.add))
                link(dve.tensor_scalar(comb, comb, far_s[:, 0:1], None, ALU.add))
                v = grid(logit[:, 0:PAST - BLK], NBLK - 1)
                dve.tensor_tensor(v, v, bc(comb[:, 0:7].unsqueeze(2), [P, NBLK - 1, BLK]), ALU.add)
                v = logit[:, PAST - BLK:PAST - PAGE]
                link(dve.tensor_scalar(v, v, comb[:, 7:8], None, ALU.add))
                dve.tensor_reduce(st[:, 48:49], logit, AX.X, ALU.max, negate=True).then_inc(s("l_max"), 1)
                dve.wait_ge(s("l_exp"), g + 1)
                link(dve.reciprocal(st[:, 50:51], st[:, 49:50]))
                dve.tensor_scalar(logit, logit, st[:, 50:51], None, ALU.mult).then_inc(s("l_norm"), 1)

            for n in range(QUADS // 4):
                dve.wait_ge(s("page_sc"), 4 * n + 4)
                dve.tensor_copy(logits[n // 4][:, 512 * (n % 4):512 * (n % 4) + 512], ps[:, 4 + n % 2, :]).then_inc(s("sc_taken"), 1)
                if n % 4 == 3:
                    softmax(n // 4)
            for g in range(2):
                dve.wait_ge(s("pv_s"), KEY_PAGES // 16 * (g + 1))
                dve.tensor_tensor(o_rows[:, g, :].rearrange("p (h d) -> p h d", h=AH), grid(ps[:, g, :], AH),
                                  bc(const("row_head").unsqueeze(2), [P, AH, AD]), ALU.mult).then_inc(s("o_rows"), 1)
            dve.wait_ge(s("oa_taken"), 2)
            dve.wait_ge(s("v_out"), 32)
            dve.memset(att.rearrange("p a b -> p (a b)"), 0.0).then_inc(*done("att_set"))
            dve.memset(gkT, 1.0).then_inc(*done("gk_ones"))
            link(dve.memset(q_mask, 0.0))
            link(dve.memset(on_[0:NS, :, :], 0.0))
            for h in range(GH):
                dve.wait_ge(s("la_ps"), h + 1)
                parts = [(ps[:, 0, :], la[:, 0:512], kend.rearrange("p a b -> p (a b)")[:, 0:512]),
                         (ps[0:NS, 1, 0:P], la[0:NS, 512:640], kend.rearrange("p a b -> p (a b)")[0:NS, 512:640])]
                for a, b, c in parts:
                    last = dve.tensor_scalar(b, a, 0.0, None, ALU.min)
                last.then_inc(s("la_min"), 1)
                dve.wait_ge(s("la_min"), h + 1)
                dve.wait_ge(s("la_ln"), h + 1)
                for a, b, c in parts:
                    last = dve.tensor_tensor(b, b, c, ALU.subtract)
                link(last)
                for a, b, c in parts:
                    last = dve.tensor_scalar(b, b, 1.0 / GNORM, None, ALU.mult)
                last.then_inc(s("la_ready"), 1)
                dve.wait_ge(s("e_ready"), h + 1)
                dve.tensor_copy(e_end[:, 0:SEQ], ps[:, 2, :])
                link(dve.tensor_copy(e_end[:, sample], ps[:, 3, 0:NS]))
                for v, src, n, w in ((e_end[:, 0:SEQ], ps[:, 2, :], NCH, CHUNK), (e_end[:, sample], ps[:, 3, 0:NS], DEC_B, DEC_T)):
                    last = dve.tensor_tensor(grid(v, n), bc(grid(src, n)[:, :, w - 1:w], [P, n, w]), grid(v, n), ALU.subtract)
                last.then_inc(s("end_ready"), 1)
                decay = st[:, 100:124]
                dve.tensor_copy(decay[:, 0:NCH].unsqueeze(2), grid(e_cum[:, 0:SEQ], NCH)[:, :, CHUNK - 1:CHUNK])
                link(dve.tensor_copy(decay[:, NCH:].unsqueeze(2), grid(e_cum[:, sample], DEC_B)[:, :, DEC_T - 1:DEC_T]))
                dve.wait_ge(s("qk_ps"), h + 1)
                dve.scalar_tensor_tensor(halves(e_cum), wide(2), GDK ** -0.5, halves(e_cum), ALU.mult, ALU.mult)
                link(dve.tensor_tensor(halves(e_neg), wide(3), halves(e_neg), ALU.mult))
                dve.wait_ge(s("e_end"), h + 1)
                dve.tensor_tensor(halves(e_end), wide(3), halves(e_end), ALU.mult).then_inc(s("qkt_ready"), 1)
                dve.tensor_copy(grid(q_mask, DEC_B)[:, :, 0:DEC_T], e_cum[:, sample].rearrange("p (b t) -> p b t", t=DEC_T))\
                   .then_inc(s("q_mask"), 1)
                def finish(i, T):
                    n = 5 * h + i
                    c = 64 + 2 * (n % 2)
                    dve.wait_ge(s("o_sq"), n + 1)
                    dve.tensor_scalar(st[0:T, c:c + 1], st[0:T, 60:61], 1.0 / GDV, EPS, ALU.mult, ALU.add).then_inc(s("o_var"), 1)
                    dve.wait_ge(s("o_rstd"), n + 1)
                    dve.wait_ge(s("og_ready"), n + 1)
                    dve.scalar_tensor_tensor(on_[0:T, n % 2, :], ps[0:T, i % 2, 0:GDV], st[0:T, c + 1:c + 2], og[0:T, i, :],
                                             ALU.mult, ALU.mult).then_inc(s("on_ready"), 1)

                def masked(i, T, mask, n):
                    dve.wait_ge(s("att_ps"), n + 1)
                    dst = att[:, i % 2, :] if T == P else cmp8[0:NS, 0, 0:NS]
                    dve.copy_predicated(dst, mask.bitcast(U32), ps[0:T, 2, P * (i % 2):P * (i % 2) + T]).then_inc(s("att_ready"), 1)

                for i in range(PT):
                    masked(i, P, const("chunk_causal"), 5 * h + i)
                    for c in range(CPT * i, CPT * i + CPT):
                        n = NCH * h + c
                        dve.wait_ge(s("u_ps"), n + 1)
                        new, old = state[:, (c + 1) % 2, :], state[:, c % 2, :]
                        if c == 0:
                            if h:
                                dve.wait_ge(s("state_p_out"), 16 * h)
                            dve.tensor_copy(new, ps[:, 4 + c % 4, 0:GDV]).then_inc(s("state_new"), 1)
                        else:
                            dve.wait_ge(s("state_new"), n)
                            dve.wait_ge(s("inter"), (NCH - 1) * h + c - 1)
                            dve.scalar_tensor_tensor(new, old, decay[:, c:c + 1], ps[:, 4 + c % 4, 0:GDV], ALU.mult, ALU.add)\
                               .then_inc(s("state_new"), 1)
                    finish(i, P)
                if h == 0:
                    link(dve.memset(cmp8[0:NS, 0, 0:NS], 0.0))
                masked(4, NS, const("seq_causal"), 5 * h + 4)
                dve.tensor_tensor(kend_m, bc(kend[0:NS, 4, :].unsqueeze(1), [NS, DEC_B, P]),
                                  bc(const("seq_member").unsqueeze(2), [NS, DEC_B, P]), ALU.mult).then_inc(s("kend_m"), 1)
                finish(4, NS)
                for b in range(DEC_B):
                    n = DEC_B * h + b
                    dve.wait_ge(s("us_ps"), n + 1)
                    dve.scalar_tensor_tensor(state_s[:, b, :], state_s[:, b, :], decay[:, NCH + b:NCH + b + 1],
                                             ps[:, 4 + b % 4, 0:GDV], ALU.mult, ALU.add).then_inc(s("state_s_new"), 1)
            for t in range(KD):
                for v, w, a in ((m_a, 2, "a"), (m_b, 3, "b")):
                    dve.wait_ge(s(f"g{a}_sig"), t + 1)
                    dve.wait_ge(s(f"p{a}_ps"), t + 1)
                    dve.tensor_tensor(halves(v[:, t % 2, :]), halves(v[:, t % 2, :]), wide(w), ALU.mult).then_inc(s("m_ready" if a == "b" else "m_half"), 1)
            for t in range(KD):
                w = 2 * (t % 3)
                dve.wait_ge(s("out_ps"), t + 1)
                g1 = mod[:, 2, t, 0:1]
                dve.scalar_tensor_tensor(xT[:, t, 0:HALF], ps[:, w, 0:HALF], g1, xT[:, t, 0:HALF], ALU.mult, ALU.add)
                dve.scalar_tensor_tensor(xT[:, t, HALF:SEQ], ps[:, w + 1, 0:SEQ - HALF], g1, xT[:, t, HALF:SEQ], ALU.mult, ALU.add)
                z = st[:, 128 + 32 * (t % 2):160 + 32 * (t % 2)]
                link(dve.tensor_tensor(by_sequence(z), by_sequence(ps[:, w + 1, SEQ - HALF:HALF]),
                                       bc(mod[:, 2, t, 1:].unsqueeze(2), [P, DEC_B, DEC_T]), ALU.mult))
                dve.tensor_tensor(xT[:, t, sample], xT[:, t, sample], z, ALU.add).then_inc(s("x1T"), 1)
            dve.wait_ge(s("sq_used"), 2 * KD)
            link(dve.tensor_scalar(halves(var2), wide(3), 1.0 / D, EPS, ALU.mult, ALU.add))
            dve.reciprocal(var2, var2).then_inc(*done("var2_ready"))
            dve.wait_ge(*after("rstd2_ready"))
            modulate(1, rstd2, "h2")
            dve.wait_ge(s("h2_ready"), KD)
            for t in range(KD):
                dve.tensor_copy(g_exp[:, t, 0:P], bc(mod[:, 5, t, 0:1], [P, P]))
                last = dve.tensor_copy(by_sequence(g_exp[:, t, P:]), bc(mod[:, 5, t, 1:].unsqueeze(2), [P, DEC_B, DEC_T]))
            last.then_inc(*done("g_exp2"))
            for i, (_, T) in enumerate(TILES):
                dve.wait_ge(s("h2_tr"), i + 1)
                dve.tensor_copy(grid(h2_tok[0:T, i, :], 2), ps[0:T, 0:2, :]).then_inc(s("h2_tok"), 1)
            link(dve.memset(lg[:, :, :], 0.0))
            dve.wait_ge(*after("lg_ps"))
            dve.tensor_copy(lg[:, 0:PT, :], grid(ps[:, 6, 0:PT * 36], PT))
            link(dve.tensor_copy(lg[0:NS, PT, :], ps[0:NS, 6, PT * 36:5 * 36]))
            lgg = lg[:, :, 0:NG]
            W = P
            c0, c1 = (grid(cmp8[:, a, 0:80], 5).rearrange("p a (j i) -> p a j i", j=NG) for a in range(2))
            gsel = cmp8[:, 1, 128:148].rearrange("p (a j) -> p a j", a=5)

            def tie(dst, v, n, low):
                a = grid(cmp8[:, 0, 0:n * n], n)
                b = grid(cmp8[:, 1, 0:n * n], n)
                vi, vj = bc(v.unsqueeze(1), [P, n, n]), bc(v.unsqueeze(2), [P, n, n])
                link(dve.tensor_tensor(a, vi, vj, ALU.is_equal))
                link(dve.tensor_tensor(a, a, grid(low, n), ALU.mult))
                link(dve.tensor_tensor(b, vi, vj, ALU.is_gt))
                link(dve.tensor_tensor(a, a, b, ALU.add))
                link(dve.tensor_reduce(dst, a, AX.X, ALU.add))

            grank = cmp8[:, 1, 100:120].rearrange("p (a j) -> p a j", a=5)
            for i in range(5):
                tie(grank[:, i, :], lg[:, i, 0:NG], NG, own_lower4)
            link(dve.tensor_scalar(gsel, grank, 0.5, None, ALU.is_lt))
            gmax = st[:, 128:133]
            link(dve.tensor_reduce(gmax, lgg, AX.X, ALU.max))
            dve.tensor_tensor(both[:, :, 0:NG], lgg, bc(gmax.unsqueeze(2), [P, 5, NG]), ALU.subtract).then_inc(*done("lg_max"))
            dve.wait_ge(*after("lg_exp"))
            psum_g = st[:, 136:141]
            link(dve.tensor_reduce(psum_g, both[:, :, 0:NG], AX.X, ALU.add))
            pg = st[:, 144:149]
            link(dve.reciprocal(pg, psum_g))
            e4 = lg[:, :, NG:].rearrange("p a (g e) -> p a g e", g=NG)
            b4 = both[:, :, :].rearrange("p a (g e) -> p a g e", g=NG)
            link(dve.tensor_tensor(b4, e4, bc(gsel.unsqueeze(3), [P, 5, NG, EPG]), ALU.mult))
            ein = st[:, 152:192].rearrange("p (a e) -> p a e", a=5)
            link(dve.tensor_reduce(ein, both[:, :, :].rearrange("p a (g e) -> p a e g", g=NG), AX.X, ALU.add))
            erank = st[:, 208:248].rearrange("p (a e) -> p a e", a=5)
            for i in range(5):
                tie(erank[:, i, :], ein[:, i, :], EPG, own_lower8)
            hots = []
            for c, oh in ((0, one1), (1, one2)):
                r = cmp8[:, 0, 0:40].rearrange("p (a e) -> p a e", a=5)
                link(dve.tensor_scalar(r, erank, float(c), None, ALU.is_equal))
                o4 = oh[:, :, :].rearrange("p a (g e) -> p a g e", g=NG)
                for i in range(5):
                    dve.tensor_tensor(o4[:, i], bc(gsel[:, i, :].unsqueeze(2), [P, NG, EPG]), bc(r[:, i, :].unsqueeze(1), [P, NG, EPG]), ALU.mult)
                z = cmp8[:, 0, 40:80].rearrange("p (a e) -> p a e", a=5)
                link(dve.tensor_tensor(z, r, ein, ALU.mult))
                link(dve.tensor_reduce(st[:, 192 + 8 * c:197 + 8 * c], z, AX.X, ALU.add))
            dve.tensor_tensor(st[:, 200:205], st[:, 200:205], st[:, 192:197], ALU.subtract).then_inc(*done("e_gap"))
            real = bc(const("token_real").unsqueeze(2), [P, 5, NE])
            link(dve.tensor_tensor(both[:, :, :], one1[:, :, :], one2[:, :, :], ALU.add))
            dve.tensor_tensor(both[:, :, :], both[:, :, :], real, ALU.mult).then_inc(*done("chosen"))
            dve.wait_ge(*after("e_gap_exp"))
            den = st[:, 128:133]
            link(dve.tensor_scalar(den, st[:, 200:205], 1.0, None, ALU.add))
            link(dve.reciprocal(den, den))
            link(dve.tensor_tensor(wts[:, 0, :], den, pg, ALU.mult))
            link(dve.tensor_tensor(wts[:, 1, :], wts[:, 0, :], st[:, 200:205], ALU.mult))
            link(dve.tensor_copy(tok_i[:, :], const("token_id")))
            dve.wait_ge(*after("pos_ps"))
            link(dve.tensor_copy(cnt[:, :], ps[:, 7, 5 * NE:6 * NE]))
            over = blk_cmp[:, 0:NE * EDGES].rearrange("p (e c) -> p e c", e=NE)
            link(dve.tensor_tensor(over, bc(cnt[:, :].unsqueeze(2), [P, NE, EDGES]),
                                   bc(const("block_edge").unsqueeze(1), [P, NE, EDGES]), ALU.is_gt))
            link(dve.tensor_reduce(cnt[:, :], over, AX.X, ALU.add))
            ends = [cmp8[:, a, 0:NE] for a in range(2)]
            link(dve.tensor_copy(ends[0], cnt[:, :]))
            step = 1
            while step < NE:
                a, b = ends
                dve.tensor_copy(b[:, 0:step], a[:, 0:step])
                link(dve.tensor_tensor(b[:, step:], a[:, step:], a[:, 0:NE - step], ALU.add))
                ends, step = [b, a], 2 * step
            ends = ends[0]
            over = blk_cmp[:, 0:NE * MORE].rearrange("p (c e) -> p c e", c=MORE)
            link(dve.tensor_tensor(over, bc(ends.unsqueeze(1), [P, MORE, NE]), bc(const("more_id").unsqueeze(2), [P, MORE, NE]), ALU.is_le))
            link(dve.tensor_reduce(blk_cmp[:, 0:MORE], over, AX.X, ALU.add))
            link(dve.tensor_scalar(blk_cmp[:, 0:MORE], blk_cmp[:, 0:MORE], float(NE - 1), None, ALU.min))
            link(dve.tensor_copy(more_i[:, 0:MORE], blk_cmp[0:1, 0:MORE]))
            ids = const("expert_id")
            link(dve.tensor_tensor(base[:, :], ends, cnt[:, :], ALU.subtract))
            link(dve.tensor_tensor(base[:, :], base[:, :], ids, ALU.subtract))
            link(dve.tensor_scalar(base[:, :], base[:, :], float(CAP), float(CAP * (NE - 1)), ALU.mult, ALU.add))
            pos = grid(ps[:, 7, 0:5 * NE], 5)
            over = grid(blk_cmp[:, 0:5 * NE], 5)
            link(dve.tensor_scalar(over, pos, float(CAP), None, ALU.is_ge))
            link(dve.tensor_tensor(over, over, bc(base[:, :].unsqueeze(1), [P, 5, NE]), ALU.mult))
            link(dve.scalar_tensor_tensor(over, bc(ids.unsqueeze(1), [P, 5, NE]), float(CAP), over, ALU.mult, ALU.add))
            link(dve.tensor_tensor(both[:, :, :], over, pos, ALU.add))
            for c, oh in ((0, one1), (1, one2)):
                link(dve.tensor_tensor(oh[:, :, :], oh[:, :, :], both[:, :, :], ALU.mult))
                link(dve.tensor_reduce(dest[:, c, :], oh[:, :, :], AX.X, ALU.add))
            link(dve.tensor_copy(dest_i[:, :, :], dest[:, :, :]))
            link(dve.tensor_scalar(row_i[:, :, :], dest_i[:, :, :], CAP - 1, None, ALU.bitwise_and))
            link(dve.tensor_scalar(dest_i[:, :, :], dest_i[:, :, :], CAP.bit_length() - 1, None, ALU.logical_shift_right))
            dve.scalar_tensor_tensor(dest_i[:, :, :], row_i[:, :, :], float(EB), dest_i[:, :, :], ALU.mult, ALU.add)\
               .then_inc(*done("dest_ready"))
            dve.wait_ge(s("idx_in"), 16)
            dve.tensor_copy(more_i[:, MORE:], ends[0:1, NE - 1:NE]).then_inc(*done("more_ready"))
            def dve_down(e, it, par, first=False):
                dve.wait_ge(w_used, e * 3 + (EXP_USED + 3))
                if not first:
                    dve.wait_ge(s(f"ye_out{par}"), it * 16)
                dve.tensor_copy(ye[par], ps[:, 4 + par, :]).then_inc(s("ye_ready"), 1)

            def dve_step(e, it, par, before):
                if before:
                    dve_down(e - 1, before[0], 1 - par, isinstance(before[0], int) and before[0] == 0)
                dve.wait_ge(w_used, e * 3 + (EXP_USED + 2))
                dve.wait_ge(s("hid_gate"), e + 1)
                dve.tensor_tensor(hid[par], hid[par], ps[:, 2 + par, 256:512], ALU.mult).then_inc(s("hid"), 1)

            dve_step(0, 0, 0, None)
            dve_step(1, 0, 1, (0,))
            dve_step(2, 1, 0, (0,))
            with dve.Fori(1, NE // 2 - 1) as i:
                dve_step(2 * i + 1, i, 1, (i,))
                dve_step(2 * i + 2, i + 1, 0, (i,))
            dve_step(NE - 1, NE // 2 - 1, 1, (NE // 2 - 1,))
            dve_down(NE - 1, NE // 2 - 1, 1)

            def more(c):
                dve.wait_ge(s("xs_tr"), c + NE)
                dve.tensor_copy(idx_cur[:, :], idx[:, bass.DynSlice(c + NE, 1)]).then_inc(s("idx_cur"), 1)
                dve_step(c + NE, c + NE // 2, 0, None)
                dve_down(c + NE, c + NE // 2, 0)

            further_blocks(dve, more)
            for i, (_, T) in enumerate(TILES):
                q = i % 2
                dve.wait_ge(s(f"ya_in{q}"), 32 * (i // 2) + 32)
                a, b = ya[0:T, q, :], yb[0:T, q, :]
                link(dve.tensor_scalar(a, a, wts[0:T, 0, i:i + 1], None, ALU.mult))
                link(dve.scalar_tensor_tensor(a, b, wts[0:T, 1, i:i + 1], a, ALU.mult, ALU.add))
                link(dve.tensor_tensor(a, a, g2p if i < PT else g2s, ALU.mult))
                dve.tensor_tensor(a, a, x1_tok[0:T, i, :], ALU.add).then_inc(s("y_ready"), 1)
        @blk.tensor
        def _(pe):
            def mm(out, lhsT, rhs, start, stop, **k):
                return pe.matmul(out, lhsT, rhs, start=start, stop=stop, **k)

            def product(w, lhs, rhs, K, rows=P):
                for half in range(2):
                    for k in range(K):
                        last = mm(ps[0:rows, 2 * w + half, 0:HALF], lhs(k), rhs(k)[:, HALF * half:HALF * half + HALF], k == 0, k == K - 1)
                return last

            def turn(out, v):
                n = v.shape[0]
                return pe.transpose(out, v, ident[0:n, 0:n])

            pe.wait_ge(s("const_in"), 16)
            pe.wait_ge(s("vec_in"), 48)
            turn(ps[:, 5, 128:192], vrow)
            pe.wait_ge(*after("c_silu"))
            for k in range(KD):
                last = turn(ps[:, 5, 9 * k:9 * k + 9], crow[:, 1, P * k:P * k + P])
            last.then_inc(*done("c_tr"))
            pe.wait_ge(*after("cT"))
            for i in range(len(ADA) + 1):
                if i:
                    pe.wait_ge(s("mod_rows"), i)
                    for j in range(4):
                        at = 9 * (4 * (i - 1) + j)
                        last = turn(ps[:, 4, at:at + 9], mod_rows[:, (i - 1) % 2, P * j:P * j + P])
                    last.then_inc(s("mod_tr"), 1)
                if i < len(ADA):
                    n = ADA[i]
                    landed(pe, n)
                    w = grid(slot(n), KD)
                    for k in range(KD):
                        last = mm(ps[0:DEC_B + 1, 5, :], cT[:, k, :], w[:, k, :], k == 0, k == KD - 1)
                    last.then_inc(w_used, 1)
                if i < AH // 2:
                    pe.wait_ge(*after("rbw_ready"))
                    for h in (2 * i, 2 * i + 1):
                        if h >= 2:
                            pe.wait_ge(s("bias_copied"), h - 1)
                        mm(ps[:, 6 + h % 2, 0:TAB], rbw[:, P * h:P * h + P], hot, True, True).then_inc(s("bias_ps"), 1)
                k = i - AH // 2
                if 0 <= k < KD:
                    pe.wait_ge(s("x_in"), 32)
                    if k >= 2:
                        pe.wait_ge(s("xT_ready"), k - 1)
                    for j in range(PT):
                        turn(ps[:, 2 * (k % 2), P * j:P * j + P], x_tok[:, j, P * k:P * k + P])
                    turn(ps[:, 2 * (k % 2) + 1, 0:NS], x_tok[0:NS, PT, P * k:P * k + P]).then_inc(s("x_tr"), 1)
                y = k - 1
                if 0 <= y < KD:
                    if y == 0:
                        pe.wait_ge(s("bias_copied"), AH)
                    pe.wait_ge(s("sq_ready"), y + 1)
                    for half in range(2):
                        last = mm(ps[:, 6 + half, 0:HALF], ones, sq[:, y % 2, HALF * half:HALF * half + HALF], y == 0, y == KD - 1)
                    last.then_inc(s("sq_used"), 1)
            pe.wait_ge(s("h_ready"), KD)
            pe.wait_ge(*after("h_sample"))
            for n in range(15 + 1):
                if n < 15:
                    t0, T = TILES[n % 5]
                    b = QKV[n // 5]
                    landed(pe, b)
                    w = grid(slot(b), KD)
                    if 4 <= n < 14:
                        pe.wait_ge(s("pj_free"), n - 3)
                    elif n == 14:
                        pe.wait_ge(s("v_ready"), 1)
                    for k in range(KD):
                        last = mm(ps[0:T, n % 4, :], hT[:, k, t0:t0 + T], w[:, k, :], k == 0, k == KD - 1)
                    last.then_inc(s("pj"), 1)
                if 1 <= n <= 10:
                    y = n - 1
                    t0, T = TILES[y % 5]
                    pe.wait_ge(s("qk_tok"), y + 1)
                    if y >= 2:
                        pe.wait_ge(s("qk_T"), y - 1)
                    for a in range(PAIRS):
                        last = turn(ps[:, 4 + y % 2, T * a:T * a + T], tok[0:T, y % 2, P * a:P * a + P])
                    last.then_inc(s("qk_tr"), 1)
            pe.wait_ge(s("qk_T"), 10)
            pe.wait_ge(s("v_ready"), 5)
            for x in range(32 + 3):
                if x < 32:
                    h, i = x // 4, x % 4
                    rows = slice(64 * (h % 2), 64 * (h % 2) + 64)
                    n = P * (i + 1)
                    if x >= 2:
                        pe.wait_ge(s("sc_max"), x - 1)
                    mm(ps[:, x % 2, 0:n], qT[rows, h // 2, P * i:P * i + P], kT[rows, h // 2, 0:n], True, True).then_inc(s("sc_ps"), 1)
                if 2 <= x <= 33:
                    y = x - 2
                    pe.wait_ge(s("p_norm"), y + 1)
                    if y >= 2:
                        pe.wait_ge(s("p_T"), y - 1)
                    for j in range(y % 4 + 1):
                        last = turn(ps[:, 2 + y % 2, P * j:P * j + P], sc_p[:, y % 3, P * j:P * j + P])
                    last.then_inc(s("p_tr"), 1)
                if x >= 3:
                    y = x - 3
                    h, i = y // 4, y % 4
                    pe.wait_ge(s("p_T"), y + 1)
                    if y >= 2:
                        pe.wait_ge(s("p_ov"), y - 1)
                    rows = slice(64 * (h % 2), 64 * (h % 2) + 64)
                    for j in range(i + 1):
                        last = mm(ps[rows, 4 + y % 2, 0:P], v_tok[:, j, AD * h:AD * h + AD], pt_p[:, y % 2, P * j:P * j + P], j == 0, j == i)
                    last.then_inc(s("p_pv"), 1)
            pe.wait_ge(*after("q_row"))
            pe.wait_ge(s("p_ov"), 32)
            for b in range(DEC_B):
                r = slice(32 * (b % 4), 32 * (b % 4) + 32)
                for a in range(PAIRS):
                    last = mm(ps[r, 3, NS * (b // 4):NS * (b // 4) + NS], q_row[:, a, b, :], kT[:, a, sample], a == 0, a == PAIRS - 1,
                              skip_group_check=True)
            last.then_inc(*done("own_ps"))

            def weights_turned(g):
                pe.wait_ge(s("l_norm"), g + 1)
                for q in range(4):
                    if q >= 2:
                        pe.wait_ge(s("pr_T"), 5 * g + q - 1)
                    for page in range(4 * q, 4 * q + 4):
                        last = turn(ps[:, 6 + q % 2, P * (page % 4):P * (page % 4) + P], logits[g][:, P * page:P * page + P])
                    last.then_inc(s("pr_tr"), 1)
                turn(ps[0:NS, 3, 384:512], logits[g][:, PAST:]).then_inc(s("pr_tr"), 1)

            def attend(g):
                pe.wait_ge(s("pr_T"), 5 * g + 5)
                for j in range(4):
                    mm(ps[32 * j:32 * j + 32, g, :], prT[0:NS, PAGES, 32 * j:32 * j + 32], v_tok[0:NS, PT, :], True, False,
                       skip_group_check=True)
                for i in range(PAGES // 2):
                    n = PAGED[("v", PAGES // 2 * g + i)]
                    landed(pe, n)
                    for page in (2 * i, 2 * i + 1):
                        for j in range(4):
                            q = 4 * (page % 2) + j
                            last = mm(ps[32 * j:32 * j + 32, g, :], prT[:, page, 32 * j:32 * j + 32], slot(n)[:, AW * q:AW * q + AW],
                                      False, page == PAGES - 1, skip_group_check=True)
                    last.then_inc(s("pv_s"), 1)

            def selected(g):
                pe.wait_ge(s("o_rows"), g + 1)
                if g:
                    pe.wait_ge(s("oa_taken"), g)
                for a in range(PAIRS):
                    last = mm(ps[:, 2, 64 * g + 16 * a:64 * g + 16 * a + 16], o_rows[:, g, P * a:P * a + P], const("row_token"), True, True)
                last.then_inc(s("o_sel"), 1)

            for quad in range(QUADS + 1):
                if quad < QUADS:
                    for pg in range(4 * quad, 4 * quad + 4):
                        n = PAGED[("k", pg // 8)]
                        landed(pe, n)
                        if pg >= 3:
                            pe.wait_ge(s("page_T"), pg - 2)
                        for a in range(PAIRS):
                            last = turn(ps[:, pg % 3, P * a:P * a + P], slot(n)[:, AW * (pg % 8) + P * a:AW * (pg % 8) + P * a + P])
                        last.then_inc(s("page_tr"), 1)
                if quad:
                    y = quad - 1
                    g, page = y // PAGES, y % PAGES
                    pe.wait_ge(s("page_T"), 4 * y + 4)
                    if page % 4 == 0 and y >= 8:
                        pe.wait_ge(s("sc_taken"), y // 4 - 1)
                    for a in range(PAIRS):
                        for j in range(4):
                            last = mm(ps[32 * j:32 * j + 32, 4 + y // 4 % 2, P * (page % 4):P * (page % 4) + P], q_row[:, a, 4 * g + j, :],
                                      kpage[:, (4 * y + j) % 8, P * a:P * a + P], a == 0, a == PAIRS - 1, skip_group_check=True)
                    last.then_inc(s("page_sc"), 1)
                if quad == WEIGHTS_AT:
                    weights_turned(0)
            attend(0)
            weights_turned(1)
            selected(0)
            attend(1)
            selected(1)
            pe.wait_ge(s("oa_taken"), 2)
            product(0, lambda k: wgk[:, k, :], lambda k: hT[:, k, :], KD, RANK).then_inc(*done("gk_ps"))
            pe.wait_ge(*after("gk_ready"))
            for h in range(GH):
                a_blk, b_blk = GLA[h]
                if h:
                    pe.wait_ge(s("og_T"), 5 * h)
                for i, (t0, T) in enumerate(TILES):
                    out = ps[0:T, i // 4, P * (i % 4):P * (i % 4) + P]
                    last = mm(out, gkT[:, t0:t0 + T], gk2[:, P * h:P * h + P], True, True)
                last.then_inc(s("la_ps"), 1)
                landed(pe, a_blk)
                wq = grid(slot(a_blk)[:, 0:KD * P], KD)
                wk = grid(slot(a_blk)[:, KD * P:2 * KD * P], KD)
                wv = grid(slot(a_blk)[:, 2 * KD * P:], KD)
                if h:
                    pe.wait_ge(s("state_s_new"), DEC_B * h)
                product(2, lambda k: wq[:, k, :], lambda k: hT[:, k, :], KD)
                product(3, lambda k: wk[:, k, :], lambda k: hT[:, k, :], KD).then_inc(s("qk_ps"), 1)
                pe.wait_ge(s("la_ready"), h + 1)
                for i in range(PT):
                    mm(ps[:, 2, P * i:P * i + P], la[:, P * i:P * i + P], const("chunk_causal"), True, True)
                mm(ps[:, 3, 0:NS], la[0:NS, 4 * P:5 * P], const("seq_causal"), True, True).then_inc(s("cum_ps"), 1)
                for i, (t0, T) in enumerate(TILES):
                    if i == 4:
                        pe.wait_ge(s("end_ready"), h + 1)
                        pe.wait_ge(s("e_ready"), h + 1)
                    for k in range(KD):
                        last = mm(ps[0:T, i // 2, GDV * (i % 2):GDV * (i % 2) + GDV], hT[:, k, t0:t0 + T], wv[:, k, :], k == 0, k == KD - 1)
                    if i % 2 or i == PT:
                        last.then_inc(s("v_ps"), 1)
                landed(pe, b_blk)
                wo = grid(slot(b_blk)[:, 0:KD * GDV], KD)
                pe.wait_ge(s("qkt_ready"), h + 1)
                for i, (t0, T) in enumerate(TILES):
                    for k in range(KD):
                        last = mm(ps[0:T, 4 + i // 2, GDV * (i % 2):GDV * (i % 2) + GDV], hT[:, k, t0:t0 + T], wo[:, k, :], k == 0, k == KD - 1)
                    if i % 2 or i == PT:
                        last.then_inc(s("og_ps"), 1)
                for i in range(PT):
                    turn(ps[:, 3, P * i:P * i + P], e_end[:, P * i:P * i + P])
                turn(ps[0:NS, 7, 0:P], e_end[:, sample]).then_inc(s("kend_tr"), 1)
                pe.wait_ge(s("kend_ready"), h + 1)
                pe.wait_ge(s("vg_ready"), 5 * h + 5)
                pe.wait_ge(s("og_raw"), 5 * h + 5)
                if h == 0:
                    pe.wait_ge(*after("att_set"))

                def turned(i, T):
                    n = 5 * h + i
                    pe.wait_ge(s("on_ready"), n + 1)
                    if n:
                        pe.wait_ge(s("og_T"), n)
                    for a in range(2):
                        last = turn(ps[:, 3, T * a:T * a + T], on_[0:T, n % 2, P * a:P * a + P])
                    last.then_inc(s("on_tr"), 1)

                for i in range(PT):
                    t0 = P * i
                    mm(ps[:, 2, P * (i % 2):P * (i % 2) + P], e_neg[:, t0:t0 + P], e_cum[:, t0:t0 + P], True, True).then_inc(s("att_ps"), 1)
                    for c in range(CPT):
                        n = NCH * h + CPT * i + c
                        if n >= 4:
                            pe.wait_ge(s("state_new"), n - 3)
                        r = slice(CHUNK * c, CHUNK * c + CHUNK)
                        mm(ps[:, 4 + c, 0:GDV], kend[r, i, :], v_g[r, i, :], True, True).then_inc(s("u_ps"), 1)
                    pe.wait_ge(s("att_ready"), 5 * h + i + 1)
                    if i >= 2:
                        pe.wait_ge(s("on_ready"), 5 * h + i - 1)
                    last = mm(ps[:, i % 2, 0:GDV], att[:, i % 2, :], v_g[:, i, :], True, False, skip_group_check=True)
                    for c in range(CPT):
                        n = CPT * i + c
                        if n == 0:
                            continue
                        pe.wait_ge(s("state_new"), NCH * h + n)
                        r = slice(CHUNK * c, CHUNK * c + CHUNK)
                        last = mm(ps[r, i % 2, 0:GDV], e_cum[:, t0 + CHUNK * c:t0 + CHUNK * c + CHUNK], state[:, n % 2, :], False, c == CPT - 1,
                                  skip_group_check=True)
                        last.then_inc(s("inter"), 1)
                    if i:
                        turned(i - 1, P)
                mm(ps[0:NS, 2, 0:NS], e_neg[:, sample], e_cum[:, sample], True, True).then_inc(s("att_ps"), 1)
                turned(3, P)
                pe.wait_ge(s("att_ready"), 5 * h + 5)
                pe.wait_ge(s("q_mask"), h + 1)
                pe.wait_ge(s("state_s_in"), 16 * h + 16)
                mm(ps[0:NS, 0, 0:GDV], cmp8[0:NS, 0, 0:NS], v_g[0:NS, 4, :], True, False)
                for b in range(DEC_B):
                    last = mm(ps[0:NS, 0, 0:GDV], q_mask[:, NS * b:NS * b + NS], state_s[:, b, :], False, b == DEC_B - 1)
                last.then_inc(s("o_ps"), 1)
                pe.wait_ge(s("kend_m"), h + 1)
                pe.wait_ge(s("state_new"), NCH * h + NCH)
                for b in range(DEC_B):
                    if b >= 4:
                        pe.wait_ge(s("state_s_new"), DEC_B * h + b - 3)
                    mm(ps[:, 4 + b % 4, 0:GDV], kend_m[:, b, :], v_g[0:NS, 4, :], True, True).then_inc(s("us_ps"), 1)
                turned(4, NS)
            pe.wait_ge(s("og_T"), 5 * GH)
            pe.wait_ge(s("state_s_new"), DEC_B * GH)
            for t in range(KD):
                n = MERGE[t]
                landed(pe, n)
                wga, wgb, wb = (grid(slot(n)[:, KD * P * a:KD * P * a + KD * P], KD) for a in range(3))
                wa = grid(slot(n)[:, 3 * KD * P:3 * KD * P + AW], AW // P)
                if t:
                    pe.wait_ge(s("ga_sig"), t)
                product(0, lambda k: wga[:, k, :], lambda k: hT[:, k, :], KD).then_inc(s("ga_ps"), 1)
                if t:
                    pe.wait_ge(s("gb_sig"), t)
                product(1, lambda k: wgb[:, k, :], lambda k: hT[:, k, :], KD).then_inc(s("gb_ps"), 1)
                if t:
                    pe.wait_ge(s("m_half"), t)
                product(2, lambda k: wa[:, k, :], lambda k: o_aT[:, k, :], AW // P).then_inc(s("pa_ps"), 1)
                if t:
                    pe.wait_ge(s("m_ready"), t)
                product(3, lambda k: wb[:, k, :], lambda k: o_gT[:, k, :], KD).then_inc(s("pb_ps"), 1)
            pe.wait_ge(s("merged"), KD)
            for t in range(KD):
                n = OUT[t // 4]
                landed(pe, n)
                w = grid(slot(n), KD)
                if t >= 3:
                    pe.wait_ge(s("x1T"), t - 2)
                product(t % 3, lambda k: w[:, k, P * (t % 4):P * (t % 4) + P], lambda k: mergedT[:, k, :], KD).then_inc(s("out_ps"), 1)
            for k in range(KD):
                pe.wait_ge(s("sq_ready"), KD + k + 1)
                for half in range(2):
                    last = mm(ps[:, 6 + half, 0:HALF], ones, sq2[:, k % 2, HALF * half:HALF * half + HALF], k == 0, k == KD - 1)
                last.then_inc(s("sq_used"), 1)
            for i, (t0, T) in enumerate(TILES):
                if i:
                    pe.wait_ge(s("x1_tok"), i)
                for k in range(KD):
                    last = turn(ps[0:T, 2 + k // 4, P * (k % 4):P * (k % 4) + P], xT[:, k, t0:t0 + T])
                last.then_inc(s("x1_tr"), 1)
            pe.wait_ge(s("h2_ready"), KD)
            pe.wait_ge(*after("h2_sample"))
            for i, (t0, T) in enumerate(TILES):
                if i:
                    pe.wait_ge(s("h2_tok"), i)
                for k in range(KD):
                    last = turn(ps[0:T, k // 4, P * (k % 4):P * (k % 4) + P], hT[:, k, t0:t0 + T])
                last.then_inc(s("h2_tr"), 1)
            pe.wait_ge(s("router_in"), 64)
            for i, (t0, T) in enumerate(TILES):
                out = ps[0:T, 6, 36 * i:36 * i + 36]
                for k in range(KD):
                    mm(out, hT[:, k, t0:t0 + T], wr[:, k, :], k == 0, False)
                last = mm(out, ones[0:1, 0:T], brow[:, :], False, True)
            last.then_inc(*done("lg_ps"))
            pe.wait_ge(*after("chosen"))
            for i in range(6):
                out = ps[:, 7, NE * i:NE * i + NE]
                top = min(i, 4)
                for j in range(top + 1):
                    last = mm(out, const("before") if j == i else ones, both[:, j, :], j == 0, j == top)
            last.then_inc(*done("pos_ps"))
            pe.wait_ge(*after("g_exp2"))
            for t in range(KD):
                turn(ps[:, 4 + t // 4, P * (t % 4):P * (t % 4) + P], g_exp[:, t, 0:P])
            pe.wait_ge(*after("more_ready"))
            for t in range(KD):
                last = turn(ps[0:NS, 6 + t // 4, P * (t % 4):P * (t % 4) + P], g_exp[:, t, P:])
            last.then_inc(*done("g_tr"))
            pe.wait_ge(*after("g_rows"))
            pe.wait_ge(s("h2_tok"), 5)
            pe.wait_ge(s("x1_tok"), 5)

            def step(e, it, par, before):
                pe.wait_ge(s(f"xs_in{par}"), it * 16 + 16)
                rows = xs[par].rearrange("r (p k) -> r k p", k=KD)
                mm(ps[:, par, 0:CAP], rows[:, 0, :], ident[0:CAP, 0:CAP], True, True)
                for j in range(1, KD):
                    last = turn(ps[:, par, CAP * j:CAP * j + CAP], rows[:, j, :])
                last.then_inc(s("xs_tr"), 1)
                if before:
                    down(e - 1, before[0], 1 - par)
                pe.wait_ge(s("xsT"), e + 1)
                for m in range(2):
                    q = (N0 + 3 * par + m) % RING
                    pe.wait_ge(slot_sem[q], it * 16 + (EXP_COUNT[q] + 16))
                    w = ring[:, q, :].rearrange("p (k c j) -> p k j c", k=KD, j=4)
                    for f in range(4):
                        for k in range(KD):
                            last = mm(ps[:, 2 + par, 256 * m + CAP * f:256 * m + CAP * f + CAP], w[:, k, f, :], xsT[par][:, CAP * k:CAP * k + CAP],
                                      k == 0, k == KD - 1)
                    last.then_inc(w_used, 1)

            def down(e, it, par):
                q = (N0 + 3 * par + 2) % RING
                pe.wait_ge(slot_sem[q], it * 16 + (EXP_COUNT[q] + 16))
                pe.wait_ge(s("hid"), e + 1)
                w = grid(ring[:, q, :], 4)
                for f in range(4):
                    for half in range(2):
                        last = mm(ps[CAP * half:CAP * half + CAP, 4 + par, :], hid[par][:, CAP * f:CAP * f + CAP],
                                  w[:, f, 512 * half:512 * half + 512], f == 0, f == 3, skip_group_check=True)
                last.then_inc(w_used, 1)

            step(0, 0, 0, None)
            with pe.Fori(0, NE // 2 - 1) as i:
                step(2 * i + 1, i, 1, (i,))
                step(2 * i + 2, i + 1, 0, (i,))
            step(NE - 1, NE // 2 - 1, 1, (NE // 2 - 1,))
            down(NE - 1, NE // 2 - 1, 1)

            def more(c):
                step(c + NE, c + NE // 2, 0, None)
                down(c + NE, c + NE // 2, 0)

            further_blocks(pe, more)


_INS = ['x_prompt', 'x_sample', 'c_prompt', 'c_sample', 'cache_k', 'cache_v', 'state_gla', 'page_table',
        'rel_bias', 'norm1_g', 'norm2_g', 'w_ada', 'b_ada', 'w_in', 'w_gk2', 'b_gk', 'q_norm_g', 'k_norm_g', 'o_norm_g',
        'w_branch_a', 'w_branch_b', 'w_out', 'w_router_group', 'b_router_group', 'w_router_expert',
        'b_router_expert', 'w_exp_gate', 'w_exp_up', 'w_exp_down']
_OUTS = [(1, SEQ, D), (DEC_B, DEC_T, D), (1, 1, SEQ, AH, AD), (1, 1, SEQ, AH, AD), (1, 1, GH, GDK, GDV),
         (1, DEC_B, DEC_T, AH, AD), (1, DEC_B, DEC_T, AH, AD), (1, DEC_B, GH, GDK, GDV)]


def kernel(**inputs):
    import concourse.bacc as bacc
    from concourse.bass_utils import run_bass_kernel_spmd

    nc = bacc.Bacc("TRN2", target_bir_lowering=False, num_devices=1)
    arrays, args = {}, []
    for name in _INS + ["shape_table"]:
        a = np.ascontiguousarray(CONST_TABLE if name == "shape_table" else inputs[name])
        arrays["in_" + name] = a
        args.append(nc.dram_tensor("in_" + name, a.shape, mybir.dt.from_np(a.dtype), kind="ExternalInput").ap())
    for i, shape in enumerate(_OUTS):
        args.append(nc.dram_tensor(f"out_{i}", shape, F32, kind="ExternalOutput").ap())
    layer_kernel(nc, *args)
    r = run_bass_kernel_spmd(nc, [arrays], core_ids=[0])
    return tuple(r.results[0][f"out_{i}"] for i in range(len(_OUTS)))
```

```python
from contextlib import ExitStack

import numpy as np
import concourse.bass as bass
from concourse import mybir

ALU = mybir.AluOpType
ACT = mybir.ActivationFunctionType
F32 = mybir.dt.float32
I32 = mybir.dt.int32
U32 = mybir.dt.uint32
AX = mybir.AxisListType

P = 128
D = 1024
KD = D // P
SEQ, DEC_B, DEC_T = 512, 8, 4
NS = DEC_B * DEC_T
NT = SEQ + NS
PT = SEQ // P
TILES = [(t * P, P) for t in range(PT)] + [(SEQ, NS)]
HALF = NT // 2
PAST, PAGE = 2048, 128
PAGES = PAST // PAGE
AH, AD = 8, 64
AW = AH * AD
PAIRS = AH // 2
BLK = 256
NBLK = PAST // BLK
TOPK = 3
BUCKETS, MAXDIST = 32, 128
GH, GDK, GDV = 4, 128, 256
RANK = 16
GNORM = 16.0
CHUNK = 32
NCH = SEQ // CHUNK
CPT = P // CHUNK
NG, EPG, NE = 4, 8, 32
CAP = 64
MORE = 2 * NT // CAP - 1
EB = NE + MORE
EDGES = -(-NT // CAP) - 1
EPS = 1e-6
NEG = -1e30
OFF = dict(qa=0, ka=AW, va=2 * AW, qg=3 * AW, kg=3 * AW + 512, vg=3 * AW + 1024, og=3 * AW + 2048,
           gk=3 * AW + 3072, ga=3 * AW + 3088, gb=3 * AW + 4112)
RING = 6
UNIT = KD * 512
TAB = 384
WORK = 16550
RBM = 255


def shape_constants():
    c = {}
    i = np.arange(P)
    c["ident"] = np.eye(P)
    c["ones"] = np.ones((P, P))
    c["before"] = (i[:, None] < i[None, :])
    c["chunk_causal"] = (i[:, None] <= i[None, :]) & (i[:, None] // CHUNK == i[None, :] // CHUNK)
    s = i[:NS]
    c["seq_causal"] = (s[:, None] <= s[None, :]) & (s[:, None] // DEC_T == s[None, :] // DEC_T)
    c["seq_member"] = (s[:, None] // DEC_T == np.arange(DEC_B)[None, :])
    dist = RBM - np.arange(TAB)
    n = np.maximum(dist, 0)
    exact = BUCKETS // 2
    nf = np.maximum(n, 1).astype(np.float32)
    large = exact + (np.log(nf / np.float32(exact)) / np.float32(np.log(MAXDIST / exact))
                     * np.float32(BUCKETS - exact)).astype(np.int32)
    bucket = np.where(n < exact, n, np.minimum(large, BUCKETS - 1))
    hot = np.zeros((BUCKETS + 1, TAB))
    hot[bucket, np.arange(TAB)] = 1
    hot[:, dist < 0] = 0
    hot[BUCKETS, dist < 0] = 1
    c["lower_index"] = np.broadcast_to((np.arange(8)[None, :] < np.arange(8)[:, None]).reshape(1, 64), (P, 64))
    c["lower_index4"] = np.broadcast_to((np.arange(4)[None, :] < np.arange(4)[:, None]).reshape(1, 16), (P, 16))
    tok = i[:, None] + P * np.arange(PT + 1)[None, :]
    c["token_real"] = tok < NT
    c["token_id"] = np.where(tok < NT, tok, 0)
    c["count"] = np.broadcast_to(np.arange(CAP)[None, :], (P, CAP))
    c["block_edge"] = np.broadcast_to(CAP * (1 + np.arange(EDGES))[None, :], (P, EDGES))
    c["row_head"] = i[:, None] % 32 // DEC_T == np.arange(AH)[None, :]
    c["row_token"] = (i[:, None] // 32 == np.arange(16)[None, :] // DEC_T) & (i[:, None] % DEC_T == np.arange(16)[None, :] % DEC_T)
    c["row_sequence"] = i[:, None] % 32 == np.arange(DEC_B + 1)[None, :]
    c["chunk_member"] = i[:, None] // CHUNK == np.arange(CPT)[None, :]
    c["minus_half"] = np.full((P, 8), -0.5)
    c["bucket_hot"] = hot
    at, cols = {}, 0
    for k, v in c.items():
        at[k] = (cols, v.shape[0], v.shape[1])
        cols += v.shape[1]
    table = np.zeros((P, cols), np.float32)
    for k, v in c.items():
        o, r, w = at[k]
        table[:r, o:o + w] = v
    return table, at


CONST_TABLE, CONST_AT = shape_constants()


def layer_kernel(nc, x_prompt, x_sample, c_prompt, c_sample, cache_k, cache_v, state_gla, page_table,
                 rel_bias, norm1_g, norm2_g, w_ada, b_ada, w_in, w_gk2, b_gk, q_norm_g, k_norm_g, o_norm_g,
                 w_branch_a, w_branch_b, w_out, w_router_group, b_router_group, w_router_expert,
                 b_router_expert, w_exp_gate, w_exp_up, w_exp_down, shape_table,
                 y_prompt, y_sample, k_prompt, v_prompt, state_prompt, k_sample, v_sample, state_sample):
    with ExitStack() as ctx:
        def sb(name, shape, dt=F32):
            return ctx.enter_context(nc.sbuf_tensor(name, shape, dt))

        def sem(name):
            return ctx.enter_context(nc.semaphore(name))

        bias_dram = nc.dram_tensor("bias_rows", [AH, P, TAB], F32, kind="Internal").ap()
        h2_dram = nc.dram_tensor("h2_rows", [NT, D], F32, kind="Internal").ap()
        y_dram = nc.dram_tensor("expert_rows", [CAP * EB, D], F32, kind="Internal").ap()

        KEPT = CONST_AT["bucket_hot"][0]
        cst = sb("cst", [P, KEPT])

        def const(name):
            o, r, w = CONST_AT[name]
            return cst[0:r, o:o + w]

        ident, ones = const("ident"), const("ones")
        ring = sb("ring", [P, RING, UNIT])
        xT = sb("xT", [P, KD, NT])
        hT = sb("hT", [P, KD, NT])
        work = sb("work", [P, WORK])
        vT = sb("vT", [P, 64])
        mod = sb("mod", [P, 6, KD, DEC_B + 1])
        gain = sb("gain", [P, 2, KD, DEC_B + 1])
        wgk = sb("wgk", [P, KD, RANK])
        gk2 = sb("gk2", [RANK + 1, 512])
        qkg = sb("qkg", [P, 2, AD])
        ong = sb("ong", [P, GDV])
        rbx = sb("rbx", [BUCKETS + 1, AH])
        rbfar = sb("rbfar", [P, AH])
        st = sb("stats", [P, 256])
        far_s = sb("far_s", [P, 1])
        ps = ctx.enter_context(nc.psum_tensor("ps", [P, 8, 512], F32))

        def carve(base, *sizes):
            out = []
            for n in sizes:
                out.append(work[:, base:base + n])
                base += n
            assert base <= WORK, base
            return out

        def grid(v, n):
            return v.rearrange("p (a b) -> p a b", a=n)

        o_aT = grid(work[:, 0:PAIRS * NT], PAIRS)
        o_gT = grid(work[:, 2176:2176 + KD * NT], KD)

        def wide(w, rows=P):
            return ps[0:rows, 2 * w:2 * w + 2, 0:HALF]

        def halves(v):
            return v.rearrange("p (a c) -> p a c", a=2)

        S = {}

        def s(name):
            if name not in S:
                S[name] = sem(name)
            return S[name]

        slot_sem = [sem(f"slot{i}_landed") for i in range(RING)]
        page_sem = [sem(f"pages{i}_landed") for i in range(RING)]
        w_used = sem("w_used")
        slot_count = [0] * RING
        stream = []

        def add_block(pieces, dmas, used):
            n = len(stream)
            slot_count[n % RING] += 16 * dmas
            stream.append((slot_count[n % RING], pieces, used))
            return n

        def slot(n):
            return ring[:, n % RING, :]

        def columns(w, lo, n, cols, at=0, k=KD):
            dst = slot(n)[:, at:at + k * cols].rearrange("p (k c) -> p k c", k=k)
            return dst, w.rearrange("(k p) c -> p k c", p=P)[:, :, lo:lo + cols]

        def block(used, *parts):
            n = len(stream)
            return add_block([columns(w, lo, n, cols, at, k) for w, lo, cols, at, k in parts], len(parts), used)

        ADA = [block((w_used, i + 1), (w_ada[0], 512 * i, 512, 0, KD)) for i in range(12)]
        QKV = [block((s("pj"), 5 * i + 5), (w_in[0], OFF[c], 512, 0, KD)) for i, c in enumerate(("qa", "ka", "va"))]
        PAGED = {}
        for what in ("k", "v"):
            for i in range(DEC_B * PAGES // 8):
                used = (s("page_tr"), 8 * i + 8) if what == "k" else (s("pv_s"), i + 1)
                PAGED[(what, i)] = add_block((what, i), PAGES // 4, used)
        GLA = []
        for h in range(GH):
            a = block((s("v_ps"), 3 * h + 3), (w_in[0], OFF["qg"] + GDK * h, GDK, 0, KD), (w_in[0], OFF["kg"] + GDK * h, GDK, KD * GDK, KD),
                      (w_in[0], OFF["vg"] + GDV * h, GDV, 2 * KD * GDK, KD))
            b = block((s("og_ps"), 3 * h + 3), (w_in[0], OFF["og"] + GDV * h, GDV, 0, KD))
            GLA.append((a, b))
        MERGE = [block((s("pb_ps"), t + 1), (w_in[0], OFF["ga"] + P * t, P, 0, KD), (w_in[0], OFF["gb"] + P * t, P, KD * P, KD),
                       (w_branch_b[0], P * t, P, 2 * KD * P, KD), (w_branch_a[0], P * t, P, 3 * KD * P, AW // P))
                 for t in range(KD)]
        OUT = [block((s("out_ps"), 4 * i + 4), (w_out[0], 512 * i, 512, 0, KD)) for i in range(2)]
        N0 = len(stream)
        EXP_USED = len(ADA)
        EXP_COUNT = [slot_count[i] for i in range(RING)]

        def landed(pe, n):
            pe.wait_ge(slot_sem[n % RING], stream[n][0])
            if isinstance(stream[n][1], tuple):
                paged = [m for m in PAGED.values() if m % RING == n % RING and m <= n]
                pe.wait_ge(page_sem[n % RING], 16 * PAGES // 4 * len(paged))

        ONCE = {
            "pe": ["c_tr", "own_ps", "gk_ps", "lgT_ps", "lg_ps", "g_tr", "pos_ps", "idx_ps"],
            "dve": ["rbx_set", "sample_set", "cT", "rbw_ready", "var_ready", "h_sample", "q_row", "att_set", "gk_ones",
                    "var2_ready", "h2_sample", "g_exp2", "lg_max", "chosen", "e_gap", "idx_hot", "idx_ready", "dest_ready", "more_ready"],
            "act": ["c_silu", "rstd_ready", "gk_ready", "rstd2_ready", "lgT", "lg_exp", "e_gap_exp", "g_rows", "rows_out"],
            "pool": ["zero_rows"],
        }
        once_sem = {e: sem(e + "_steps") for e in ONCE}

        def done(name):
            return next(once_sem[e] for e in ONCE if name in ONCE[e]), 1

        def after(name):
            return next((once_sem[e], ONCE[e].index(name) + 1) for e in ONCE if name in ONCE[e])

        KEY_PAGES = DEC_B * PAGES
        QUADS = KEY_PAGES // 4
        EXP_AT, WEIGHTS_AT = 22, 24

        class Chain:

            def __init__(self, name):
                self.sem, self.n = sem(name), 0

            def __call__(self, eng, ins):
                ins.then_inc(self.sem, 1)
                self.n += 1
                eng.wait_ge(self.sem, self.n)

        dve_chain, act_chain = Chain("dve_own"), Chain("act_own")

        x_tok, sq, var, rstd, rbw, crow, vrow, hot, mod_rows, cT = carve(
            2176, 5 * D, 2 * NT, NT, NT, AH * P, 2 * D, P, TAB, 2 * 512, KD * 32)
        crow, vrow, hot = grid(crow[0:DEC_B + 1], 2), vrow[0:64, :], hot[0:BUCKETS + 1, :]
        near_s, own_s, ptab = carve(16000, PAGE + DEC_T, 2 * NS, DEC_B * PAGES)
        own_s, ptab = grid(own_s, 2), ptab[0:1, :].bitcast(I32)
        x_tok, mod_rows = grid(x_tok, 5), grid(mod_rows, 2)
        cT = grid(cT, KD)
        sq = grid(sq, 2)
        bias_stage = grid(hT[:, :, :].rearrange("p k t -> p (k t)")[:, 0:AH * TAB], AH)
        rbw = rbw[0:BUCKETS + 1, :]

        qT, kT, v_tok, near, sc_p, pt_p, tok, tok_sq = carve(
            2176, PAIRS * NT, PAIRS * NT, 5 * AW, AH * 2 * P, 3 * 512, 2 * 512, 2 * AW, AW)
        qT, kT, v_tok = grid(qT, PAIRS), grid(kT, PAIRS), grid(v_tok, 5)
        near, sc_p, pt_p, tok = grid(near, AH), grid(sc_p, 3), grid(pt_p, 2), grid(tok, 2)
        after_v = 2176 + 2 * PAIRS * NT + 5 * AW
        kpage, = carve(2176, 8 * AW)
        q_row, = carve(2176 + 2 * PAIRS * NT, PAIRS * DEC_B * 32)
        prT, logit0, logit1 = carve(after_v, (PAGES + 1) * P, PAST + NS, PAST + NS)
        o_rows = grid(kpage[:, 0:2 * AW], 2)
        prT, logits, kpage = grid(prT, PAGES + 1), [logit0, logit1], grid(kpage, 8)
        q_row = q_row.rearrange("p (a b c) -> p a b c", a=PAIRS, b=DEC_B)
        cmp8 = sb("cmp8", [P, 2, 5 * NE])
        junk = cmp8[:, :, :].rearrange("p a b -> p (a b)")[:, 64:64 + GDV]

        (e_cum, e_neg, e_end, v_g, og, la, kend, state, att, state_s, q_mask, on_, gkT) = carve(
            2176 + KD * NT, NT, NT, NT, 5 * GDV, 5 * GDV, 8 * P, 5 * P, 2 * GDV, 2 * P, DEC_B * GDV, 288, 2 * GDV, NT)
        v_g, og, kend, state, att = grid(v_g, 5), grid(og, 5), grid(kend, 5), grid(state, 2), grid(att, 2)
        state_s, on_ = grid(state_s, DEC_B), grid(on_, 2)
        states = [state[:, 0, :], state[:, 1, :], e_end[:, 0:GDV], e_end[:, GDV:2 * GDV]]
        kend_m = grid(la, DEC_B)[0:NS]
        kend_c = la.rearrange("p (i c d) -> p i c d", i=2, c=CPT)
        gkT = gkT[0:RANK + 1, :]

        mergedT, m_a, m_b = carve(2176 + KD * NT, KD * NT, 2 * NT, 2 * NT)
        mergedT, m_a, m_b = grid(mergedT, KD), grid(m_a, 2), grid(m_b, 2)
        sq2, var2, rstd2 = carve(2176, 2 * NT, NT, NT)
        sq2 = grid(sq2, 2)

        h2_tok, x1_tok, g2p, g2s, g_exp = carve(0, 5 * D, 5 * D, D, D, KD * (P + NS))
        wr, lg, one1, one2, both = carve(13600, KD * (NG + NE), 5 * (NG + NE), 5 * NE, 5 * NE, 5 * NE)
        wr, lg = grid(wr, KD), grid(lg, 5)
        less, more_than, row_hot, block_hot = carve(10 * D, 5 * 64, 5 * 64, 2 * 5 * CAP, 2 * 5 * EB)
        lgT = row_hot[0:NG + NE, 0:NT]
        one1, one2, both = grid(one1, 5), grid(one2, 5), grid(both, 5)
        run = grid(less[:, 0:5 * NE], 5)
        h2_tok, x1_tok, g_exp = grid(h2_tok, 5), grid(x1_tok, 5), grid(g_exp, KD)
        g2s = g2s[0:NS, :]
        hflat = hT[:, :, :].rearrange("p a b -> p (a b)")
        xflat = xT[:, :, :].rearrange("p a b -> p (a b)")
        ya = [h2_tok[:, i, :] for i in range(5)]
        yb = [xflat[:, D * (i + 1):D * (i + 2)] for i in range(3)] + carve(12288, D, D)
        xs = [hflat[0:CAP, D * i:D * i + D] for i in range(2)]
        xsT = [hflat[:, 2 * D + 512 * i:2 * D + 512 * i + 512] for i in range(2)]
        hid = [hflat[:, 3 * D + 256 * (i + 1):3 * D + 256 * (i + 2)] for i in range(2)]
        ye = [xflat[:, 512 * i:512 * i + 512] for i in range(2)]

        blk_cmp, zero_rows = carve(14600, NE * MORE, D)
        zero_rows = zero_rows[0:CAP, :]
        wts = sb("wts", [P, 2, 5])
        dest = sb("dest", [P, 2, 5])
        dest_i = sb("dest_i", [P, 2, 5], I32)
        row_i = sb("row_i", [P, 2, 5], I32)
        blk_i = sb("blk_i", [P, 2, 5], I32)
        place = sb("place", [P, 2, 2, 5])
        rbias = sb("rbias", [NG + NE, 1])
        cnt = sb("cnt", [P, NE])
        base = sb("base", [P, NE])
        more_i = sb("more_i", [1, MORE + 1], I32)
        idx = sb("idx", [CAP, EB], I32)

        idx_cur = sb("idx_cur", [CAP, 1], I32)

        def bc(v, shape):
            return v.broadcast_to(shape)

        def further_blocks(eng, body):
            eng.wait_ge(*after("more_ready"))
            count = eng.value_load(more_i[0:1, MORE:MORE + 1], min_val=0, max_val=MORE)
            with eng.If(count > 0):
                with eng.Fori(0, MORE) as c:
                    with eng.If(count > c):
                        body(c)
            return count

        sample = slice(SEQ, NT)
        own_lower8, own_lower4 = const("lower_index"), const("lower_index4")
        blk = ctx.enter_context(nc.Block())

        def load_pages(eng, n, pieces, which, sems):
            what, i = pieces
            cache = cache_k if what == "k" else cache_v
            for q in which:
                pg = 8 * i + q
                at = (4 * (pg // (4 * PAGES)) + pg % 4) * PAGES + pg // 4 % PAGES
                page = eng.value_load(ptab[0:1, at:at + 1], min_val=0, max_val=cache.shape[1] - 1)
                src = cache[0, bass.DynSlice(page, 1)].rearrange("a t h d -> (a t) (h d)")
                eng.dma_start(slot(n)[:, AW * q:AW * q + AW], src).then_inc(sems[n % RING], 16)

        @blk.sync
        def _(sp):
            sp.wait_ge(s("small_in"), 16 * 10)
            for n, (_, pieces, _) in enumerate(stream):
                if n >= RING:
                    sp.wait_ge(*stream[n - RING][2])
                if isinstance(pieces, tuple):
                    sp.wait_ge(s("page_table_in"), 16)
                    load_pages(sp, n, pieces, range(0, 8, 2), slot_sem)
                else:
                    for dst, src in pieces:
                        sp.dma_start(dst, src).then_inc(slot_sem[n % RING], 16)

            def expert_blocks(e, par, before, expert=None):
                for m, w in enumerate((w_exp_gate, w_exp_up, w_exp_down)):
                    at = 3 * par + m
                    sp.wait_ge(*(stream[N0 + at - RING][2] if before is None else (w_used, before * 3 + (EXP_USED + m + 1))))
                    src = w[0, bass.DynSlice(e if expert is None else expert, 1)].rearrange("a (p k) c -> p (a k c)", k=w.shape[2] // P)
                    sp.dma_start(slot(N0 + at), src).then_inc(slot_sem[(N0 + at) % RING], 16)

            for par in range(2):
                expert_blocks(par, par, None)
            with sp.Fori(1, NE // 2) as i:
                for par in range(2):
                    expert_blocks(2 * i + par, par, 2 * i + (par - 2))

            def more(c):
                expert = sp.value_load(more_i[0:1, bass.DynSlice(c, 1)], min_val=0, max_val=NE - 1)
                expert_blocks(c + NE, 0, c + (NE - 1), expert)

            further_blocks(sp, more)

        @blk.gpsimd
        def _(pool):
            minus_half = const("minus_half")
            pool.wait_ge(s("bias_copied"), AH)
            pool.dma_start(bias_dram.rearrange("h p c -> p h c"), bias_stage).then_inc(s("bias_out"), 16)
            pool.wait_ge(s("bias_out"), 16)
            for j in range(4):
                src = bass.AP(tensor=bias_dram.tensor, offset=P - 1, ap=[[P * TAB, AH], [TAB - 1, DEC_T], [1, PAGE + DEC_T]])
                pool.dma_start(near_s[32 * j:32 * j + 32, :], src).then_inc(s("near_s_in"), 16)
                src = bass.AP(tensor=bias_dram.tensor, offset=0, ap=[[P * TAB, AH], [TAB, DEC_T], [1, 1]])
                pool.dma_start(far_s[32 * j:32 * j + 32, :], src, allow_slow_non_contiguous=True).then_inc(s("near_s_in"), 16)
            pool.wait_ge(s("const_in"), 16)
            pool.wait_ge(s("h_ready"), KD)
            src = bass.AP(tensor=bias_dram.tensor, offset=P - 1, ap=[[TAB - 1, P], [P * TAB, AH], [1, 2 * P]])
            pool.dma_start(near, src).then_inc(s("near_in"), 16)
            for m in range(11):
                if m < 10:
                    pool.wait_ge(s("qk_var"), m + 1)
                    T = TILES[m % 5][1]
                    v8 = st[0:T, 16 * (m % 2):16 * (m % 2) + 8]
                    pool.tensor_tensor(st[0:T, 16 * (m % 2) + 8:16 * (m % 2) + 16], v8, minus_half[0:T, 0:8],
                                       ALU.pow).then_inc(s("qk_rstd"), 1)
                if m - 1 >= 5:
                    i = m - 6
                    pool.wait_ge(s("qk_tok"), m)
                    dst = (k_prompt[0, 0, P * i:P * i + P] if i < PT else k_sample[0].rearrange("b t h d -> (b t) h d"))
                    T = TILES[i][1]
                    pool.dma_start(dst.rearrange("t h d -> t (h d)"), tok[0:T, (m - 1) % 2, :]).then_inc(s(f"k_out{(m - 1) % 2}"), 16)
            pool.wait_ge(s("v_ready"), 5)
            pool.dma_start(v_prompt[0, 0].rearrange("(i p) h d -> p i (h d)", p=P), v_tok[:, 0:PT, :]).then_inc(s("v_out"), 16)
            pool.dma_start(v_sample[0].rearrange("b t h d -> (b t) (h d)"), v_tok[0:NS, PT, :]).then_inc(s("v_out"), 16)
            pool.wait_ge(s("k_out0"), 16 * 2)
            pool.wait_ge(s("k_out1"), 16 * 3)
            pool.wait_ge(s("v_out"), 32)
            pool.wait_ge(s("page_table_in"), 16)
            for what in ("k", "v"):
                for i in range(KEY_PAGES // 8):
                    n = PAGED[(what, i)]
                    pool.wait_ge(*stream[n - RING][2])
                    load_pages(pool, n, (what, i), range(1, 8, 2), page_sem)
            for h in range(GH):
                if h:
                    pool.wait_ge(s("state_s_out"), 16 * h)
                else:
                    pool.wait_ge(s("oa_taken"), 2)
                pool.dma_start(state_s, state_gla[0, :, h].rearrange("b k v -> k b v")).then_inc(s("state_s_in"), 16)
                for i, (_, T) in enumerate(TILES):
                    n = 5 * h + i
                    pool.wait_ge(s("og_raw"), n + 1)
                    pool.tensor_tensor(og[0:T, i, :], og[0:T, i, :], ong[0:T, :], ALU.mult).then_inc(s("og_ready"), 1)
                for i, (_, T) in enumerate(TILES):
                    n = 5 * h + i
                    pool.wait_ge(s("o_var"), n + 1)
                    c = 64 + 2 * (n % 2)
                    pool.tensor_tensor(st[0:T, c + 1:c + 2], st[0:T, c:c + 1], minus_half[0:T, 0:1], ALU.pow).then_inc(s("o_rstd"), 1)
                    if i == 3:
                        pool.wait_ge(s("state_new"), NCH * (h + 1))
                        pool.dma_start(state_prompt[0, 0, h], states[NCH % 4]).then_inc(s("state_p_out"), 16)
                pool.wait_ge(s("state_s_new"), DEC_B * (h + 1))
                pool.dma_start(state_sample[0, :, h].rearrange("b k v -> k b v"), state_s).then_inc(s("state_s_out"), 16)
            pool.wait_ge(s("state_s_out"), 16 * GH)
            pool.wait_ge(s("state_p_out"), 16 * GH)
            for t in range(KD):
                pool.wait_ge(s("m_ready"), t + 1)
                pool.tensor_tensor(halves(mergedT[:, t, :]), halves(m_a[:, t % 2, :]), halves(m_b[:, t % 2, :]), ALU.add).then_inc(s("merged"), 1)
            pool.memset(zero_rows, 0.0).then_inc(*done("zero_rows"))
            pool.wait_ge(*after("zero_rows"))
            dst = y_dram.rearrange("(r b) c -> r b c", b=EB)[:, NE:, :]
            pool.dma_start(dst, bc(zero_rows.unsqueeze(1), [CAP, MORE, D])).then_inc(s("y_cleared"), 16)
            pool.dma_start(wr[:, :, 0:NG], w_router_group[0].rearrange("(k p) c -> p k c", p=P)).then_inc(s("router_in"), 16)
            pool.dma_start(wr[:, :, NG:NG + NE], w_router_expert[0].rearrange("(k p) c -> p k c", p=P)).then_inc(s("router_in"), 16)
            for i, (t0, T) in enumerate(TILES):
                pool.wait_ge(s("tok_taken"), 5 + i + 1)
                pool.dma_start(h2_dram[t0:t0 + T, :], h2_tok[0:T, i, :]).then_inc(s("h2_out"), 16)
            pool.wait_ge(s("h2_out"), 80)
            pool.wait_ge(*after("lg_ps"))
            pool.wait_ge(*after("idx_ready"))
            for e in range(NE):
                if e >= 2:
                    pool.wait_ge(s("xs_tr"), e - 1)
                pool.indirect_dma_start(xs[e % 2], None, h2_dram[:, :],
                                        bass.IndirectOffsetOnAxis(ap=idx[:, e:e + 1], axis=0)).then_inc(s(f"xs_in{e % 2}"), 16)
            turns = pool.alloc_register("turns")
            pool.reg_mov(turns, 1)

            def more(c):
                pool.wait_ge(s("idx_cur"), turns)
                pool.reg_add(turns, turns, 1)
                pool.wait_ge(s("y_cleared"), 16)
                pool.indirect_dma_start(xs[0], None, h2_dram[:, :],
                                        bass.IndirectOffsetOnAxis(ap=idx_cur[:, 0:1], axis=0)).then_inc(s("xs_in0"), 16)

            further_blocks(pool, more)
            pool.wait_ge(s("y_cleared"), 16)
            pool.wait_ge(*after("rows_out"))
            pool.wait_ge(*after("dest_ready"))
            for i, (_, T) in enumerate(TILES):
                for c, v in ((0, ya), (1, yb)):
                    pool.indirect_dma_start(v[i][0:T, :], None, y_dram[:, :],
                                            bass.IndirectOffsetOnAxis(ap=dest_i[0:T, c, i:i + 1], axis=0)).then_inc(s(f"y{c}_in{i}"), 16)
            for i, (_, T) in enumerate(TILES):
                pool.wait_ge(s("y_gated"), i + 1)
                pool.tensor_tensor(ya[i][0:T, :], ya[i][0:T, :], x1_tok[0:T, i, :], ALU.add).then_inc(s("y_ready"), 1)

        @blk.scalar
        def _(act):
            act.dma_start(crow[0:1, 0, :], c_prompt).then_inc(s("c_in"), 16)
            act.dma_start(crow[1:DEC_B + 1, 0, :], c_sample).then_inc(s("c_in"), 16)
            act.dma_start(cst[:, :], shape_table[:, 0:KEPT]).then_inc(s("const_in"), 16)
            act.dma_start(vrow[0:48, :], b_ada[0].rearrange("(a p) -> a p", p=P)).then_inc(s("vec_in"), 16)
            act.dma_start(vrow[48:56, :], norm1_g[0].rearrange("(a p) -> a p", p=P)).then_inc(s("vec_in"), 16)
            act.dma_start(vrow[56:64, :], norm2_g[0].rearrange("(a p) -> a p", p=P)).then_inc(s("vec_in"), 16)
            act.dma_start(hot, shape_table[0:BUCKETS + 1, KEPT:]).then_inc(s("small_in"), 16)
            act.wait_ge(*after("rbx_set"))
            act.dma_start(rbx[0:BUCKETS, :], rel_bias).then_inc(s("small_in"), 16)
            act.dma_start(ptab[:, :], page_table.rearrange("(a b) n -> a (b n)", a=1)).then_inc(s("page_table_in"), 16)

            def rows(v, n):
                return bass.AP(tensor=v.tensor, offset=v.offset, ap=[[0, P], [1, n]])

            act.dma_start(qkg[:, 0, :], rows(q_norm_g, AD)).then_inc(s("small_in"), 16)
            act.dma_start(qkg[:, 1, :], rows(k_norm_g, AD)).then_inc(s("small_in"), 16)
            act.dma_start(ong[:, :], rows(o_norm_g, GDV)).then_inc(s("small_in"), 16)
            act.dma_start(wgk[:, :, :], w_in[0].rearrange("(k p) c -> p k c", p=P)[:, :, OFF["gk"]:OFF["gk"] + RANK]).then_inc(s("small_in"), 16)
            act.dma_start(gk2[0:RANK, :], w_gk2[0]).then_inc(s("small_in"), 16)
            act.dma_start(gk2[RANK:, :], b_gk).then_inc(s("small_in"), 16)
            act.dma_start(rbias[0:NG, :], b_router_group.rearrange("a g -> g a")).then_inc(s("small_in"), 16)
            act.dma_start(rbias[NG:, :], b_router_expert.rearrange("a g -> g a")).then_inc(s("small_in"), 16)
            act.dma_start(x_tok[:, 0:PT, :], x_prompt[0].rearrange("(i p) d -> p i d", p=P)).then_inc(s("x_in"), 16)
            act.dma_start(x_tok[0:NS, PT, :], x_sample.rearrange("b t d -> (b t) d")).then_inc(s("x_in"), 16)

            act.wait_ge(s("c_in"), 32)
            act.activation(crow[:, 1, :], crow[:, 0, :], ACT.Silu).then_inc(*done("c_silu"))
            for h in range(AH):
                act.wait_ge(s("bias_ps"), h + 1)
                act.activation(bias_stage[:, h, :], ps[:, 6 + h % 2, 0:TAB], ACT.Copy)
                act.activation(rbfar[:, h:h + 1], ps[:, 6 + h % 2, 0:1], ACT.Copy).then_inc(s("bias_copied"), 1)
            for k in range(KD):
                act.wait_ge(s("xT_ready"), k + 1)
                if k >= 2:
                    act.wait_ge(s("sq_used"), k - 1)
                act.activation(sq[:, k % 2, :], xT[:, k, :], ACT.Square).then_inc(s("sq_ready"), 1)
            act.wait_ge(*after("var_ready"))
            act.activation(rstd, var, ACT.Sqrt).then_inc(*done("rstd_ready"))

            def modulate(a, name):
                for k in range(KD):
                    act.wait_ge(s(name + "_scaled"), k + 1)
                    act.activation(hT[:, k, 0:SEQ], hT[:, k, 0:SEQ], ACT.Identity, bias=mod[:, 3 * a, k, 0:1],
                                   scale=gain[:, a, k, 0:1]).then_inc(s(name + "_ready"), 1)

            modulate(0, "h")
            for n in range(15):
                t0, T = TILES[n % 5]
                act.wait_ge(s("pj"), n + 1)
                if n == 0:
                    act.wait_ge(s("h_ready"), KD)
                if n < 10:
                    if n:
                        act.wait_ge(s("qk_var"), n)
                    act.activation(tok_sq[0:T, :], ps[0:T, n % 4, :], ACT.Square).then_inc(s("qk_sq"), 1)
                else:
                    act.activation(v_tok[0:T, n % 5, :], ps[0:T, n % 4, :], ACT.Copy).then_inc(s("v_ready"), 1)
            for x in range(34):
                if x < 32:
                    n = P * (x % 4 + 1)
                    c = 32 + 4 * (x % 2)
                    act.wait_ge(s("sc_max"), x + 1)
                    act.activation(sc_p[:, x % 3, 0:n], sc_p[:, x % 3, 0:n], ACT.Exp, bias=st[:, c:c + 1],
                                   accum_out=st[:, c + 1:c + 2]).then_inc(s("sc_exp"), 1)
                if x >= 2:
                    y = x - 2
                    act.wait_ge(s("p_tr"), y + 1)
                    if y >= 2:
                        act.wait_ge(s("p_pv"), y - 1)
                    act.activation(pt_p[:, y % 2, 0:P * (y % 4 + 1)], ps[:, 2 + y % 2, 0:P * (y % 4 + 1)], ACT.Copy).then_inc(s("p_T"), 1)
            def exponent(g):
                act.wait_ge(s("l_max"), g + 1)
                act.activation(logits[g], logits[g], ACT.Exp, bias=st[:, 48:49], accum_out=st[:, 49:50]).then_inc(s("l_exp"), 1)

            def weights(g):
                if g:
                    act.wait_ge(s("pv_s"), KEY_PAGES // 16)
                for q in range(5):
                    act.wait_ge(s("pr_tr"), 5 * g + q + 1)
                    if q < 4:
                        act.activation(prT[:, 4 * q:4 * q + 4, :], grid(ps[:, 6 + q % 2, :], 4), ACT.Copy).then_inc(s("pr_T"), 1)
                    else:
                        act.activation(prT[0:NS, PAGES, :], ps[0:NS, 3, 384:512], ACT.Copy).then_inc(s("pr_T"), 1)

            act.wait_ge(s("p_ov"), 32)
            act.wait_ge(s("p_pv"), 32)
            act.wait_ge(s("k_out0"), 16 * 2)
            act.wait_ge(s("k_out1"), 16 * 3)
            act.wait_ge(*after("own_ps"))
            for pg in range(KEY_PAGES):
                act.wait_ge(s("page_tr"), pg + 1)
                if pg >= 8:
                    act.wait_ge(s("page_sc"), pg // 4 - 1)
                act.activation(kpage[:, pg % 8, :], ps[:, pg % 3, :], ACT.Copy).then_inc(s("page_T"), 1)
                if pg == 4 * EXP_AT + 3:
                    exponent(0)
                if pg == 4 * WEIGHTS_AT + 3:
                    weights(0)
            exponent(1)
            weights(1)
            for g in range(2):
                act.wait_ge(s("o_sel"), g + 1)
                act.activation(o_aT[:, :, SEQ + 16 * g:SEQ + 16 * g + 16], grid(ps[:, 2, 64 * g:64 * g + 64], PAIRS), ACT.Copy)\
                   .then_inc(s("oa_taken"), 1)
            act.wait_ge(*after("gk_ps"))
            act.wait_ge(*after("gk_ones"))
            act.wait_ge(s("v_out"), 32)
            act.activation(halves(gkT[0:RANK, :]), wide(2, RANK), ACT.Copy).then_inc(*done("gk_ready"))
            for h in range(GH):
                act.wait_ge(s("la_min"), h + 1)
                parts = [(ps[:, 0, :], la[:, 0:512], kend.rearrange("p a b -> p (a b)")[:, 0:512]),
                         (ps[0:NS, 1, 0:P], la[0:NS, 512:640], kend.rearrange("p a b -> p (a b)")[0:NS, 512:640])]
                for a, b, c in parts:
                    act_chain(act, act.activation(c, a, ACT.Abs))
                    act_chain(act, act.activation(c, c, ACT.Exp, scale=-1.0))
                    last = act.activation(c, c, ACT.Ln, bias=1.0)
                last.then_inc(s("la_ln"), 1)
                act.wait_ge(s("cum_ps"), h + 1)
                for a, b in ((ps[:, 2, :], slice(0, SEQ)), (ps[:, 3, 0:NS], sample)):
                    act.activation(e_cum[:, b], a, ACT.Exp)
                    last = act.activation(e_neg[:, b], a, ACT.Exp, scale=-1.0)
                last.then_inc(s("e_ready"), 1)
                act.wait_ge(s("end_ready"), h + 1)
                act.activation(e_end, e_end, ACT.Exp).then_inc(s("e_end"), 1)
                for i, (_, T) in enumerate(TILES):
                    act.wait_ge(s("v_ps"), 3 * h + i // 2 + 1)
                    act.activation(v_g[0:T, i, :], ps[0:T, i // 2, GDV * (i % 2):GDV * (i % 2) + GDV], ACT.Copy).then_inc(s("vg_ready"), 1)
                for i, (_, T) in enumerate(TILES):
                    act.wait_ge(s("og_ps"), 3 * h + i // 2 + 1)
                    act.activation(og[0:T, i, :], ps[0:T, 4 + i // 2, GDV * (i % 2):GDV * (i % 2) + GDV], ACT.Silu).then_inc(s("og_raw"), 1)
                act.wait_ge(s("kend_tr"), h + 1)
                act.activation(kend[:, 0:4, :], grid(ps[:, 3, :], 4), ACT.Copy)
                act.activation(kend[0:NS, 4, :], ps[0:NS, 7, 0:P], ACT.Copy).then_inc(s("kend_ready"), 1)
                def squares(i):
                    T = TILES[i][1]
                    n = 5 * h + i
                    act.wait_ge(*((s("inter"), (NCH - 1) * h + CPT * i + CPT - 1) if i < PT else (s("o_ps"), h + 1)))
                    if n >= 1:
                        act.wait_ge(s("o_var"), n)
                    act.activation(junk[0:T, :], ps[0:T, i % 2, 0:GDV], ACT.Square,
                                   accum_out=st[0:T, 60:61]).then_inc(s("o_sq"), 1)

                squares(0)
                squares(1)
                for i, (t0, T) in enumerate(TILES):
                    if i + 2 <= PT:
                        squares(i + 2)
                    act.wait_ge(s("on_tr"), 5 * h + i + 1)
                    act.activation(o_gT[:, 2 * h:2 * h + 2, t0:t0 + T], grid(ps[:, 3, 0:2 * T], 2), ACT.Copy).then_inc(s("og_T"), 1)
            act.wait_ge(s("state_p_out"), 16 * GH)
            act.wait_ge(s("state_s_out"), 16 * GH)
            for t in range(KD):
                act.wait_ge(s("ga_ps"), t + 1)
                if t >= 2:
                    act.wait_ge(s("merged"), t - 1)
                act.activation(halves(m_a[:, t % 2, :]), wide(0), ACT.Sigmoid).then_inc(s("ga_sig"), 1)
                act.wait_ge(s("gb_ps"), t + 1)
                act.activation(halves(m_b[:, t % 2, :]), wide(1), ACT.Sigmoid).then_inc(s("gb_sig"), 1)
            for k in range(KD):
                act.wait_ge(s("x1T"), k + 1)
                if k == 0:
                    act.wait_ge(s("out_ps"), KD)
                if k >= 2:
                    act.wait_ge(s("sq_used"), KD + k - 1)
                act.activation(sq2[:, k % 2, :], xT[:, k, :], ACT.Square).then_inc(s("sq_ready"), 1)

            def to_tokens(n):
                T = TILES[n % 5][1]
                act.wait_ge(s("tok_tr"), n + 1)
                act.activation(grid((x1_tok, h2_tok)[n // 5][0:T, n % 5, :], 2), ps[0:T, 2 * (n % 3):2 * (n % 3) + 2, :], ACT.Copy)\
                   .then_inc(s("tok_taken"), 1)

            act.wait_ge(*after("var2_ready"))
            act.activation(rstd2, var2, ACT.Sqrt).then_inc(*done("rstd2_ready"))
            to_tokens(0)
            modulate(1, "h2")
            to_tokens(1)
            to_tokens(2)
            act.wait_ge(*after("lgT_ps"))
            act.activation(halves(lgT), wide(3, NG + NE), ACT.Identity, bias=rbias[:, 0:1]).then_inc(*done("lgT"))
            for n in range(3, 10):
                to_tokens(n)
            act.wait_ge(*after("lg_max"))
            act.activation(both[:, :, 0:NG], both[:, :, 0:NG], ACT.Exp).then_inc(*done("lg_exp"))
            act.wait_ge(*after("e_gap"))
            act.activation(st[:, 200:205], st[:, 200:205], ACT.Exp).then_inc(*done("e_gap_exp"))
            act.wait_ge(*after("g_tr"))
            act.wait_ge(*after("idx_ready"))
            act.activation(grid(g2p, 2), ps[:, 0:2, :], ACT.Copy)
            act.activation(grid(g2s, 2), ps[0:NS, 2:4, :], ACT.Copy).then_inc(*done("g_rows"))
            def act_down(e, par):
                act.wait_ge(s("ye_ready"), e + 1)
                dst = y_dram.rearrange("(r b) (h c) -> b h r c", b=EB, h=2)[bass.DynSlice(e, 1)].rearrange("a h r c -> (a h) r c")
                act.dma_start(dst, ye[par]).then_inc(s(f"ye_out{par}"), 16)

            def act_step(e, par, before):
                act.wait_ge(s("xs_tr"), e + 1)
                act.activation(xsT[par], ps[:, par, :], ACT.Copy).then_inc(s("xsT"), 1)
                if before:
                    act_down(e - 1, 1 - par)
                act.wait_ge(w_used, e * 3 + (EXP_USED + 2))
                act.activation(hid[par], ps[:, 2 + par, 0:256], ACT.Silu).then_inc(s("hid_gate"), 1)

            act_step(0, 0, False)
            with act.Fori(0, NE // 2 - 1) as i:
                act_step(2 * i + 1, 1, True)
                act_step(2 * i + 2, 0, True)
            act_step(NE - 1, 1, True)
            act_down(NE - 1, 1)

            def more(c):
                act_step(c + NE, 0, False)
                act_down(c + NE, 0)

            count = further_blocks(act, more)
            act.wait_ge(s("ye_out1"), 16 * (NE // 2))
            act.wait_ge(s("ye_out0"), count * 16 + 16 * (NE // 2))
            act.activation(st[0:1, 250:251], st[0:1, 200:201], ACT.Copy).then_inc(*done("rows_out"))
            for i, (t0, T) in enumerate(TILES):
                act.wait_ge(s(f"y0_in{i}"), 16)
                act.activation(ya[i][0:T, :], ya[i][0:T, :], ACT.Copy, scale=wts[0:T, 0, i:i + 1]).then_inc(s("ya_scaled"), 1)
            for i, (t0, T) in enumerate(TILES):
                act.wait_ge(s("y_ready"), i + 1)
                dst = y_prompt[0, t0:t0 + T, :] if i < PT else y_sample.rearrange("b t d -> (b t) d")
                act.dma_start(dst, ya[i][0:T, :]).then_inc(s("y_out"), 16)
            act.wait_ge(s("y_out"), 80)
        @blk.vector
        def _(dve):
            link = lambda ins: dve_chain(dve, ins)
            dve.memset(rbx[:, :], NEG).then_inc(*done("rbx_set"))
            dve.memset(own_s, NEG).then_inc(*done("sample_set"))
            dve.wait_ge(*after("sample_set"))
            link(dve.memset(cT.rearrange("p k c -> p (k c)"), 0.0))
            dve.wait_ge(*after("c_tr"))
            link(dve.tensor_copy(vT[:, :], ps[:, 5, 128:192]))
            dve.tensor_copy(cT[:, :, 0:DEC_B + 1], grid(ps[:, 5, 0:72], KD)).then_inc(*done("cT"))
            dve.wait_ge(s("small_in"), 16 * 10)
            dve.wait_ge(s("const_in"), 16)
            link(dve.tensor_scalar(qkg[:, 0, :], qkg[:, 0, :], AD ** -0.5, None, ALU.mult))
            dve.tensor_copy(rbw.rearrange("b (h p) -> b h p", h=AH), bc(rbx[:, :].unsqueeze(2), [BUCKETS + 1, AH, P])).then_inc(*done("rbw_ready"))
            for i in range(len(ADA)):
                k = i - AH // 2 - 1
                if k >= 0:
                    dve.wait_ge(s("x_tr"), k + 1)
                    w = k % 2
                    dve.tensor_copy(xT[:, k, 0:SEQ], ps[:, 2 * w, :])
                    dve.tensor_copy(xT[:, k, sample], ps[:, 2 * w + 1, 0:NS]).then_inc(s("xT_ready"), 1)
                dve.wait_ge(w_used, i + 1)
                if i >= 2:
                    dve.wait_ge(s("mod_tr"), i - 1)
                dve.tensor_copy(mod_rows[:, i % 2, :], ps[:, 5, :]).then_inc(s("mod_rows"), 1)
            dve.wait_ge(s("x_tr"), KD)
            dve.tensor_copy(xT[:, KD - 1, 0:SEQ], ps[:, 2, :])
            dve.tensor_copy(xT[:, KD - 1, sample], ps[:, 3, 0:NS]).then_inc(s("xT_ready"), 1)
            dve.wait_ge(s("sq_used"), KD)
            link(dve.tensor_scalar(halves(var), wide(3), 1.0 / D, EPS, ALU.mult, ALU.add))
            dve.reciprocal(var, var).then_inc(*done("var_ready"))
            dve.wait_ge(s("mod_tr"), len(ADA))
            flat_mod = mod[:, :, :, :].rearrange("p a k c -> p (a k) c")
            link(dve.tensor_tensor(flat_mod, grid(ps[:, 4, 0:432], 48), bc(vT[:, 0:48].unsqueeze(2), [P, 48, DEC_B + 1]), ALU.add))
            for a in range(2):
                last = dve.scalar_tensor_tensor(gain[:, a, :, :], mod[:, 3 * a + 1, :, :], 1.0,
                                                bc(vT[:, 48 + 8 * a:56 + 8 * a].unsqueeze(2), [P, KD, DEC_B + 1]), ALU.add, ALU.mult)
            link(last)

            def by_sequence(v):
                return v.rearrange("p (b t) -> p b t", t=DEC_T)

            def modulate(a, r, ready):
                for k in range(KD):
                    dve.tensor_tensor(hT[:, k, :], xT[:, k, :], r, ALU.mult).then_inc(s(ready + "_scaled"), 1)
                dve.wait_ge(s(ready + "_scaled"), KD)
                v = hT[:, :, sample].rearrange("p k (b t) -> p k b t", t=DEC_T)
                full = [P, KD, DEC_B, DEC_T]
                link(dve.tensor_tensor(v, v, bc(gain[:, a, :, 1:].unsqueeze(3), full), ALU.mult))
                dve.tensor_tensor(v, v, bc(mod[:, 3 * a, :, 1:].unsqueeze(3), full), ALU.add).then_inc(*done(ready + "_sample"))

            dve.wait_ge(*after("rstd_ready"))
            dve.wait_ge(s("bias_out"), 16)
            modulate(0, rstd, "h")
            dve.wait_ge(s("near_s_in"), 16 * 8)
            for g in range(2):
                for j in range(4):
                    q = slice(32 * j, 32 * j + 32)
                    b = DEC_T * (4 * g + j)
                    dve.tensor_copy(own_s[q, g, b:b + DEC_T], near_s[q, PAGE:PAGE + DEC_T])
            for m in range(11):
                if m < 10:
                    t0, T = TILES[m % 5]
                    c = 16 * (m % 2)
                    dve.wait_ge(s("qk_sq"), m + 1)
                    link(dve.tensor_reduce(st[0:T, c:c + 8], tok_sq[0:T, :].rearrange("p (h d) -> p h d", h=AH), AX.X, ALU.add))
                    dve.tensor_scalar(st[0:T, c:c + 8], st[0:T, c:c + 8], 1.0 / AD, EPS, ALU.mult, ALU.add).then_inc(s("qk_var"), 1)
                if m:
                    y = m - 1
                    t0, T = TILES[y % 5]
                    dve.wait_ge(s("qk_tr"), y + 1)
                    dst = (qT, kT)[y // 5]
                    dve.tensor_copy(dst[:, :, t0:t0 + T], grid(ps[:, 4 + y % 2, 0:4 * T], PAIRS)).then_inc(s("qk_T"), 1)
                if m < 10:
                    t0, T = TILES[m % 5]
                    c = 16 * (m % 2)
                    dve.wait_ge(s("qk_rstd"), m + 1)
                    if m >= 7:
                        dve.wait_ge(s(f"k_out{m % 2}"), 16 * ((m - 5) // 2))
                    v = tok[0:T, m % 2, :].rearrange("p (h d) -> p h d", h=AH)
                    dve.tensor_tensor(v, grid(ps[0:T, m % 4, :], AH), bc(st[0:T, c + 8:c + 16].unsqueeze(2), [T, AH, AD]),
                                      ALU.mult).then_inc(s("pj_free"), 1)
                    dve.wait_ge(s("pj_free"), m + 1)
                    dve.tensor_tensor(v, v, bc(qkg[0:T, m // 5, :].unsqueeze(1), [T, AH, AD]), ALU.mult).then_inc(s("qk_tok"), 1)
            dve.wait_ge(s("near_in"), 16)
            for x in range(32 + 4):
                if x < 32:
                    h, i = x // 4, x % 4
                    c = 32 + 4 * (x % 2)
                    n = P * (i + 1)
                    far = P * max(i - 1, 0)
                    dve.wait_ge(s("sc_ps"), x + 1)
                    if x >= 3:
                        dve.wait_ge(s("p_tr"), x - 2)
                    if far:
                        dve.tensor_scalar(sc_p[:, x % 3, 0:far], ps[:, x % 2, 0:far], rbfar[:, h:h + 1], None, ALU.add)
                    link(dve.tensor_tensor(sc_p[:, x % 3, far:n], ps[:, x % 2, far:n], near[:, h, 2 * P - (n - far):2 * P], ALU.add))
                    dve.tensor_reduce(st[:, c:c + 1], sc_p[:, x % 3, 0:n], AX.X, ALU.max, negate=True).then_inc(s("sc_max"), 1)
                if 1 <= x <= 32:
                    y = x - 1
                    c = 32 + 4 * (y % 2)
                    n = P * (y % 4 + 1)
                    dve.wait_ge(s("sc_exp"), y + 1)
                    link(dve.reciprocal(st[:, c + 2:c + 3], st[:, c + 1:c + 2]))
                    dve.tensor_scalar(sc_p[:, y % 3, 0:n], sc_p[:, y % 3, 0:n], st[:, c + 2:c + 3], None, ALU.mult).then_inc(s("p_norm"), 1)
                if x >= 4:
                    y = x - 4
                    h, i = y // 4, y % 4
                    rows = slice(64 * (h % 2), 64 * (h % 2) + 64)
                    dve.wait_ge(s("p_pv"), y + 1)
                    dve.tensor_copy(o_aT[rows, h // 2, P * i:P * i + P], ps[rows, 4 + y % 2, 0:P]).then_inc(s("p_ov"), 1)
            dve.wait_ge(s("k_out0"), 16 * 2)
            dve.wait_ge(s("k_out1"), 16 * 3)
            dve.wait_ge(s("v_out"), 32)
            link(dve.memset(q_row.rearrange("p a b c -> p (a b c)"), 0.0))
            for a in range(PAIRS):
                for odd in range(2):
                    rows = slice(64 * odd, 64 * odd + 64)
                    c = 8 * a + 4 * odd
                    last = dve.tensor_copy(q_row[rows, a, :, c:c + DEC_T], qT[rows, a, sample].rearrange("p (b t) -> p b t", t=DEC_T))
            last.then_inc(*done("q_row"))
            dve.wait_ge(*after("own_ps"))
            for g in range(2):
                dve.tensor_tensor(logits[g][:, PAST:], ps[:, 3, NS * g:NS * g + NS], own_s[:, g, :], ALU.add)

            def softmax(g):
                logit = logits[g]
                dve.wait_ge(s("sc_taken"), 4 * g + 4)
                gate, comb = st[:, 80:88], st[:, 88:96]
                link(dve.tensor_reduce(gate, grid(logit[:, 0:PAST], NBLK), AX.X, ALU.add))
                c0, c1 = grid(cmp8[:, 0, 0:64], 8), grid(cmp8[:, 1, 0:64], 8)
                gi, gj = bc(gate.unsqueeze(1), [P, 8, 8]), bc(gate.unsqueeze(2), [P, 8, 8])
                link(dve.tensor_tensor(c0, gi, gj, ALU.is_equal))
                link(dve.tensor_tensor(c0, c0, grid(own_lower8, 8), ALU.mult))
                link(dve.tensor_tensor(c1, gi, gj, ALU.is_gt))
                link(dve.tensor_tensor(c0, c0, c1, ALU.add))
                link(dve.tensor_reduce(comb, c0, AX.X, ALU.add))
                link(dve.tensor_scalar(comb, comb, float(TOPK), NEG, ALU.is_ge, ALU.mult))
                near_part = logit[:, PAST - PAGE:PAST]
                link(dve.scalar_tensor_tensor(near_part, near_part, comb[:, 7:8], near_s[:, 0:PAGE], ALU.add, ALU.add))
                link(dve.tensor_scalar(comb, comb, far_s[:, 0:1], None, ALU.add))
                v = grid(logit[:, 0:PAST - BLK], NBLK - 1)
                dve.tensor_tensor(v, v, bc(comb[:, 0:7].unsqueeze(2), [P, NBLK - 1, BLK]), ALU.add)
                v = logit[:, PAST - BLK:PAST - PAGE]
                link(dve.tensor_scalar(v, v, comb[:, 7:8], None, ALU.add))
                dve.tensor_reduce(st[:, 48:49], logit, AX.X, ALU.max, negate=True).then_inc(s("l_max"), 1)
                dve.wait_ge(s("l_exp"), g + 1)
                link(dve.reciprocal(st[:, 50:51], st[:, 49:50]))
                dve.tensor_scalar(logit, logit, st[:, 50:51], None, ALU.mult).then_inc(s("l_norm"), 1)

            for n in range(QUADS // 4):
                dve.wait_ge(s("page_sc"), 4 * n + 4)
                dve.tensor_copy(logits[n // 4][:, 512 * (n % 4):512 * (n % 4) + 512], ps[:, 4 + n % 2, :]).then_inc(s("sc_taken"), 1)
                if n % 4 == 3:
                    softmax(n // 4)
            for g in range(2):
                dve.wait_ge(s("pv_s"), KEY_PAGES // 16 * (g + 1))
                dve.tensor_tensor(o_rows[:, g, :].rearrange("p (h d) -> p h d", h=AH), grid(ps[:, g, :], AH),
                                  bc(const("row_head").unsqueeze(2), [P, AH, AD]), ALU.mult).then_inc(s("o_rows"), 1)
            dve.wait_ge(s("oa_taken"), 2)
            dve.wait_ge(s("v_out"), 32)
            dve.memset(att.rearrange("p a b -> p (a b)"), 0.0).then_inc(*done("att_set"))
            dve.memset(gkT, 1.0).then_inc(*done("gk_ones"))
            link(dve.memset(q_mask, 0.0))
            link(dve.memset(on_[0:NS, :, :], 0.0))
            for h in range(GH):
                dve.wait_ge(s("la_ps"), h + 1)
                parts = [(ps[:, 0, :], la[:, 0:512], kend.rearrange("p a b -> p (a b)")[:, 0:512]),
                         (ps[0:NS, 1, 0:P], la[0:NS, 512:640], kend.rearrange("p a b -> p (a b)")[0:NS, 512:640])]
                for a, b, c in parts:
                    last = dve.tensor_scalar(b, a, 0.0, None, ALU.min)
                last.then_inc(s("la_min"), 1)
                dve.wait_ge(s("la_min"), h + 1)
                dve.wait_ge(s("la_ln"), h + 1)
                for a, b, c in parts:
                    last = dve.tensor_tensor(b, b, c, ALU.subtract)
                link(last)
                for a, b, c in parts:
                    last = dve.tensor_scalar(b, b, 1.0 / GNORM, None, ALU.mult)
                last.then_inc(s("la_ready"), 1)
                dve.wait_ge(s("e_ready"), h + 1)
                dve.tensor_copy(e_end[:, 0:SEQ], ps[:, 2, :])
                link(dve.tensor_copy(e_end[:, sample], ps[:, 3, 0:NS]))
                for v, src, n, w in ((e_end[:, 0:SEQ], ps[:, 2, :], NCH, CHUNK), (e_end[:, sample], ps[:, 3, 0:NS], DEC_B, DEC_T)):
                    last = dve.tensor_tensor(grid(v, n), bc(grid(src, n)[:, :, w - 1:w], [P, n, w]), grid(v, n), ALU.subtract)
                last.then_inc(s("end_ready"), 1)
                decay = st[:, 100:124]
                dve.tensor_copy(decay[:, 0:NCH].unsqueeze(2), grid(e_cum[:, 0:SEQ], NCH)[:, :, CHUNK - 1:CHUNK])
                link(dve.tensor_copy(decay[:, NCH:].unsqueeze(2), grid(e_cum[:, sample], DEC_B)[:, :, DEC_T - 1:DEC_T]))
                dve.wait_ge(s("qk_ps"), h + 1)
                dve.scalar_tensor_tensor(halves(e_cum), wide(2), GDK ** -0.5, halves(e_cum), ALU.mult, ALU.mult)
                link(dve.tensor_tensor(halves(e_neg), wide(3), halves(e_neg), ALU.mult))
                dve.wait_ge(s("e_end"), h + 1)
                dve.tensor_tensor(halves(e_end), wide(3), halves(e_end), ALU.mult).then_inc(s("qkt_ready"), 1)
                dve.tensor_copy(grid(q_mask, DEC_B)[:, :, 0:DEC_T], e_cum[:, sample].rearrange("p (b t) -> p b t", t=DEC_T))\
                   .then_inc(s("q_mask"), 1)
                def finish(i, T):
                    n = 5 * h + i
                    c = 64 + 2 * (n % 2)
                    dve.wait_ge(s("o_sq"), n + 1)
                    dve.tensor_scalar(st[0:T, c:c + 1], st[0:T, 60:61], 1.0 / GDV, EPS, ALU.mult, ALU.add).then_inc(s("o_var"), 1)
                    dve.wait_ge(s("o_rstd"), n + 1)
                    dve.wait_ge(s("og_ready"), n + 1)
                    dve.scalar_tensor_tensor(on_[0:T, n % 2, :], ps[0:T, i % 2, 0:GDV], st[0:T, c + 1:c + 2], og[0:T, i, :],
                                             ALU.mult, ALU.mult).then_inc(s("on_ready"), 1)

                def masked(i, T, mask, n):
                    dve.wait_ge(s("att_ps"), n + 1)
                    dst = att[:, i % 2, :] if T == P else cmp8[0:NS, 0, 0:NS]
                    dve.copy_predicated(dst, mask.bitcast(U32), ps[0:T, 2, P * (i % 2):P * (i % 2) + T]).then_inc(s("att_ready"), 1)

                def by_chunk(i):
                    dve.tensor_tensor(kend_c[:, i % 2], bc(kend[:, i, :].unsqueeze(1), [P, CPT, P]),
                                      bc(const("chunk_member").unsqueeze(2), [P, CPT, P]), ALU.mult).then_inc(s("kend_c"), 1)

                dve.wait_ge(s("kend_ready"), h + 1)
                by_chunk(0)
                for i in range(PT):
                    if i < PT - 1:
                        by_chunk(i + 1)
                    masked(i, P, const("chunk_causal"), 5 * h + i)
                    for c in range(CPT * i, CPT * i + CPT):
                        n = NCH * h + c
                        dve.wait_ge(s("u_ps"), n + 1)
                        new, old = states[(c + 1) % 4], states[c % 4]
                        if c == 0:
                            if h:
                                dve.wait_ge(s("state_p_out"), 16 * h)
                            dve.tensor_copy(new, ps[:, 4 + c % 4, 0:GDV]).then_inc(s("state_new"), 1)
                        else:
                            dve.wait_ge(s("state_new"), n)
                            if c > 3:
                                dve.wait_ge(s("inter"), (NCH - 1) * h + c - 3)
                            dve.scalar_tensor_tensor(new, old, decay[:, c:c + 1], ps[:, 4 + c % 4, 0:GDV], ALU.mult, ALU.add)\
                               .then_inc(s("state_new"), 1)
                    if i:
                        finish(i - 1, P)
                if h == 0:
                    link(dve.memset(cmp8[0:NS, 0, 0:NS], 0.0))
                masked(4, NS, const("seq_causal"), 5 * h + 4)
                dve.tensor_tensor(kend_m, bc(kend[0:NS, 4, :].unsqueeze(1), [NS, DEC_B, P]),
                                  bc(const("seq_member").unsqueeze(2), [NS, DEC_B, P]), ALU.mult).then_inc(s("kend_m"), 1)
                finish(3, P)
                finish(4, NS)
                for b in range(DEC_B):
                    n = DEC_B * h + b
                    dve.wait_ge(s("us_ps"), n + 1)
                    dve.scalar_tensor_tensor(state_s[:, b, :], state_s[:, b, :], decay[:, NCH + b:NCH + b + 1],
                                             ps[:, 4 + b % 4, 0:GDV], ALU.mult, ALU.add).then_inc(s("state_s_new"), 1)
            for t in range(KD):
                for v, w, a in ((m_a, 2, "a"), (m_b, 3, "b")):
                    dve.wait_ge(s(f"g{a}_sig"), t + 1)
                    dve.wait_ge(s(f"p{a}_ps"), t + 1)
                    dve.tensor_tensor(halves(v[:, t % 2, :]), halves(v[:, t % 2, :]), wide(w), ALU.mult).then_inc(s("m_ready" if a == "b" else "m_half"), 1)
            for t in range(KD):
                w = 2 * (t % 3)
                dve.wait_ge(s("out_ps"), t + 1)
                g1 = mod[:, 2, t, 0:1]
                dve.scalar_tensor_tensor(xT[:, t, 0:HALF], ps[:, w, 0:HALF], g1, xT[:, t, 0:HALF], ALU.mult, ALU.add)
                dve.scalar_tensor_tensor(xT[:, t, HALF:SEQ], ps[:, w + 1, 0:SEQ - HALF], g1, xT[:, t, HALF:SEQ], ALU.mult, ALU.add)
                z = st[:, 128 + 32 * (t % 2):160 + 32 * (t % 2)]
                link(dve.tensor_tensor(by_sequence(z), by_sequence(ps[:, w + 1, SEQ - HALF:HALF]),
                                       bc(mod[:, 2, t, 1:].unsqueeze(2), [P, DEC_B, DEC_T]), ALU.mult))
                dve.tensor_tensor(xT[:, t, sample], xT[:, t, sample], z, ALU.add).then_inc(s("x1T"), 1)
            dve.wait_ge(s("sq_used"), 2 * KD)
            link(dve.tensor_scalar(halves(var2), wide(3), 1.0 / D, EPS, ALU.mult, ALU.add))
            dve.reciprocal(var2, var2).then_inc(*done("var2_ready"))
            dve.wait_ge(*after("rstd2_ready"))
            modulate(1, rstd2, "h2")
            dve.wait_ge(s("h2_ready"), KD)
            for t in range(KD):
                dve.tensor_copy(g_exp[:, t, 0:P], bc(mod[:, 5, t, 0:1], [P, P]))
                last = dve.tensor_copy(by_sequence(g_exp[:, t, P:]), bc(mod[:, 5, t, 1:].unsqueeze(2), [P, DEC_B, DEC_T]))
            last.then_inc(*done("g_exp2"))
            link(dve.memset(lg[:, :, :], 0.0))
            dve.wait_ge(*after("lg_ps"))
            dve.tensor_copy(lg[:, 0:PT, :], grid(ps[:, 7, 0:PT * 36], PT))
            link(dve.tensor_copy(lg[0:NS, PT, :], ps[0:NS, 7, PT * 36:5 * 36]))
            lgg = lg[:, :, 0:NG]
            st5 = lambda c: st[:, c:c + 5]
            gmax = st5(128)
            link(dve.tensor_reduce(gmax, lgg, AX.X, ALU.max))
            dve.tensor_tensor(both[:, :, 0:NG], lgg, bc(gmax.unsqueeze(2), [P, 5, NG]), ALU.subtract).then_inc(*done("lg_max"))

            def rank(dst, v, n, low):
                full = [P, 5, n, n]
                a, b = (w[:, 0:5 * n * n].rearrange("p (a j i) -> p a j i", a=5, j=n) for w in (less, more_than))
                vi, vj = bc(v.unsqueeze(2), full), bc(v.unsqueeze(3), full)
                dve.tensor_tensor(b, vi, vj, ALU.is_gt)
                link(dve.tensor_tensor(a, vi, vj, ALU.is_equal))
                link(dve.tensor_tensor(a, a, bc(grid(low, n).unsqueeze(1), full), ALU.mult))
                link(dve.tensor_tensor(a, a, b, ALU.add))
                link(dve.tensor_reduce(dst, a, AX.X, ALU.add))

            gsel = cmp8[:, 1, 128:148].rearrange("p (a j) -> p a j", a=5)
            grank = cmp8[:, 1, 100:120].rearrange("p (a j) -> p a j", a=5)
            rank(grank, lgg, NG, own_lower4)
            link(dve.tensor_scalar(gsel, grank, 0.5, None, ALU.is_lt))
            e4 = lg[:, :, NG:].rearrange("p a (g e) -> p a g e", g=NG)
            e_in4 = more_than[:, 0:5 * NE].rearrange("p (a g e) -> p a g e", a=5, g=NG)
            link(dve.tensor_tensor(e_in4, e4, bc(gsel.unsqueeze(3), [P, 5, NG, EPG]), ALU.mult))
            ein = st[:, 152:192].rearrange("p (a e) -> p a e", a=5)
            link(dve.tensor_reduce(ein, more_than[:, 0:5 * NE].rearrange("p (a g e) -> p a e g", a=5, g=NG), AX.X, ALU.add))
            erank = st[:, 208:248].rearrange("p (a e) -> p a e", a=5)
            rank(erank, ein, EPG, own_lower8)
            picked = [cmp8[:, 0, 40 * c:40 * c + 40].rearrange("p (a e) -> p a e", a=5) for c in range(2)]
            for c in range(2):
                last = dve.tensor_scalar(picked[c], erank, float(c), None, ALU.is_equal)
            link(last)
            for c, oh in ((0, one1), (1, one2)):
                last = dve.tensor_tensor(oh[:, :, :].rearrange("p a (g e) -> p a g e", g=NG), bc(gsel.unsqueeze(3), [P, 5, NG, EPG]),
                                         bc(picked[c].unsqueeze(2), [P, 5, NG, EPG]), ALU.mult)
            link(last)
            dve.wait_ge(*after("lg_exp"))
            psum_g = st5(136)
            link(dve.tensor_reduce(psum_g, both[:, :, 0:NG], AX.X, ALU.add))
            link(dve.tensor_tensor(both[:, :, :], one1[:, :, :], one2[:, :, :], ALU.add))
            link(dve.tensor_tensor(both[:, :, :], both[:, :, :], bc(const("token_real").unsqueeze(2), [P, 5, NE]), ALU.mult))
            link(dve.tensor_copy(run[:, 0, :], both[:, 0, :]))
            for i in range(1, 4):
                link(dve.tensor_tensor(run[:, i, :], run[:, i - 1, :], both[:, i, :], ALU.add))
            dve.tensor_tensor(run[:, 4, :], run[:, 3, :], both[:, 4, :], ALU.add).then_inc(*done("chosen"))
            for c in range(2):
                last = dve.tensor_tensor(picked[c], picked[c], ein, ALU.mult)
            link(last)
            for c in range(2):
                last = dve.tensor_reduce(st5(192 + 8 * c), picked[c], AX.X, ALU.add)
            link(last)
            dve.tensor_tensor(st5(200), st5(200), st5(192), ALU.subtract).then_inc(*done("e_gap"))
            dve.wait_ge(*after("pos_ps"))
            link(dve.tensor_copy(cnt[:, :], ps[:, 7, 5 * NE:6 * NE]))
            over = blk_cmp[:, 0:NE * EDGES].rearrange("p (e c) -> p e c", e=NE)
            link(dve.tensor_tensor(over, bc(cnt[:, :].unsqueeze(2), [P, NE, EDGES]),
                                   bc(const("block_edge").unsqueeze(1), [P, NE, EDGES]), ALU.is_gt))
            link(dve.tensor_reduce(cnt[:, :], over, AX.X, ALU.add))
            ends = [cmp8[:, a, 0:NE] for a in range(2)]
            link(dve.tensor_copy(ends[0], cnt[:, :]))
            step = 1
            while step < NE:
                a, b = ends
                dve.tensor_copy(b[:, 0:step], a[:, 0:step])
                link(dve.tensor_tensor(b[:, step:], a[:, step:], a[:, 0:NE - step], ALU.add))
                ends, step = [b, a], 2 * step
            ends = ends[0]
            ids = const("count")[:, 0:NE]
            link(dve.tensor_tensor(base[:, :], ends, cnt[:, :], ALU.subtract))
            link(dve.tensor_tensor(base[:, :], base[:, :], ids, ALU.subtract))
            link(dve.tensor_scalar(base[:, :], base[:, :], float(CAP), float(CAP * (NE - 1)), ALU.mult, ALU.add))
            pos = grid(ps[:, 7, 0:5 * NE], 5)
            over = grid(blk_cmp[:, 0:5 * NE], 5)
            link(dve.tensor_scalar(over, pos, float(CAP), None, ALU.is_ge))
            link(dve.tensor_tensor(over, over, bc(base[:, :].unsqueeze(1), [P, 5, NE]), ALU.mult))
            link(dve.scalar_tensor_tensor(over, bc(ids.unsqueeze(1), [P, 5, NE]), float(CAP), over, ALU.mult, ALU.add))
            link(dve.tensor_tensor(both[:, :, :], over, pos, ALU.add))
            for oh in (one1, one2):
                last = dve.tensor_tensor(oh[:, :, :], oh[:, :, :], both[:, :, :], ALU.mult)
            link(last)
            for c, oh in ((0, one1), (1, one2)):
                last = dve.tensor_reduce(dest[:, c, :], oh[:, :, :], AX.X, ALU.add)
            link(last)
            link(dve.tensor_copy(dest_i[:, :, :], dest[:, :, :]))
            dve.tensor_scalar(row_i[:, :, :], dest_i[:, :, :], CAP - 1, None, ALU.bitwise_and)
            link(dve.tensor_scalar(blk_i[:, :, :], dest_i[:, :, :], CAP.bit_length() - 1, None, ALU.logical_shift_right))
            dve.tensor_copy(place[:, 0], row_i[:, :, :])
            link(dve.tensor_copy(place[:, 1], blk_i[:, :, :]))
            rh, bh = (v.rearrange("p (c a r) -> p c a r", c=2, a=5) for v in (row_hot, block_hot))
            for c in range(2):
                dve.tensor_tensor(rh[:, c], bc(place[:, 0, c, :].unsqueeze(2), [P, 5, CAP]), bc(const("count").unsqueeze(1), [P, 5, CAP]), ALU.is_equal)
                last = dve.tensor_tensor(bh[:, c], bc(place[:, 1, c, :].unsqueeze(2), [P, 5, EB]), bc(const("count")[:, 0:EB].unsqueeze(1), [P, 5, EB]),
                                         ALU.is_equal)
            link(last)
            for c in range(2):
                last = dve.tensor_tensor(rh[:, c], rh[:, c], bc(const("token_id").unsqueeze(2), [P, 5, CAP]), ALU.mult)
            last.then_inc(*done("idx_hot"))
            dve.wait_ge(*after("idx_ps"))
            dve.tensor_copy(idx[:, :], ps[0:CAP, 6, 0:EB]).then_inc(*done("idx_ready"))
            dve.scalar_tensor_tensor(dest_i[:, :, :], row_i[:, :, :], float(EB), blk_i[:, :, :], ALU.mult, ALU.add)\
               .then_inc(*done("dest_ready"))
            over = blk_cmp[:, 0:NE * MORE].rearrange("p (c e) -> p c e", c=MORE)
            link(dve.tensor_tensor(over, bc(ends.unsqueeze(1), [P, MORE, NE]), bc(const("count")[:, 0:MORE].unsqueeze(2), [P, MORE, NE]), ALU.is_le))
            link(dve.tensor_reduce(blk_cmp[:, 0:MORE], over, AX.X, ALU.add))
            link(dve.tensor_scalar(blk_cmp[:, 0:MORE], blk_cmp[:, 0:MORE], float(NE - 1), None, ALU.min))
            link(dve.tensor_copy(more_i[:, 0:MORE], blk_cmp[0:1, 0:MORE]))
            dve.wait_ge(*after("e_gap_exp"))
            pg, den = st5(144), st5(128)
            link(dve.reciprocal(pg, psum_g))
            link(dve.tensor_scalar(den, st5(200), 1.0, None, ALU.add))
            link(dve.reciprocal(den, den))
            link(dve.tensor_tensor(wts[:, 0, :], den, pg, ALU.mult))
            link(dve.tensor_tensor(wts[:, 1, :], wts[:, 0, :], st5(200), ALU.mult))
            dve.tensor_copy(more_i[:, MORE:], ends[0:1, NE - 1:NE]).then_inc(*done("more_ready"))
            def dve_down(e, it, par, first=False):
                dve.wait_ge(w_used, e * 3 + (EXP_USED + 3))
                if not first:
                    dve.wait_ge(s(f"ye_out{par}"), it * 16)
                dve.tensor_copy(ye[par], ps[:, 4 + par, :]).then_inc(s("ye_ready"), 1)

            def dve_step(e, it, par, before):
                if before:
                    dve_down(e - 1, before[0], 1 - par, isinstance(before[0], int) and before[0] == 0)
                dve.wait_ge(w_used, e * 3 + (EXP_USED + 2))
                dve.wait_ge(s("hid_gate"), e + 1)
                dve.tensor_tensor(hid[par], hid[par], ps[:, 2 + par, 256:512], ALU.mult).then_inc(s("hid"), 1)

            dve_step(0, 0, 0, None)
            dve_step(1, 0, 1, (0,))
            dve_step(2, 1, 0, (0,))
            with dve.Fori(1, NE // 2 - 1) as i:
                dve_step(2 * i + 1, i, 1, (i,))
                dve_step(2 * i + 2, i + 1, 0, (i,))
            dve_step(NE - 1, NE // 2 - 1, 1, (NE // 2 - 1,))
            dve_down(NE - 1, NE // 2 - 1, 1)

            def more(c):
                dve.wait_ge(s("xs_tr"), c + NE)
                dve.tensor_copy(idx_cur[:, :], idx[:, bass.DynSlice(c + NE, 1)]).then_inc(s("idx_cur"), 1)
                dve_step(c + NE, c + NE // 2, 0, None)
                dve_down(c + NE, c + NE // 2, 0)

            further_blocks(dve, more)
            for i, (_, T) in enumerate(TILES):
                dve.wait_ge(s("ya_scaled"), i + 1)
                dve.wait_ge(s(f"y1_in{i}"), 16)
                a, b = ya[i][0:T, :], yb[i][0:T, :]
                link(dve.scalar_tensor_tensor(a, b, wts[0:T, 1, i:i + 1], a, ALU.mult, ALU.add))
                dve.tensor_tensor(a, a, g2p if i < PT else g2s, ALU.mult).then_inc(s("y_gated"), 1)

        @blk.tensor
        def _(pe):
            def mm(out, lhsT, rhs, start, stop, **k):
                return pe.matmul(out, lhsT, rhs, start=start, stop=stop, **k)

            def product(w, lhs, rhs, K, rows=P):
                for half in range(2):
                    for k in range(K):
                        last = mm(ps[0:rows, 2 * w + half, 0:HALF], lhs(k), rhs(k)[:, HALF * half:HALF * half + HALF], k == 0, k == K - 1)
                return last

            def turn(out, v):
                n = v.shape[0]
                return pe.transpose(out, v, ident[0:n, 0:n])

            pe.wait_ge(s("const_in"), 16)
            pe.wait_ge(s("vec_in"), 48)
            turn(ps[:, 5, 128:192], vrow)
            pe.wait_ge(*after("c_silu"))
            for k in range(KD):
                last = turn(ps[:, 5, 9 * k:9 * k + 9], crow[:, 1, P * k:P * k + P])
            last.then_inc(*done("c_tr"))
            pe.wait_ge(*after("cT"))
            for i in range(len(ADA) + 1):
                if i:
                    pe.wait_ge(s("mod_rows"), i)
                    for j in range(4):
                        at = 9 * (4 * (i - 1) + j)
                        last = mm(ps[:, 4, at:at + 9], mod_rows[:, (i - 1) % 2, P * j:P * j + P], const("row_sequence"), True, True)
                    last.then_inc(s("mod_tr"), 1)
                if i < len(ADA):
                    n = ADA[i]
                    landed(pe, n)
                    w = grid(slot(n), KD)
                    for k in range(KD):
                        r = slice(32 * (k % 4), 32 * (k % 4) + 32)
                        last = mm(ps[r, 5, :], cT[:, k, :], w[:, k, :], k < 4, k >= 4, skip_group_check=True)
                    last.then_inc(w_used, 1)
                if i < AH // 2:
                    pe.wait_ge(*after("rbw_ready"))
                    for h in (2 * i, 2 * i + 1):
                        if h >= 2:
                            pe.wait_ge(s("bias_copied"), h - 1)
                        mm(ps[:, 6 + h % 2, 0:TAB], rbw[:, P * h:P * h + P], hot, True, True).then_inc(s("bias_ps"), 1)
                k = i - AH // 2
                if 0 <= k < KD:
                    pe.wait_ge(s("x_in"), 32)
                    if k >= 2:
                        pe.wait_ge(s("xT_ready"), k - 1)
                    for j in range(PT):
                        turn(ps[:, 2 * (k % 2), P * j:P * j + P], x_tok[:, j, P * k:P * k + P])
                    turn(ps[:, 2 * (k % 2) + 1, 0:NS], x_tok[0:NS, PT, P * k:P * k + P]).then_inc(s("x_tr"), 1)
                y = k - 1
                if 0 <= y < KD:
                    if y == 0:
                        pe.wait_ge(s("bias_copied"), AH)
                    pe.wait_ge(s("sq_ready"), y + 1)
                    for half in range(2):
                        last = mm(ps[:, 6 + half, 0:HALF], ones, sq[:, y % 2, HALF * half:HALF * half + HALF], y == 0, y == KD - 1)
                    last.then_inc(s("sq_used"), 1)
            for n in range(15 + 1):
                if n < 15:
                    t0, T = TILES[n % 5]
                    b = QKV[n // 5]
                    landed(pe, b)
                    w = grid(slot(b), KD)
                    if 4 <= n < 14:
                        pe.wait_ge(s("pj_free"), n - 3)
                    elif n == 14:
                        pe.wait_ge(s("v_ready"), 1)
                    if n == PT:
                        pe.wait_ge(*after("h_sample"))
                    for k in range(KD):
                        if n == 0:
                            pe.wait_ge(s("h_ready"), k + 1)
                        last = mm(ps[0:T, n % 4, :], hT[:, k, t0:t0 + T], w[:, k, :], k == 0, k == KD - 1)
                    last.then_inc(s("pj"), 1)
                if 1 <= n <= 10:
                    y = n - 1
                    t0, T = TILES[y % 5]
                    pe.wait_ge(s("qk_tok"), y + 1)
                    if y >= 2:
                        pe.wait_ge(s("qk_T"), y - 1)
                    for a in range(PAIRS):
                        last = turn(ps[:, 4 + y % 2, T * a:T * a + T], tok[0:T, y % 2, P * a:P * a + P])
                    last.then_inc(s("qk_tr"), 1)
            pe.wait_ge(s("qk_T"), 10)
            pe.wait_ge(s("v_ready"), 5)
            for x in range(32 + 3):
                if x < 32:
                    h, i = x // 4, x % 4
                    rows = slice(64 * (h % 2), 64 * (h % 2) + 64)
                    n = P * (i + 1)
                    if x >= 2:
                        pe.wait_ge(s("sc_max"), x - 1)
                    mm(ps[:, x % 2, 0:n], qT[rows, h // 2, P * i:P * i + P], kT[rows, h // 2, 0:n], True, True).then_inc(s("sc_ps"), 1)
                if 2 <= x <= 33:
                    y = x - 2
                    pe.wait_ge(s("p_norm"), y + 1)
                    if y >= 2:
                        pe.wait_ge(s("p_T"), y - 1)
                    for j in range(y % 4 + 1):
                        last = turn(ps[:, 2 + y % 2, P * j:P * j + P], sc_p[:, y % 3, P * j:P * j + P])
                    last.then_inc(s("p_tr"), 1)
                if x >= 3:
                    y = x - 3
                    h, i = y // 4, y % 4
                    pe.wait_ge(s("p_T"), y + 1)
                    if y >= 2:
                        pe.wait_ge(s("p_ov"), y - 1)
                    rows = slice(64 * (h % 2), 64 * (h % 2) + 64)
                    for j in range(i + 1):
                        last = mm(ps[rows, 4 + y % 2, 0:P], v_tok[:, j, AD * h:AD * h + AD], pt_p[:, y % 2, P * j:P * j + P], j == 0, j == i)
                    last.then_inc(s("p_pv"), 1)
            pe.wait_ge(*after("q_row"))
            pe.wait_ge(s("p_ov"), 32)
            for b in range(DEC_B):
                r = slice(32 * (b % 4), 32 * (b % 4) + 32)
                for a in range(PAIRS):
                    last = mm(ps[r, 3, NS * (b // 4):NS * (b // 4) + NS], q_row[:, a, b, :], kT[:, a, sample], a == 0, a == PAIRS - 1,
                              skip_group_check=True)
            last.then_inc(*done("own_ps"))

            def weights_turned(g):
                pe.wait_ge(s("l_norm"), g + 1)
                for q in range(4):
                    if q >= 2:
                        pe.wait_ge(s("pr_T"), 5 * g + q - 1)
                    for page in range(4 * q, 4 * q + 4):
                        last = turn(ps[:, 6 + q % 2, P * (page % 4):P * (page % 4) + P], logits[g][:, P * page:P * page + P])
                    last.then_inc(s("pr_tr"), 1)
                turn(ps[0:NS, 3, 384:512], logits[g][:, PAST:]).then_inc(s("pr_tr"), 1)

            def attend(g):
                pe.wait_ge(s("pr_T"), 5 * g + 5)
                for j in range(4):
                    mm(ps[32 * j:32 * j + 32, g, :], prT[0:NS, PAGES, 32 * j:32 * j + 32], v_tok[0:NS, PT, :], True, False,
                       skip_group_check=True)
                for i in range(PAGES // 2):
                    if g == 0 and i == 2:
                        pe.wait_ge(s("sc_taken"), QUADS // 4)
                        product(2, lambda k: wgk[:, k, :], lambda k: hT[:, k, :], KD, RANK).then_inc(*done("gk_ps"))
                    n = PAGED[("v", PAGES // 2 * g + i)]
                    landed(pe, n)
                    for page in (2 * i, 2 * i + 1):
                        for j in range(4):
                            q = 4 * (page % 2) + j
                            last = mm(ps[32 * j:32 * j + 32, g, :], prT[:, page, 32 * j:32 * j + 32], slot(n)[:, AW * q:AW * q + AW],
                                      False, page == PAGES - 1, skip_group_check=True)
                    last.then_inc(s("pv_s"), 1)

            def selected(g):
                pe.wait_ge(s("o_rows"), g + 1)
                if g:
                    pe.wait_ge(s("oa_taken"), g)
                for a in range(PAIRS):
                    last = mm(ps[:, 2, 64 * g + 16 * a:64 * g + 16 * a + 16], o_rows[:, g, P * a:P * a + P], const("row_token"), True, True)
                last.then_inc(s("o_sel"), 1)

            for quad in range(QUADS + 1):
                if quad < QUADS:
                    for pg in range(4 * quad, 4 * quad + 4):
                        n = PAGED[("k", pg // 8)]
                        landed(pe, n)
                        if pg >= 3:
                            pe.wait_ge(s("page_T"), pg - 2)
                        for a in range(PAIRS):
                            last = turn(ps[:, pg % 3, P * a:P * a + P], slot(n)[:, AW * (pg % 8) + P * a:AW * (pg % 8) + P * a + P])
                        last.then_inc(s("page_tr"), 1)
                if quad:
                    y = quad - 1
                    g, page = y // PAGES, y % PAGES
                    pe.wait_ge(s("page_T"), 4 * y + 4)
                    if page % 4 == 0 and y >= 8:
                        pe.wait_ge(s("sc_taken"), y // 4 - 1)
                    for a in range(PAIRS):
                        for j in range(4):
                            last = mm(ps[32 * j:32 * j + 32, 4 + y // 4 % 2, P * (page % 4):P * (page % 4) + P], q_row[:, a, 4 * g + j, :],
                                      kpage[:, (4 * y + j) % 8, P * a:P * a + P], a == 0, a == PAIRS - 1, skip_group_check=True)
                    last.then_inc(s("page_sc"), 1)
                if quad == WEIGHTS_AT:
                    weights_turned(0)
            attend(0)
            weights_turned(1)
            selected(0)
            attend(1)
            selected(1)
            pe.wait_ge(s("oa_taken"), 2)
            pe.wait_ge(*after("gk_ready"))
            for h in range(GH):
                a_blk, b_blk = GLA[h]
                if h:
                    pe.wait_ge(s("og_T"), 5 * h)
                for i, (t0, T) in enumerate(TILES):
                    out = ps[0:T, i // 4, P * (i % 4):P * (i % 4) + P]
                    last = mm(out, gkT[:, t0:t0 + T], gk2[:, P * h:P * h + P], True, True)
                last.then_inc(s("la_ps"), 1)
                landed(pe, a_blk)
                wq = grid(slot(a_blk)[:, 0:KD * P], KD)
                wk = grid(slot(a_blk)[:, KD * P:2 * KD * P], KD)
                wv = grid(slot(a_blk)[:, 2 * KD * P:], KD)
                if h:
                    pe.wait_ge(s("state_s_new"), DEC_B * h)
                product(2, lambda k: wq[:, k, :], lambda k: hT[:, k, :], KD)
                product(3, lambda k: wk[:, k, :], lambda k: hT[:, k, :], KD).then_inc(s("qk_ps"), 1)
                pe.wait_ge(s("la_ready"), h + 1)
                for i in range(PT):
                    mm(ps[:, 2, P * i:P * i + P], la[:, P * i:P * i + P], const("chunk_causal"), True, True)
                mm(ps[:, 3, 0:NS], la[0:NS, 4 * P:5 * P], const("seq_causal"), True, True).then_inc(s("cum_ps"), 1)
                for i, (t0, T) in enumerate(TILES):
                    if i == 4:
                        pe.wait_ge(s("end_ready"), h + 1)
                        pe.wait_ge(s("e_ready"), h + 1)
                    for k in range(KD):
                        last = mm(ps[0:T, i // 2, GDV * (i % 2):GDV * (i % 2) + GDV], hT[:, k, t0:t0 + T], wv[:, k, :], k == 0, k == KD - 1)
                    if i % 2 or i == PT:
                        last.then_inc(s("v_ps"), 1)
                landed(pe, b_blk)
                wo = grid(slot(b_blk)[:, 0:KD * GDV], KD)
                pe.wait_ge(s("qkt_ready"), h + 1)
                for i, (t0, T) in enumerate(TILES):
                    for k in range(KD):
                        last = mm(ps[0:T, 4 + i // 2, GDV * (i % 2):GDV * (i % 2) + GDV], hT[:, k, t0:t0 + T], wo[:, k, :], k == 0, k == KD - 1)
                    if i % 2 or i == PT:
                        last.then_inc(s("og_ps"), 1)
                for i in range(PT):
                    turn(ps[:, 3, P * i:P * i + P], e_end[:, P * i:P * i + P])
                turn(ps[0:NS, 7, 0:P], e_end[:, sample]).then_inc(s("kend_tr"), 1)
                pe.wait_ge(s("kend_ready"), h + 1)
                pe.wait_ge(s("vg_ready"), 5 * h + 5)
                pe.wait_ge(s("og_raw"), 5 * h + 5)
                if h == 0:
                    pe.wait_ge(*after("att_set"))

                def turned(i, T):
                    n = 5 * h + i
                    pe.wait_ge(s("on_ready"), n + 1)
                    if n:
                        pe.wait_ge(s("og_T"), n)
                    for a in range(2):
                        last = turn(ps[:, 3, T * a:T * a + T], on_[0:T, n % 2, P * a:P * a + P])
                    last.then_inc(s("on_tr"), 1)

                for i in range(PT):
                    t0 = P * i
                    mm(ps[:, 2, P * (i % 2):P * (i % 2) + P], e_neg[:, t0:t0 + P], e_cum[:, t0:t0 + P], True, True).then_inc(s("att_ps"), 1)
                    pe.wait_ge(s("kend_c"), PT * h + i + 1)
                    for c in range(CPT):
                        n = NCH * h + CPT * i + c
                        if n >= 4:
                            pe.wait_ge(s("state_new"), n - 3)
                        mm(ps[:, 4 + c, 0:GDV], kend_c[:, i % 2, c, :], v_g[:, i, :], True, True).then_inc(s("u_ps"), 1)
                    pe.wait_ge(s("att_ready"), 5 * h + i + 1)
                    if i >= 2:
                        pe.wait_ge(s("on_ready"), 5 * h + i - 1)
                    last = mm(ps[:, i % 2, 0:GDV], att[:, i % 2, :], v_g[:, i, :], True, False, skip_group_check=True)
                    for c in range(CPT):
                        n = CPT * i + c
                        if n == 0:
                            continue
                        pe.wait_ge(s("state_new"), NCH * h + n)
                        r = slice(CHUNK * c, CHUNK * c + CHUNK)
                        last = mm(ps[r, i % 2, 0:GDV], e_cum[:, t0 + CHUNK * c:t0 + CHUNK * c + CHUNK], states[n % 4], False, c == CPT - 1,
                                  skip_group_check=True)
                        last.then_inc(s("inter"), 1)
                    if i >= 2:
                        turned(i - 2, P)
                mm(ps[0:NS, 2, 0:NS], e_neg[:, sample], e_cum[:, sample], True, True).then_inc(s("att_ps"), 1)
                turned(2, P)
                pe.wait_ge(s("att_ready"), 5 * h + 5)
                pe.wait_ge(s("q_mask"), h + 1)
                pe.wait_ge(s("state_s_in"), 16 * h + 16)
                mm(ps[0:NS, 0, 0:GDV], cmp8[0:NS, 0, 0:NS], v_g[0:NS, 4, :], True, False)
                for b in range(DEC_B):
                    last = mm(ps[0:NS, 0, 0:GDV], q_mask[:, NS * b:NS * b + NS], state_s[:, b, :], False, b == DEC_B - 1)
                last.then_inc(s("o_ps"), 1)
                turned(3, P)
                pe.wait_ge(s("kend_m"), h + 1)
                pe.wait_ge(s("state_new"), NCH * h + NCH)
                for b in range(DEC_B):
                    if b >= 4:
                        pe.wait_ge(s("state_s_new"), DEC_B * h + b - 3)
                    mm(ps[:, 4 + b % 4, 0:GDV], kend_m[:, b, :], v_g[0:NS, 4, :], True, True).then_inc(s("us_ps"), 1)
                turned(4, NS)
            pe.wait_ge(s("og_T"), 5 * GH)
            pe.wait_ge(s("state_s_new"), DEC_B * GH)
            for t in range(KD):
                n = MERGE[t]
                landed(pe, n)
                wga, wgb, wb = (grid(slot(n)[:, KD * P * a:KD * P * a + KD * P], KD) for a in range(3))
                wa = grid(slot(n)[:, 3 * KD * P:3 * KD * P + AW], AW // P)
                if t:
                    pe.wait_ge(s("ga_sig"), t)
                product(0, lambda k: wga[:, k, :], lambda k: hT[:, k, :], KD).then_inc(s("ga_ps"), 1)
                if t:
                    pe.wait_ge(s("gb_sig"), t)
                product(1, lambda k: wgb[:, k, :], lambda k: hT[:, k, :], KD).then_inc(s("gb_ps"), 1)
                if t:
                    pe.wait_ge(s("m_half"), t)
                product(2, lambda k: wa[:, k, :], lambda k: o_aT[:, k, :], AW // P).then_inc(s("pa_ps"), 1)
                if t:
                    pe.wait_ge(s("m_ready"), t)
                product(3, lambda k: wb[:, k, :], lambda k: o_gT[:, k, :], KD).then_inc(s("pb_ps"), 1)
            pe.wait_ge(s("merged"), KD)
            for t in range(KD):
                n = OUT[t // 4]
                landed(pe, n)
                w = grid(slot(n), KD)
                if t >= 3:
                    pe.wait_ge(s("x1T"), t - 2)
                product(t % 3, lambda k: w[:, k, P * (t % 4):P * (t % 4) + P], lambda k: mergedT[:, k, :], KD).then_inc(s("out_ps"), 1)
            for k in range(KD):
                pe.wait_ge(s("sq_ready"), KD + k + 1)
                for half in range(2):
                    last = mm(ps[:, 6 + half, 0:HALF], ones, sq2[:, k % 2, HALF * half:HALF * half + HALF], k == 0, k == KD - 1)
                last.then_inc(s("sq_used"), 1)
            def to_tokens(n):
                t0, T = TILES[n % 5]
                if n >= 3:
                    pe.wait_ge(s("tok_taken"), n - 2)
                v = (xT, hT)[n // 5]
                for k in range(KD):
                    last = turn(ps[0:T, 2 * (n % 3) + k // 4, P * (k % 4):P * (k % 4) + P], v[:, k, t0:t0 + T])
                last.then_inc(s("tok_tr"), 1)

            for n in range(3):
                to_tokens(n)
            pe.wait_ge(s("router_in"), 32)
            for half in range(2):
                if half:
                    pe.wait_ge(*after("h2_sample"))
                for k in range(KD):
                    if half == 0:
                        pe.wait_ge(s("h2_ready"), k + 1)
                    last = mm(ps[0:NG + NE, 6 + half, 0:HALF], wr[:, k, :], hT[:, k, HALF * half:HALF * half + HALF], k == 0, k == KD - 1)
            last.then_inc(*done("lgT_ps"))
            to_tokens(3)
            pe.wait_ge(*after("lgT"))
            for i, (t0, T) in enumerate(TILES):
                last = turn(ps[0:T, 7, 36 * i:36 * i + 36], lgT[:, t0:t0 + T])
            last.then_inc(*done("lg_ps"))
            for n in range(4, 10):
                to_tokens(n)
            pe.wait_ge(*after("g_exp2"))
            pe.wait_ge(s("tok_taken"), 10)
            for t in range(KD):
                turn(ps[:, t // 4, P * (t % 4):P * (t % 4) + P], g_exp[:, t, 0:P])
            for t in range(KD):
                last = turn(ps[0:NS, 2 + t // 4, P * (t % 4):P * (t % 4) + P], g_exp[:, t, P:])
            last.then_inc(*done("g_tr"))
            pe.wait_ge(*after("chosen"))
            for i in range(5):
                out = ps[:, 7, NE * i:NE * i + NE]
                last = mm(out, const("before"), both[:, i, :], True, i == 0)
                if i:
                    last = mm(out, ones, run[:, i - 1, :], False, True)
            mm(ps[:, 7, 5 * NE:6 * NE], ones, run[:, 4, :], True, True).then_inc(*done("pos_ps"))
            pe.wait_ge(*after("idx_hot"))
            for n in range(10):
                last = mm(ps[0:CAP, 6, 0:EB], row_hot[:, CAP * n:CAP * n + CAP], block_hot[:, EB * n:EB * n + EB], n == 0, n == 9)
            last.then_inc(*done("idx_ps"))
            pe.wait_ge(*after("g_rows"))

            def step(e, it, par, before):
                pe.wait_ge(s(f"xs_in{par}"), it * 16 + 16)
                rows = xs[par].rearrange("r (p k) -> r k p", k=KD)
                mm(ps[:, par, 0:CAP], rows[:, 0, :], ident[0:CAP, 0:CAP], True, True)
                for j in range(1, KD):
                    last = turn(ps[:, par, CAP * j:CAP * j + CAP], rows[:, j, :])
                last.then_inc(s("xs_tr"), 1)
                if before:
                    down(e - 1, before[0], 1 - par)
                pe.wait_ge(s("xsT"), e + 1)
                for m in range(2):
                    q = (N0 + 3 * par + m) % RING
                    pe.wait_ge(slot_sem[q], it * 16 + (EXP_COUNT[q] + 16))
                    w = ring[:, q, :].rearrange("p (k c j) -> p k j c", k=KD, j=4)
                    for f in range(4):
                        for k in range(KD):
                            last = mm(ps[:, 2 + par, 256 * m + CAP * f:256 * m + CAP * f + CAP], w[:, k, f, :], xsT[par][:, CAP * k:CAP * k + CAP],
                                      k == 0, k == KD - 1)
                    last.then_inc(w_used, 1)

            def down(e, it, par):
                q = (N0 + 3 * par + 2) % RING
                pe.wait_ge(slot_sem[q], it * 16 + (EXP_COUNT[q] + 16))
                pe.wait_ge(s("hid"), e + 1)
                w = grid(ring[:, q, :], 4)
                for f in range(4):
                    for half in range(2):
                        last = mm(ps[CAP * half:CAP * half + CAP, 4 + par, :], hid[par][:, CAP * f:CAP * f + CAP],
                                  w[:, f, 512 * half:512 * half + 512], f == 0, f == 3, skip_group_check=True)
                last.then_inc(w_used, 1)

            step(0, 0, 0, None)
            with pe.Fori(0, NE // 2 - 1) as i:
                step(2 * i + 1, i, 1, (i,))
                step(2 * i + 2, i + 1, 0, (i,))
            step(NE - 1, NE // 2 - 1, 1, (NE // 2 - 1,))
            down(NE - 1, NE // 2 - 1, 1)

            def more(c):
                step(c + NE, c + NE // 2, 0, None)
                down(c + NE, c + NE // 2, 0)

            further_blocks(pe, more)


_INS = ['x_prompt', 'x_sample', 'c_prompt', 'c_sample', 'cache_k', 'cache_v', 'state_gla', 'page_table',
        'rel_bias', 'norm1_g', 'norm2_g', 'w_ada', 'b_ada', 'w_in', 'w_gk2', 'b_gk', 'q_norm_g', 'k_norm_g', 'o_norm_g',
        'w_branch_a', 'w_branch_b', 'w_out', 'w_router_group', 'b_router_group', 'w_router_expert',
        'b_router_expert', 'w_exp_gate', 'w_exp_up', 'w_exp_down']
_OUTS = [(1, SEQ, D), (DEC_B, DEC_T, D), (1, 1, SEQ, AH, AD), (1, 1, SEQ, AH, AD), (1, 1, GH, GDK, GDV),
         (1, DEC_B, DEC_T, AH, AD), (1, DEC_B, DEC_T, AH, AD), (1, DEC_B, GH, GDK, GDV)]


def kernel(**inputs):
    import concourse.bacc as bacc
    from concourse.bass_utils import run_bass_kernel_spmd

    nc = bacc.Bacc("TRN2", target_bir_lowering=False, num_devices=1)
    arrays, args = {}, []
    for name in _INS + ["shape_table"]:
        a = np.ascontiguousarray(CONST_TABLE if name == "shape_table" else inputs[name])
        arrays["in_" + name] = a
        args.append(nc.dram_tensor("in_" + name, a.shape, mybir.dt.from_np(a.dtype), kind="ExternalInput").ap())
    for i, shape in enumerate(_OUTS):
        args.append(nc.dram_tensor(f"out_{i}", shape, F32, kind="ExternalOutput").ap())
    layer_kernel(nc, *args)
    r = run_bass_kernel_spmd(nc, [arrays], core_ids=[0])
    return tuple(r.results[0][f"out_{i}"] for i in range(len(_OUTS)))
```
